# Optimizing a Trainium2 kernel written in Bass

```python
import math
import jax, jax.numpy as jnp
from jax import lax
import numpy as np

D_MODEL = 2048
BATCH = 1
SEQ = 256
DEPTH = 2
DEC_BATCH = 8
DEC_SEQ = 4
PAST_LEN = 1024
PAGE_SIZE = 128

N_EVEN = (DEPTH + 1) // 2
N_ODD = DEPTH // 2
W_A = D_MODEL // 2
H_A = 8
DH_A = W_A // H_A
MOBA_BLOCK = 256
MOBA_TOPK = 3
Q_CHUNK = 16
W_B = D_MODEL // 2
POOL_WINDOWS = (2, 4, 8, 16)
N_POOL = len(POOL_WINDOWS)
GW_B = W_B // N_POOL
POOL_HIST = max(POOL_WINDOWS) - 1
W_C = D_MODEL
H_C = 8
DH_C = W_C // H_C
MLSTM_CHUNK = 64
F_BIAS = 3.0
EPS = 1e-6

kernel_name = 'moba_pool_mlstm_hybrid_step'

def _rmsnorm(x, g):
    xf = x.astype(jnp.float32)
    r = xf * lax.rsqrt(jnp.mean(xf * xf, axis=-1, keepdims=True) + EPS)
    return (r * g.astype(jnp.float32)).astype(x.dtype)

def _alibi_slopes(n_heads):
    return 2.0 ** (-8.0 * jnp.arange(1, n_heads + 1, dtype=jnp.float32) / n_heads)

def _moba_attention(q, k, v, pos0):
    B, Tq, H, Dh = q.shape
    L = k.shape[1]
    nb = -(-L // MOBA_BLOCK)
    pad = nb * MOBA_BLOCK - L
    kb = jnp.pad(k, ((0, 0), (0, pad), (0, 0), (0, 0))).reshape(B, nb, MOBA_BLOCK, H, Dh).transpose(0, 3, 1, 2, 4)
    vb = jnp.pad(v, ((0, 0), (0, pad), (0, 0), (0, 0))).reshape(B, nb, MOBA_BLOCK, H, Dh).transpose(0, 3, 1, 2, 4)
    kmean = jnp.mean(kb.astype(jnp.float32), axis=3)
    q_pos = pos0 + jnp.arange(Tq, dtype=jnp.int32)
    n_past = q_pos // MOBA_BLOCK
    gate = jnp.einsum('bqhd,bhnd->bhqn', q.astype(jnp.float32), kmean)
    blk_ids = jnp.arange(nb, dtype=jnp.int32)
    gate = jnp.where(blk_ids[None, None, None, :] < n_past[None, None, :, None], gate, -jnp.inf)
    n_sel = min(MOBA_TOPK, nb)
    _, sel = lax.top_k(gate, n_sel)
    sel = sel.astype(jnp.int32)
    own = jnp.broadcast_to(n_past[None, None, :, None], (B, H, Tq, 1))
    blocks = jnp.concatenate([sel, own], axis=-1)
    valid = jnp.concatenate([jnp.arange(n_sel)[None, :] < n_past[:, None],
                             jnp.ones((Tq, 1), dtype=bool)], axis=-1)
    M = n_sel + 1
    qc = math.gcd(Tq, Q_CHUNK)
    nc = Tq // qc
    slopes = _alibi_slopes(H)
    scale = Dh ** -0.5
    bi = jnp.arange(B)[:, None, None, None]
    hi = jnp.arange(H)[None, :, None, None]
    offs = jnp.arange(MOBA_BLOCK, dtype=jnp.int32)

    def attend(args):
        q_c, blk_c, pos_c, val_c = args
        k_sel = kb[bi, hi, blk_c]
        v_sel = vb[bi, hi, blk_c]
        s = jnp.einsum('bhqd,bhqmpd->bhqmp', q_c, k_sel, preferred_element_type=jnp.float32) * scale
        k_pos = blk_c[..., None] * MOBA_BLOCK + offs
        dist = pos_c[None, None, :, None, None] - k_pos
        s = s - slopes[None, :, None, None, None] * dist.astype(jnp.float32)
        mask = (dist >= 0) & val_c[None, None, :, :, None]
        s = jnp.where(mask, s, -jnp.inf)
        p = jax.nn.softmax(s.reshape(B, H, qc, M * MOBA_BLOCK), axis=-1).reshape(s.shape)
        o = jnp.einsum('bhqmp,bhqmpd->bhqd', p, v_sel)
        return o.astype(q.dtype)

    qt = q.transpose(0, 2, 1, 3).reshape(B, H, nc, qc, Dh).transpose(2, 0, 1, 3, 4)
    bt = blocks.reshape(B, H, nc, qc, M).transpose(2, 0, 1, 3, 4)
    pt = q_pos.reshape(nc, qc)
    vt = valid.reshape(nc, qc, M)
    out = lax.map(attend, (qt, bt, pt, vt))
    return out.transpose(1, 0, 3, 2, 4).reshape(B, Tq, H * Dh)

def _multiscale_pool(u, prev, pos0, pool_w, pool_scale):
    B, T, W = u.shape
    P = POOL_HIST
    ext = jnp.concatenate([prev.astype(jnp.float32), u.astype(jnp.float32)], axis=1)
    cs = jnp.concatenate([jnp.zeros((B, 1, W), jnp.float32), jnp.cumsum(ext, axis=1)], axis=1)
    end = cs[:, P + 1:]
    pos = pos0 + jnp.arange(T, dtype=jnp.int32)
    means = []
    for g, w in enumerate(POOL_WINDOWS):
        sl = slice(g * GW_B, (g + 1) * GW_B)
        start = cs[:, P + 1 - w:P + 1 - w + T, sl]
        cnt = jnp.minimum(w, pos + 1).astype(jnp.float32)
        means.append((end[:, :, sl] - start) / cnt[None, :, None])
    d = jnp.concatenate(means, axis=-1) - ext[:, P:]
    d = jnp.einsum('btgc,gcd->btgd', d.reshape(B, T, N_POOL, GW_B), pool_w.astype(jnp.float32)).reshape(B, T, W)
    out = (d * pool_scale.astype(jnp.float32)).astype(u.dtype)
    return out, ext[:, -P:].astype(u.dtype)

def _mlstm(q, k, v, ig, lf, C0, n0, m0):
    B, T, H, DK = q.shape
    L = MLSTM_CHUNK if T % MLSTM_CHUNK == 0 else T
    nc = T // L
    f32 = jnp.float32

    def chunks(a):
        a = a.astype(f32).reshape((B, nc, L, H) + a.shape[3:])
        return jnp.moveaxis(jnp.moveaxis(a, 1, 0), 3, 2)

    causal = jnp.tril(jnp.ones((L, L), dtype=bool))

    def step(carry, xs):
        C, n, m = carry
        qc, kc, vc, ic, fc = xs
        b = jnp.cumsum(fc, axis=-1)
        dmat = jnp.where(causal, b[..., :, None] - b[..., None, :] + ic[..., None, :], -jnp.inf)
        carry_log = b + m[..., None]
        mt = jnp.maximum(carry_log, jnp.max(dmat, axis=-1))
        s = jnp.einsum('bhtd,bhsd->bhts', qc, kc) * jnp.exp(dmat - mt[..., None])
        inter = jnp.exp(carry_log - mt)
        num = jnp.einsum('bhts,bhsv->bhtv', s, vc) + inter[..., None] * jnp.einsum('bhvd,bhtd->bhtv', C, qc)
        den = jnp.sum(s, axis=-1) + inter * jnp.einsum('bhd,bhtd->bht', n, qc)
        h = num / jnp.maximum(jnp.abs(den), jnp.exp(-mt))[..., None]
        m_new = mt[..., -1]
        w_s = jnp.exp(b[..., -1:] - b + ic - m_new[..., None])
        decay = jnp.exp(b[..., -1] + m - m_new)
        C_new = decay[..., None, None] * C + jnp.einsum('bhsv,bhsd->bhvd', vc * w_s[..., None], kc)
        n_new = decay[..., None] * n + jnp.einsum('bhs,bhsd->bhd', w_s, kc)
        return (C_new, n_new, m_new), h

    (C, n, m), h = lax.scan(step, (C0.astype(f32), n0.astype(f32), m0.astype(f32)),
                            (chunks(q), chunks(k), chunks(v), chunks(ig), chunks(lf)))
    h = jnp.swapaxes(jnp.moveaxis(h, 0, 1), 2, 3).reshape(B, T, H, -1)
    return h, C, n, m

def _cond_in(x, c, ada_w, ada_b, g_pre):
    mod = jax.nn.silu(c) @ ada_w + ada_b
    shift, scale, gate = jnp.split(mod[:, None, :], 3, axis=-1)
    return _rmsnorm(x, g_pre) * (1 + scale) + shift, gate

def _even_mixer(h, k_past, v_past, pool_prev, pos0, w_in, pool_w, pool_scale, w_out):
    B, T, _ = h.shape
    z = h @ w_in
    q, k, v, ga, u, gb = jnp.split(z, [W_A, 2 * W_A, 3 * W_A, 4 * W_A, 4 * W_A + W_B], axis=-1)
    shp = (B, T, H_A, DH_A)
    q, k, v = q.reshape(shp), k.reshape(shp), v.reshape(shp)
    k_all = k if k_past is None else jnp.concatenate([k_past.astype(k.dtype), k], axis=1)
    v_all = v if v_past is None else jnp.concatenate([v_past.astype(v.dtype), v], axis=1)
    att = _moba_attention(q, k_all, v_all, pos0)
    pooled, pool_new = _multiscale_pool(u, pool_prev, pos0, pool_w, pool_scale)
    y = jnp.concatenate([att * jax.nn.silu(ga), pooled * jax.nn.silu(gb)], axis=-1) @ w_out
    return y, k, v, pool_new

def _odd_mixer(h, C0, n0, m0, w_in, b_i, b_f, hn_gain, w_out):
    B, T, _ = h.shape
    z = h @ w_in
    q, k, v, o, g, gi, gf = jnp.split(z, [W_C, 2 * W_C, 3 * W_C, 4 * W_C, 5 * W_C, 5 * W_C + H_C], axis=-1)
    shp = (B, T, H_C, DH_C)
    ig = (gi + b_i).astype(jnp.float32)
    lf = jax.nn.log_sigmoid((gf + b_f).astype(jnp.float32))
    hc, C, n, m = _mlstm(q.reshape(shp), k.reshape(shp) * DH_C ** -0.5, v.reshape(shp), ig, lf, C0, n0, m0)
    hc = hc * jax.nn.sigmoid(o.reshape(shp).astype(jnp.float32))
    hc = hc * lax.rsqrt(jnp.mean(hc * hc, axis=-1, keepdims=True) + EPS) * hn_gain.reshape(H_C, DH_C).astype(jnp.float32)
    y = (hc.reshape(B, T, W_C).astype(h.dtype) * jax.nn.silu(g)) @ w_out
    return y, C, n, m

def setup_inputs(seed: int = 0) -> dict:
    key = jax.random.key(seed)
    ks = jax.random.split(key, 24)
    f32 = jnp.float32
    n_pages = PAST_LEN // PAGE_SIZE
    n_used = DEC_BATCH * n_pages
    n_phys = n_used + max(1, n_used // 4)
    page_table = jax.random.permutation(ks[0], n_phys)[:n_used].reshape(DEC_BATCH, n_pages).astype(jnp.int32)
    nrm = lambda k, shp, s=1.0: jax.random.normal(k, shp, f32) * s
    return {
        'x_prompt': nrm(ks[1], (BATCH, SEQ, D_MODEL)),
        'x_sample': nrm(ks[2], (DEC_BATCH, DEC_SEQ, D_MODEL)),
        'cache_k': nrm(ks[3], (N_EVEN, n_phys, PAGE_SIZE, H_A, DH_A)),
        'cache_v': nrm(ks[4], (N_EVEN, n_phys, PAGE_SIZE, H_A, DH_A)),
        'state_pool': nrm(ks[5], (N_EVEN, DEC_BATCH, POOL_HIST, W_B)),
        'state_C': nrm(ks[6], (N_ODD, DEC_BATCH, H_C, DH_C, DH_C), DH_C ** -0.5),
        'state_n': nrm(ks[7], (N_ODD, DEC_BATCH, H_C, DH_C), 0.5),
        'state_m': nrm(ks[8], (N_ODD, DEC_BATCH, H_C), 0.5),
        'page_table': page_table,
        'c_prompt': nrm(ks[9], (BATCH, D_MODEL)),
        'c_sample': nrm(ks[10], (DEC_BATCH, D_MODEL)),
        'ada_w': nrm(ks[11], (DEPTH, D_MODEL, 3 * D_MODEL), 0.5 * D_MODEL ** -0.5),
        'ada_b': nrm(ks[12], (DEPTH, 3 * D_MODEL), 0.01),
        'norm_pre': 1.0 + nrm(ks[13], (DEPTH, D_MODEL), 0.05),
        'norm_post': 1.0 + nrm(ks[14], (DEPTH, D_MODEL), 0.05),
        'w_in_even': nrm(ks[15], (N_EVEN, D_MODEL, 4 * W_A + 2 * W_B), D_MODEL ** -0.5),
        'pool_w': nrm(ks[16], (N_EVEN, N_POOL, GW_B, GW_B), GW_B ** -0.5),
        'pool_scale': 1.0 + nrm(ks[17], (N_EVEN, W_B), 0.1),
        'w_out_even': nrm(ks[18], (N_EVEN, W_A + W_B, D_MODEL), (W_A + W_B) ** -0.5),
        'w_in_odd': nrm(ks[19], (N_ODD, D_MODEL, 5 * W_C + 2 * H_C), D_MODEL ** -0.5),
        'b_igate': nrm(ks[20], (N_ODD, H_C), 0.1),
        'b_fgate': F_BIAS + nrm(ks[21], (N_ODD, H_C), 0.5),
        'head_norm': 1.0 + nrm(ks[22], (N_ODD, W_C), 0.05),
        'w_out_odd': nrm(ks[23], (N_ODD, W_C, D_MODEL), W_C ** -0.5),
    }

def reference(x_prompt, x_sample, cache_k, cache_v, state_pool, state_C, state_n, state_m, page_table,
              c_prompt, c_sample, ada_w, ada_b, norm_pre, norm_post, w_in_even, pool_w, pool_scale,
              w_out_even, w_in_odd, b_igate, b_fgate, head_norm, w_out_odd):
    xp, xs = x_prompt, x_sample
    bp, bs = x_prompt.shape[0], x_sample.shape[0]
    kp_l, vp_l, ks_l, vs_l, pp_l, ps_l = [], [], [], [], [], []
    Cp_l, np_l, mp_l, Cs_l, ns_l, ms_l = [], [], [], [], [], []
    for l in range(DEPTH):
        hp, gp = _cond_in(xp, c_prompt, ada_w[l], ada_b[l], norm_pre[l])
        hs, gs = _cond_in(xs, c_sample, ada_w[l], ada_b[l], norm_pre[l])
        if l % 2 == 0:
            e = l // 2
            prev0 = jnp.zeros((bp, POOL_HIST, W_B), xp.dtype)
            yp, kp, vp, pp = _even_mixer(hp, None, None, prev0, 0,
                                         w_in_even[e], pool_w[e], pool_scale[e], w_out_even[e])
            k_past = cache_k[e][page_table].reshape(bs, -1, H_A, DH_A)
            v_past = cache_v[e][page_table].reshape(bs, -1, H_A, DH_A)
            ys, kn, vn, ps = _even_mixer(hs, k_past, v_past, state_pool[e], k_past.shape[1],
                                         w_in_even[e], pool_w[e], pool_scale[e], w_out_even[e])
            kp_l.append(kp); vp_l.append(vp); ks_l.append(kn); vs_l.append(vn)
            pp_l.append(pp); ps_l.append(ps.astype(state_pool.dtype))
        else:
            o = l // 2
            C0 = jnp.zeros((bp, H_C, DH_C, DH_C), jnp.float32)
            n0 = jnp.zeros((bp, H_C, DH_C), jnp.float32)
            m0 = jnp.zeros((bp, H_C), jnp.float32)
            yp, Cp, npr, mp = _odd_mixer(hp, C0, n0, m0, w_in_odd[o], b_igate[o], b_fgate[o], head_norm[o], w_out_odd[o])
            ys, Cs, ns, ms = _odd_mixer(hs, state_C[o], state_n[o], state_m[o],
                                        w_in_odd[o], b_igate[o], b_fgate[o], head_norm[o], w_out_odd[o])
            Cp_l.append(Cp); np_l.append(npr); mp_l.append(mp)
            Cs_l.append(Cs.astype(state_C.dtype)); ns_l.append(ns.astype(state_n.dtype)); ms_l.append(ms.astype(state_m.dtype))
        xp = xp + gp * _rmsnorm(yp, norm_post[l])
        xs = xs + gs * _rmsnorm(ys, norm_post[l])
    return (xp, xs,
            jnp.stack(kp_l), jnp.stack(vp_l), jnp.stack(ks_l), jnp.stack(vs_l),
            jnp.stack(pp_l), jnp.stack(ps_l),
            jnp.stack(Cp_l), jnp.stack(np_l), jnp.stack(mp_l),
            jnp.stack(Cs_l), jnp.stack(ns_l), jnp.stack(ms_l))


_drawn_inputs = setup_inputs


def setup_inputs(seed=0):
    import zlib

    import numpy as np

    out = dict(_drawn_inputs(seed))
    spreads = {}
    factors = {}
    for name, (base, spread) in spreads.items():
        noise = np.random.default_rng([zlib.crc32(name.encode()), seed]).standard_normal(out[name].shape)
        drawn = base * np.exp(spread * noise) if base else spread * noise
        out[name] = __import__('jax').numpy.asarray(drawn.astype(out[name].dtype))
    for name, factor in factors.items():
        out[name] = (out[name] * factor).astype(out[name].dtype)
    return out
```

```python
import math
from contextlib import ExitStack, contextmanager

import concourse.bass as bass
from concourse import mybir

F32 = mybir.dt.float32
I32 = mybir.dt.int32
ALU = mybir.AluOpType
ACT = mybir.ActivationFunctionType
AX = mybir.AxisListType

P = 128
D = 2048
KC = D // P
TP, SB, ST = 256, 8, 4
TS = SB * ST
NT = TP + TS
NC = 1 + SB
H = 8
DH = 128
WA = H * DH
PAGES, PAGE = 8, 128
PAST = PAGES * PAGE
BLOCK = 256
NB = PAST // BLOCK
WINDOWS = (2, 4, 8, 16)
HIST = 15
GW = 256
DC = 256
EPS = 1e-6
BIG = 1e30
SCALE = DH ** -0.5
KSCALE = DC ** -0.5
N_SMALL = 12
SLOTS_FOR = dict(ada=(0, 1, 2), even=(0, 1, 2, 0, 1, 2), out=(0, 1), odd=(0, 1, 2, 0, 1))
TRIPS = dict(ada=8, even=4, out=4, odd=8)
PHASES = (("ada0", "ada"), ("even", "even"), ("out0", "out"), ("ada1", "ada"), ("odd", "odd"), ("out1", "out"))
CONST = {}
_at = 0
for _n, _w in (("ident", P), ("dist", 384), ("slope", H), ("cneg", 384), ("sbias", PAST), ("own", SB * TS), ("sneg", TS),
               ("bsel", SB), ("eps", 1), ("keep", NT), ("cut", NT), ("invcnt", 64), ("rank", NB)):
    CONST[_n] = (_at, _at + _w)
    _at += _w
CW = _at


def slab_plan():
    first, slot, uses, before = {}, [], [], []
    last, count = {}, {}
    for name, kind in PHASES:
        first[name] = len(slot)
        for s in SLOTS_FOR[kind] * TRIPS[kind]:
            count[s] = count.get(s, 0) + 1
            slot.append(s)
            uses.append(count[s])
            before.append(last.get(s))
            last[s] = len(slot) - 1
    return first, slot, uses, before


class Count:

    def __init__(self, sem):
        self.sem, self.base, self.k, self.i, self.per = sem, 0, 0, None, 0

    def inc(self, ins):
        self.k += 1
        return ins.then_inc(self.sem, 1)

    def value(self):
        return self.base + self.k if self.i is None else self.i * self.per + (self.base + self.k)

    def enter(self, i, per):
        self.base, self.k, self.i, self.per = self.base + self.k, 0, i, per

    def leave(self, trips):
        assert self.k == self.per, f"{self.k} increments a turn, {self.per} said"
        self.base, self.k, self.i = self.base + trips * self.per, 0, None


def trunk_kernel(nc, A, OUT):
    first, slot, uses, before = slab_plan()
    ctx = ExitStack()
    with ctx:
        def sb(name, shape, dt=F32):
            return ctx.enter_context(nc.sbuf_tensor(name, shape, dt))

        def sem(name):
            return ctx.enter_context(nc.semaphore(name))

        wbuf = sb("wbuf", [P, 3, KC, GW])
        xT = sb("xT", [P, KC, NT])
        hT = sb("hT", [P, KC, NT])
        yT = sb("yT", [P, KC, NT])
        modT = sb("modT", [P, 2 * 48, NC])
        cst = sb("cst", [P, CW])
        ones = sb("ones", [P, P])
        prm = sb("prm", [P, 96 + 88])
        scT = sb("scT", [P, KC, NC])
        rstd = sb("rstd", [P, NT])
        bif = sb("bif", [H, 2])
        m0 = sb("m0", [H, NT])
        ptab = sb("ptab", [1, SB * PAGES], I32)
        arena_words = 22200
        arena = sb("arena", [P, arena_words])

        def const(name, rows=P):
            a, b = CONST[name]
            return cst[0:rows, a:b]

        ident = const("ident")
        eps = const("eps")
        adab = prm[:, 0:96]
        npre, npost = prm[:, 96:128], prm[:, 128:160]
        pscale, hgain = prm[:, 160:168], prm[:, 168:184]

        class Arena:

            def __init__(self):
                self.at = 0

            def take(self, rows, *dims):
                n = math.prod(dims)
                ap = arena[0:rows, self.at:self.at + n]
                self.at += n
                assert self.at <= arena_words, self.at
                if len(dims) == 2:
                    return ap.rearrange("p (a b) -> p a b", b=dims[1])
                if len(dims) == 3:
                    return ap.rearrange("p (a b c) -> p a b c", b=dims[1], c=dims[2])
                return ap

        bank = [ctx.enter_context(nc.psum_tensor(f"bank{i}", [P, 512], F32)) for i in range(4)]
        pair = [ctx.enter_context(nc.psum_tensor(f"pair{i}", [P, 1024], F32)) for i in range(2)]
        bank += [pair[0][:, 0:512], pair[0][:, 512:1024], pair[1][:, 0:512], pair[1][:, 512:1024]]
        proj = bank[0:2]

        w_loaded = [sem(f"w_loaded{s}") for s in range(3)]
        proj_ready = sem("proj_ready")
        proj_free = sem("proj_free")
        act_order, dve_order = sem("act_order"), sem("dve_order")
        phase_met = sem("phase_met")
        small_loaded = sem("small_loaded")
        ptab_loaded = sem("ptab_loaded")
        stored = sem("stored")
        block = ctx.enter_context(nc.Block())

        pe, act, dve, pool, sp = nc.tensor, nc.scalar, nc.vector, nc.gpsimd, nc.sync

        class Own:

            def __init__(self, eng, order):
                self.eng, self.order, self.counts, self.turn = eng, order, {}, None

            def count(self, s):
                if s.name not in self.counts:
                    self.counts[s.name] = Count(s)
                    if self.turn:
                        self.counts[s.name].enter(*self.turn_of(s.name))
                return self.counts[s.name]

            def turn_of(self, name):
                i, per = self.turn
                return i, per.get(name, 0)

            def credit(self, s, n):
                c = self.count(s)
                c.k += n
                self.eng.sem_inc(s, n)

            def link(self, ins, s=None):
                c = self.count(self.order if s is None else s)
                c.inc(ins)
                self.eng.wait_ge(c.sem, c.value())

            @contextmanager
            def turns(self, start, end, **per):
                with self.eng.Fori(start, end) as i:
                    self.turn = ((i - start) if start else i, per)
                    for name, c in self.counts.items():
                        c.enter(*self.turn_of(name))
                    yield i
                    did = {n: c.k for n, c in self.counts.items() if c.k}
                    assert did == per, f"a turn raises {did}"
                    for c in self.counts.values():
                        c.leave(end - start)
                    self.turn = None

        AO, VO = Own(act, act_order), Own(dve, dve_order)
        def apart(eng):
            eng.wait_ge(small_loaded, 16 * N_SMALL)

        n_store = [0]

        def store(out, in_, slow=False):
            n_store[0] += 1
            act.dma_start(out, in_, allow_slow_non_contiguous=slow).then_inc(stored, 16)

        S = {}

        def signals(*names):
            for n in names:
                S[n] = sem(n)

        signals("c_exp", "c_silu", "c_turned", "c_read", "prm_turned", "x_turned", "x_read", "ones_set")
        for k in ("pre0", "post0", "pre1", "post1"):
            signals(f"{k}_squared", f"{k}_summed", f"{k}_rstd", f"{k}_done")
        signals("mod_turned0", "mod_turned1", "mod_read")
        signals("ga_exp", "gb_exp", "scores", "scores_read", "x_max", "p_exp", "p_ready", "pt_turned",
                "pt_read", "ktok_turned", "ktok_read", "vtok_turned", "vtok_read", "att_out", "att_read")
        signals("hist_turned", "hist_read", "u_turned", "u_read", "d_ready", "pool_out", "pool_read", "pool_loaded")
        signals("qk_kept", "silu_gb", "gate_done", "cp_stored", "kt_turned", "kt_read_act", "kt_read_dve", "s_scores", "s_read", "s_max", "s_exp", "s_ready", "s_turned", "s_pt", "s_out", "s_out_read", "qm_ready", "v_used", "s_rows", "s_rows_read")
        k_loaded = [sem(f"k_loaded{s}") for s in range(4)]
        v_loaded = [sem(f"v_loaded{s}") for s in range(4)]
        signals("gate_sums", "g_ln", "gl_ready", "rows_ready", "cw_turned", "cw_read", "wg_loaded", "sn_loaded",
                "sn_turned", "m0_loaded", "gx")
        signals("rm", "nm_bc", "kt_t", "kt_r", "vt_t", "vt_r", "st", "e_in", "e_exp", "w_ready", "bc2", "bc2_r",
                "smp_t", "smp_r", "sst", "ws_ready", "kw_ready", "qi_ready", "km_ready", "wc_ready", "ct_t", "ct_r", "outer", "c_new", "num_ready", "ns_ready", "ns_read", "num_read", "den_ready", "den_read", "cp_ready", "cp_read",
                "hs_squared", "hs_summed", "hs_read", "hs_rstd", "hs_done", "n_turned", "n_read")
        c_loaded = [sem(f"c_loaded{s}") for s in range(8)]
        c_stored = [sem(f"c_stored{s}") for s in range(8)]
        signals("y_turned", "y_read")

        def wview(w):
            return w.rearrange("(kc p) n -> p kc n", p=P)

        w_ada = [wview(A["ada_w"][l, :, :]) for l in range(2)]
        w_even = wview(A["w_in_even"][0, :, :])
        w_out = [wview(A["w_out_even"][0, :, :]), wview(A["w_out_odd"][0, :, :])]
        w_odd = wview(A["w_in_odd"][0, :, :])
        kpage = A["cache_k"][0].rearrange("g t h d -> t g (h d)")
        vpage = A["cache_v"][0].rearrange("g t h d -> t g (h d)")
        stateC = A["state_C"][0].rearrange("b h (v p) d -> p b h v d", p=P)
        outC = OUT["C_sample"][0].rearrange("b h (v p) d -> p b h v d", p=P)

        EVEN_COL = [j * WA for j in range(6)]
        ODD_COL = [0, D, 2 * D, 3 * D, 4 * D]

        ar = Arena()
        xin = ar.take(P, 2, D)
        xsin = ar.take(TS, D)
        cin = ar.take(NC, D)
        cexp = ar.take(NC, D)
        prow = ar.take(P, 2, P)
        mod_rows = [ar.take(NC, 3 * D)]
        mod_at = 4096 + 576
        ar.at = mod_at
        mod_rows.append(ar.take(NC, 3 * D))

        ar = Arena()
        kring = ar.take(P, 4, WA)
        vring = ar.take(P, 4, WA)
        qTs = ar.take(P, H, TS)
        kTs = ar.take(P, H, TS)
        gas = ar.take(P, H, TS)
        vtok_s = ar.take(TS, WA)
        gbs = ar.take(P, 8, NT)
        even_common = ar.at
        ktok_s = ar.take(TS, WA)
        zq = ar.take(P, 2, NT)
        zk = ar.take(P, 2, NT)
        zv = ar.take(P, 2, NT)
        zga = ar.take(P, 2, NT)
        ega = ar.take(P, 2, NT)
        egb = ar.take(P, 2, NT)
        xs = [ar.take(P, 384) for _ in range(2)]
        pts = [ar.take(P, 384) for _ in range(2)]
        vtok = ar.take(P, 2, GW)
        ktok = ar.take(P, 2, GW)
        stat = ar.take(P, 4, 4)
        ar.at = even_common + WA
        hist = ar.take(120, WA)
        uext = [ar.take(P, 2, 16 + TP) for _ in range(2)]
        sext = ar.take(P, 8, SB * 19)
        swin = [ar.take(P, 2 * SB, 19) for _ in range(2)]
        dT = ar.take(P, 2, NT)
        pw = ar.take(P, 8, GW)
        utok = ar.take(HIST, WA)
        ustok = ar.take(TS, WA)
        ar.at = even_common
        ktp = [ar.take(P, 2, 512) for _ in range(2)]
        qm = [ar.take(P, H * (TS + ST))]
        XW = PAST + TS
        sx = [ar.take(TS, XW)]
        pT = ar.take(P, 9 * TS)
        so = ar.take(TS, WA)
        sstat = ar.take(TS, 16)

        ar = Arena()
        cring = ar.take(P, 8, 2 * DC)
        oz = {n: ar.take(P, 2, NT) for n in ("k", "q", "eo", "g", "eg")}
        ozv = ar.take(P, 2, NT)
        tk_at = ar.at
        otk = ar.take(P, 2, DC)
        otv = ar.take(P, 2, DC)
        kw_at = ar.at
        okw = ar.take(P, 2, DC)
        otks = ar.take(TS, DC)
        otvs = ar.take(TS, DC)
        okm = ar.take(TS, SB, DC)
        oct_ = [ar.take(P, 2, DC) for _ in range(2)]
        oe = ar.take(P, 384 + TS)
        ow = ar.take(P, 384 + TS)
        ocp = ar.take(P, 2 * DC)
        obc = ar.take(P, NT + TS)
        odd_ = ar.take(P, NT)
        ort = ar.take(P, 2, NT)
        oqi = ar.take(P, 2, TS)
        oqm = ar.take(P, 2, SB * (TS + ST))
        ons = ar.take(TS, DC)
        onq = ar.take(P, 2, TS)
        gain_at = ar.at
        ogain = ar.take(P, KC, NT)
        rows = ar.take(H, 3 * NT)
        rsel = ar.take(H, P)
        cT = ar.take(P, 3, H)
        wT = ar.take(P, 3, H)
        wcol = ar.take(P, 2)
        wm = ar.take(TS, SB)
        nT = ar.take(P, 2, SB * H)
        nnew = ar.take(P, 2, SB * H)
        nprm = ar.take(P, 2, H)
        ar.at = gain_at
        gr = {n: ar.take(H, NT) for n in ("ig", "lf", "t1", "b", "c", "M", "w")}
        wg = ar.take(P, KC, 2 * H)
        snin = ar.take(SB * H, DC)
        ar.at = kw_at
        nout = ar.take(SB * H, 2, P)
        ar.at = tk_at
        npout = ar.take(H, 2, P)

        def load_slab(n, src, held=None):
            if held is not None:
                sp.wait_ge(proj_ready, held)
            sp.dma_start(wbuf[:, slot[n], :, :], src).then_inc(w_loaded[slot[n]], 16)

        def free_after(n):
            return None if before[n] is None else 2 * (before[n] + 1)

        def load_phase(name, kind, source, first_turn_ready=None):
            per = len(SLOTS_FOR[kind])
            base = first[name]
            for j in range(per):
                load_slab(base + j, source(0, j), free_after(base + j))
            with sp.Fori(1, TRIPS[kind]) as i:
                for j in range(per):
                    n = base + per + j
                    assert free_after(n) == free_after(n + per) - 2 * per
                    load_slab(n, source(i, j), (i - 1) * (2 * per) + free_after(n))

        def cols(view, start):
            return view[:, :, bass.ds(start, GW)]

        def load_odd():
            base, per = first["odd"], 5
            for j in range(per):
                load_slab(base + j, cols(w_odd, ODD_COL[j]), free_after(base + j))
                if j == 2:
                    sp.wait_ge(phase_met, 12)
                    for b in range(SB):
                        sp.dma_start(cring[:, b, :].rearrange("p (v d) -> p v d", v=2), stateC[:, b, 0, :, :]).then_inc(c_loaded[b], 16)
            with sp.Fori(1, H) as h:
                for j in range(per):
                    n = base + per + j
                    load_slab(n, cols(w_odd, h * GW + ODD_COL[j]), (h - 1) * (2 * per) + free_after(n))
                    if j == 3:
                        for b in range(SB):
                            sp.wait_ge(c_stored[b], h * 16)
                            sp.dma_start(cring[:, b, :].rearrange("p (v d) -> p v d", v=2),
                                         stateC[:, b, bass.ds(h, 1), :, :].rearrange("p h v d -> p (h v) d")).then_inc(c_loaded[b], 16)

        @block.sync
        def _(eng):
            load_phase("ada0", "ada", lambda i, j: cols(w_ada[0], i * (3 * GW) + j * GW))
            load_phase("even", "even", lambda i, j: cols(w_even, i * GW + EVEN_COL[j]))
            sp.wait_ge(phase_met, 3)
            sp.wait_ge(ptab_loaded, 16)

            def load_pages(b, ring, cache, loaded, freed, per_page, first_turn):
                for j in range(PAGES):
                    if not (first_turn and j < 4):
                        sp.wait_ge(freed, b * (PAGES * per_page) + (j - 3) * per_page)
                    page = sp.value_load(ptab[0:1, bass.ds(b * PAGES + j, 1)], min_val=0, max_val=79)
                    sp.dma_start(ring[:, j % 4, :], cache[:, bass.ds(page, 1), :].rearrange("t g x -> t (g x)"))\
                      .then_inc(loaded[j % 4], 16)

            load_pages(0, kring, kpage, k_loaded, S["kt_turned"], 2, True)
            load_pages(1, kring, kpage, k_loaded, S["kt_turned"], 2, False)
            load_pages(0, vring, vpage, v_loaded, S["v_used"], 1, True)
            with sp.Fori(2, SB) as b:
                load_pages(b, kring, kpage, k_loaded, S["kt_turned"], 2, False)
                load_pages(b - 1, vring, vpage, v_loaded, S["v_used"], 1, False)
            load_pages(SB - 1, vring, vpage, v_loaded, S["v_used"], 1, False)
            load_phase("out0", "out", lambda i, j: cols(w_out[0], i * (2 * GW) + j * GW))
            load_phase("ada1", "ada", lambda i, j: cols(w_ada[1], i * (3 * GW) + j * GW))
            load_odd()
            load_phase("out1", "out", lambda i, j: cols(w_out[1], i * (2 * GW) + j * GW))

        @block.gpsimd
        def _(eng):
            with pool.Fori(0, H) as h:
                for b in range(SB):
                    pool.wait_ge(S["c_new"], h * SB + (b + 1))
                    pool.dma_start(outC[:, b, bass.ds(h, 1), :, :].rearrange("p h v d -> p (h v) d"),
                                   cring[:, b, :].rearrange("p (v d) -> p v d", v=2)).then_inc(c_stored[b], 16)
            for b in range(SB):
                pool.wait_ge(c_stored[b], 16 * H)

        def slab_count(n0, i, per_phase, j):
            return i * per_phase + (n0 + j)

        def turn(out, in_, rows, width):
            return pe.transpose(out, in_, ident[0:rows, 0:rows])

        @block.tensor
        def _(eng):
            def product(phase, kind, i, j, rhs, width):
                per, n = len(SLOTS_FOR[kind]), first[phase] + j
                s = slot[n]
                pe.wait_ge(w_loaded[s], i * (16 * SLOTS_FOR[kind].count(s)) + 16 * uses[n])
                for mt in range(2):
                    pe.wait_ge(proj_free, i * (2 * per) + (2 * n + mt + 1))
                    for kc in range(KC):
                        last = pe.matmul(proj[mt][:, 0:width], wbuf[:, s, kc, mt * P:(mt + 1) * P], rhs[:, kc, 0:width],
                                         start=kc == 0, stop=kc == KC - 1)
                    last.then_inc(proj_ready, 1)

            def product_c(phase, i, j):
                n = first[phase] + j
                s = slot[n]
                pe.wait_ge(w_loaded[s], i * 16 + 16 * uses[n])
                for mt in range(2):
                    pe.wait_ge(proj_free, i * 6 + (2 * n + mt + 1))
                    for kc in range(KC):
                        last = pe.matmul(proj[mt][0:NC, 0:P], scT[:, kc, :], wbuf[:, s, kc, mt * P:(mt + 1) * P],
                                         start=kc == 0, stop=kc == KC - 1)
                    last.then_inc(proj_ready, 1)

            def turn_mod(l):
                pe.wait_ge(proj_free, 2 * (first[f"ada{l}"] + 3 * TRIPS["ada"]) + 2)
                for c in range(48):
                    last = turn(bank[2][:, c * NC:(c + 1) * NC], mod_rows[l][:, c * P:(c + 1) * P], NC, P)
                last.then_inc(S[f"mod_turned{l}"], 1)

            def wait_read(phase, kind, i, j):
                pe.wait_ge(proj_free, i * (2 * len(SLOTS_FOR[kind])) + (2 * (first[phase] + j) + 4))

            def sum_squares(key):
                for q in range(4):
                    pe.wait_ge(S[f"{key}_squared"], q + 1)
                    for c in range(4 * q, 4 * q + 4):
                        last = pe.matmul(bank[4][:, 0:NT], ones[:, :], yT[:, c, :], start=c == 0, stop=c == KC - 1)
                last.then_inc(S[f"{key}_summed"], 1)

            def meet(own_last, value):
                pe.wait_ge(own_last, value)
                pe.sem_inc(phase_met, 1)

            pe.wait_ge(small_loaded, 16 * N_SMALL)
            turn(bank[5][:, 0:96], prow[0:96, 0, :], 96, P)
            turn(bank[5][:, 96:184], prow[0:88, 1, :], 88, P).then_inc(S["prm_turned"], 1)
            for c in range(KC):
                if c >= 2:
                    pe.wait_ge(S["x_read"], c - 1)
                b = bank[6 + c % 2]
                turn(b[:, 0:P], xin[:, 0, c * P:(c + 1) * P], P, P)
                turn(b[:, P:2 * P], xin[:, 1, c * P:(c + 1) * P], P, P)
                turn(b[:, TP:NT], xsin[:, c * P:(c + 1) * P], TS, P).then_inc(S["x_turned"], 1)
            pe.wait_ge(S["c_silu"], 1)
            for c in range(KC):
                last = turn(bank[2][:, c * NC:(c + 1) * NC], cin[:, c * P:(c + 1) * P], NC, P)
            last.then_inc(S["c_turned"], 1)
            pe.wait_ge(S["ones_set"], 1)
            sum_squares("pre0")

            pe.wait_ge(S["c_read"], 1)
            with pe.Fori(0, TRIPS["ada"]) as i:
                for j in range(3):
                    product_c("ada0", i, j)

            turn_mod(0)
            meet(S["mod_turned0"], 1)

            pe.wait_ge(S["pre0_done"], 1)
            pe.wait_ge(phase_met, 3)
            with pe.Fori(0, TRIPS["even"]) as g:
                product("even", "even", g, 0, hT, NT)
                product("even", "even", g, 1, hT, NT)
                product("even", "even", g, 2, hT, NT)
                wait_read("even", "even", g, 1)
                pe.wait_ge(S["att_read"], g + 1)
                for hh in range(2):
                    pe.matmul(bank[2 + hh][:, 0:P], zq[:, hh, 0:P], zk[:, hh, 0:P], start=True, stop=True)
                    pe.matmul(bank[2 + hh][:, P:384], zq[:, hh, P:TP], zk[:, hh, 0:TP], start=True, stop=True)\
                      .then_inc(S["scores"], 1)
                for z, turned in ((zk, "ktok_turned"), (zv, "vtok_turned")):
                    if z is zv:
                        product("even", "even", g, 3, hT, NT)
                        pe.wait_ge(S["ktok_read"], g + 1)
                    for hh in range(2):
                        for tc in range(2):
                            turn(bank[4][:, tc * GW + hh * P:tc * GW + (hh + 1) * P], z[:, hh, tc * P:(tc + 1) * P], P, P)
                        last = turn(bank[5][0:TS, hh * P:(hh + 1) * P], z[:, hh, TP:NT], P, TS)
                    last.then_inc(S[turned], 1)
                product("even", "even", g, 4, hT, NT)
                for hh in range(2):
                    pe.wait_ge(S["p_ready"], g * 2 + (hh + 1))
                    for k in range(3):
                        last = turn(bank[6 + hh][:, k * P:(k + 1) * P], xs[hh][:, k * P:(k + 1) * P], P, P)
                    last.then_inc(S["pt_turned"], 1)
                product("even", "even", g, 5, hT, NT)
                pe.wait_ge(S["vtok_read"], g + 1)
                for hh in range(2):
                    pe.wait_ge(S["pt_read"], g * 2 + (hh + 1))
                    v = vtok[:, :, hh * P:(hh + 1) * P]
                    pe.matmul(bank[2][:, hh * TP:(hh + 1) * TP], v[:, 0, :], pts[hh][:, 0:TP], start=True, stop=True)
                    last = pe.matmul(bank[2][:, hh * TP + P:(hh + 1) * TP], v[:, 1, :], pts[hh][:, TP:384], start=False, stop=True,
                                     skip_group_check=True)
                last.then_inc(S["att_out"], 1)
            meet(S["att_out"], TRIPS["even"])

            pe.wait_ge(phase_met, 6)
            pe.wait_ge(S["pool_loaded"], 32)
            for c in range(8):
                b = bank[2 + c // 4]
                last = turn(b[:, (c % 4) * 120:(c % 4 + 1) * 120], hist[:, c * P:(c + 1) * P], 120, P)
            last.then_inc(S["hist_turned"], 1)
            for c in range(8):
                turn(pair[0][0:HIST, c * P:(c + 1) * P], yT[:, 8 + c, TP - HIST:TP], P, HIST)
                last = turn(pair[1][0:TS, c * P:(c + 1) * P], yT[:, 8 + c, TP:NT], P, TS)
            last.then_inc(S["u_turned"], 1)
            for g in range(4):
                pe.wait_ge(S["d_ready"], g + 1)
                if g == 0:
                    pe.wait_ge(S["hist_read"], 2)
                if g == 1:
                    pe.wait_ge(S["u_read"], 1)
                if g >= 2:
                    pe.wait_ge(S["pool_read"], 2 * (g - 1))
                for mt in range(2):
                    for cc in range(2):
                        last = pe.matmul(bank[2 + 2 * (g % 2) + mt][:, 0:NT], pw[:, 2 * g + cc, mt * P:(mt + 1) * P], dT[:, cc, :],
                                         start=cc == 0, stop=cc == 1)
                last.then_inc(S["pool_out"], 1)
            meet(S["pool_out"], 4)

            pe.wait_ge(phase_met, 9)

            def turn_page(b, j):
                pe.wait_ge(k_loaded[j % 4], b * 32 + 16 * (j // 4 + 1))
                pe.wait_ge(S["kt_read_act"], b * PAGES + (j + 1))
                pe.wait_ge(S["kt_read_dve"], b * PAGES + (j + 1))
                for hh in range(2):
                    for h in range(4):
                        last = turn(bank[hh][:, h * P:(h + 1) * P], kring[:, j % 4, (4 * hh + h) * P:(4 * hh + h + 1) * P], P, P)
                    last.then_inc(S["kt_turned"], 1)

            def sample_scores(b):
                turn_page(b, 0)
                pe.wait_ge(S["qm_ready"], b + 1)
                pe.wait_ge(S["s_read"], b + 1)
                for j in range(PAGES):
                    pe.wait_ge(S["kt_read_act"], b * PAGES + (j + 2))
                    pe.wait_ge(S["kt_read_dve"], b * PAGES + (j + 2))
                    if j + 1 < PAGES:
                        turn_page(b, j + 1)
                    for h in range(H):
                        pe.matmul(pair[0][0:TS, j * PAGE:(j + 1) * PAGE], qm[0][:, h * TS:(h + 1) * TS],
                                  ktp[j % 2][:, h // 4, (h % 4) * P:(h % 4 + 1) * P], start=h == 0, stop=h == H - 1)
                for h in range(H):
                    last = pe.matmul(bank[2][0:TS, 0:TS], qm[0][:, h * TS:(h + 1) * TS], kTs[:, h, :], start=h == 0, stop=h == H - 1)
                last.then_inc(S["s_scores"], 1)

            def sample_values(b):
                apart(pe)
                pe.wait_ge(S["s_ready"], b + 1)
                pe.wait_ge(S["s_out_read"], b + 1)
                for j in range(PAGES):
                    turn(bank[3][:, j * TS:(j + 1) * TS], sx[0][:, j * PAGE:(j + 1) * PAGE], TS, P)
                turn(bank[3][0:TS, PAGES * TS:(PAGES + 1) * TS], sx[0][:, PAST:XW], TS, TS).then_inc(S["s_turned"], 1)
                pe.wait_ge(S["s_pt"], b + 1)
                for j in range(PAGES):
                    pe.wait_ge(v_loaded[j % 4], b * 32 + 16 * (j // 4 + 1))
                    for half in range(2):
                        last = pe.matmul(pair[1][0:TS, half * 512:(half + 1) * 512], pT[:, j * TS:(j + 1) * TS],
                                         vring[:, j % 4, half * 512:(half + 1) * 512], start=j == 0, stop=False)
                    last.then_inc(S["v_used"], 1)
                for half in range(2):
                    last = pe.matmul(pair[1][0:TS, half * 512:(half + 1) * 512], pT[0:TS, PAGES * TS:(PAGES + 1) * TS],
                                     vtok_s[:, half * 512:(half + 1) * 512], start=False, stop=True)
                last.then_inc(S["s_rows"], 1)
                apart(pe)
                pe.wait_ge(S["s_rows_read"], b + 1)
                for h in range(H):
                    last = turn(bank[3][:, h * TS:(h + 1) * TS], so[:, h * P:(h + 1) * P], TS, P)
                last.then_inc(S["s_out"], 1)

            sample_scores(0)
            with pe.Fori(1, SB) as b:
                sample_scores(b)
                sample_values(b - 1)
            sample_values(SB - 1)
            meet(S["s_out"], SB)

            pe.wait_ge(phase_met, 12)
            with pe.Fori(0, TRIPS["out"]) as i:
                for j in range(2):
                    product("out0", "out", i, j, yT, NT)
            sum_squares("post0")
            with pe.Fori(0, TRIPS["ada"] // 2) as i:
                for j in range(3):
                    product_c("ada1", i, j)
            sum_squares("pre1")
            with pe.Fori(TRIPS["ada"] // 2, TRIPS["ada"]) as i:
                for j in range(3):
                    product_c("ada1", i, j)

            turn_mod(1)

            pe.wait_ge(S["wg_loaded"], 16)
            pe.wait_ge(S["sn_loaded"], 16)
            for dc in range(2):
                last = turn(bank[4][:, dc * 64:(dc + 1) * 64], snin[:, dc * P:(dc + 1) * P], 64, P)
            last.then_inc(S["sn_turned"], 1)
            pe.wait_ge(S["pre1_done"], 1)
            for k in range(2):
                for kc in range(KC):
                    last = pe.matmul(bank[2 + k][0:H, 0:NT], wg[:, kc, k * H:(k + 1) * H], hT[:, kc, :], start=kc == 0, stop=kc == KC - 1)
            last.then_inc(S["gate_sums"], 1)
            pe.wait_ge(S["rows_ready"], 1)
            for k, r in enumerate((gr["c"], gr["w"])):
                for s in range(3):
                    n = P if s < 2 else TS
                    last = turn(bank[5][0:n, 24 * k + 8 * s:24 * k + 8 * s + 8], r[:, s * P:s * P + n], H, n)
            last.then_inc(S["cw_turned"], 1)
            pe.wait_ge(S["cw_read"], 1)

            with pe.Fori(0, H) as h:
                product("odd", "odd", h, 0, hT, NT)
                product("odd", "odd", h, 1, hT, NT)
                wait_read("odd", "odd", h, 1)
                for tc in range(2):
                    for dc in range(2):
                        last = turn(bank[5][:, tc * DC + dc * P:tc * DC + (dc + 1) * P], oz["k"][:, dc, tc * P:(tc + 1) * P], P, P)
                last.then_inc(S["kt_t"], 1)
                pe.wait_ge(S["rm"], h + 1)
                pe.matmul(bank[6][:, 0:NT], rsel[:, :], rows[:, 0:NT], start=True, stop=True).then_inc(S["nm_bc"], 1)
                product("odd", "odd", h, 2, hT, NT)
                pe.wait_ge(S["cp_read"], h + 1)
                for dc in range(2):
                    pe.matmul(bank[7][:, 0:TP], oz["k"][:, dc, 0:P], oz["q"][:, dc, 0:TP], start=dc == 0, stop=dc == 1)
                for dc in range(2):
                    last = pe.matmul(bank[7][:, TP:384], oz["k"][:, dc, P:TP], oz["q"][:, dc, P:TP], start=dc == 0, stop=dc == 1)
                last.then_inc(S["st"], 1)
                pe.wait_ge(S["kt_r"], h + 1)
                wait_read("odd", "odd", h, 2)
                for tc in range(2):
                    for dc in range(2):
                        last = turn(bank[5][:, tc * DC + dc * P:tc * DC + (dc + 1) * P], ozv[:, dc, tc * P:(tc + 1) * P], P, P)
                last.then_inc(S["vt_t"], 1)
                pe.wait_ge(S["e_in"], h + 1)
                pe.matmul(bank[6][:, 0:NT], rsel[:, :], rows[:, NT:2 * NT], start=True, stop=True)
                pe.matmul(bank[6][:, NT:NT + TS], rsel[:, :], rows[:, 2 * NT + TP:3 * NT], start=True, stop=True).then_inc(S["bc2"], 1)
                product("odd", "odd", h, 3, hT, NT)
                pe.wait_ge(S["vt_r"], h + 1)
                for k, z in enumerate((oz["k"], ozv)):
                    for dc in range(2):
                        last = turn(bank[5][0:TS, k * DC + dc * P:k * DC + (dc + 1) * P], z[:, dc, TP:NT], P, TS)
                last.then_inc(S["smp_t"], 1)
                pe.wait_ge(S["w_ready"], h + 1)
                pe.wait_ge(S["num_read"], h + 1)
                for vc in range(2):
                    pe.matmul(bank[2 + vc][:, 0:TP], otv[:, 0, vc * P:(vc + 1) * P], ow[:, 0:TP], start=True, stop=True)
                    pe.matmul(bank[2 + vc][:, P:TP], otv[:, 1, vc * P:(vc + 1) * P], ow[:, TP:384], start=False, stop=True, skip_group_check=True)
                for dc in range(2):
                    last = pe.matmul(bank[7][0:TS, 0:TS], oz["k"][:, dc, TP:NT], oz["q"][:, dc, TP:NT], start=dc == 0, stop=dc == 1)
                last.then_inc(S["sst"], 1)
                product("odd", "odd", h, 4, hT, NT)
                apart(pe)
                pe.wait_ge(S["smp_r"], h + 1)
                pe.wait_ge(S["ws_ready"], h + 1)
                pe.matmul(bank[2][0:TS, DC:2 * DC], ow[0:TS, 384:384 + TS], otvs[:, :], start=True, stop=False)
                pe.wait_ge(S["den_read"], h + 1)
                pe.wait_ge(S["wc_ready"], h + 1)
                pe.wait_ge(S["qi_ready"], h + 1)
                pe.matmul(bank[4][:, 0:TP], ones[:, :], ow[:, 0:TP], start=True, stop=True)
                pe.matmul(bank[4][:, P:TP], ones[:, :], ow[:, TP:384], start=False, stop=True, skip_group_check=True)
                pe.matmul(bank[4][:, TP:NT], ones[0:TS, :], ow[0:TS, 384:384 + TS], start=True, stop=False)
                for dc in range(2):
                    pe.matmul(bank[4][:, TP:NT], ones[:, :], onq[:, dc, :], start=False, stop=dc == 1)
                for dc in range(2):
                    pe.matmul(bank[4][:, 320 + SB * dc:320 + SB * (dc + 1)], otks[:, dc * P:(dc + 1) * P], wm[:, :], start=True, stop=True)
                for dc in range(2):
                    for sc in range(2):
                        last = pe.matmul(bank[4][:, 336 + dc:337 + dc], otk[:, sc, dc * P:(dc + 1) * P], wcol[:, sc:sc + 1], start=sc == 0, stop=sc == 1)
                last.then_inc(S["den_ready"], 1)
                pe.wait_ge(S["bc2_r"], h + 1)
                pe.wait_ge(S["km_ready"], h + 1)

                def turn_state(b):
                    pe.wait_ge(c_loaded[b], h * 16 + 16)
                    for dc in range(2):
                        for vc in range(2):
                            last = turn(bank[5 + b % 2][:, dc * DC + vc * P:dc * DC + (vc + 1) * P],
                                        cring[:, b, vc * DC + dc * P:vc * DC + (dc + 1) * P], P, P)
                    last.then_inc(S["ct_t"], 1)

                turn_state(0)
                for b in range(SB):
                    if b + 1 < SB:
                        turn_state(b + 1)
                    if b:
                        pe.wait_ge(S["c_new"], h * SB + b)
                    for vc in range(2):
                        last = pe.matmul(bank[7][:, vc * DC:(vc + 1) * DC], otvs[:, vc * P:(vc + 1) * P], okm[:, b, :], start=True, stop=True)
                    last.then_inc(S["outer"], 1)
                    pe.wait_ge(S["ct_r"], h * SB + (b + 1))
                    for dc in range(2):
                        last = pe.matmul(bank[2][0:TS, DC:2 * DC], oqm[:, dc, b * TS:(b + 1) * TS], oct_[b % 2][:, dc, :],
                                         start=False, stop=b == SB - 1 and dc == 1)
                last.then_inc(S["ns_ready"], 1)
                pe.wait_ge(S["c_new"], h * SB + SB)
                pe.wait_ge(S["kw_ready"], h + 1)
                for vc in range(2):
                    for sc in range(2):
                        last = pe.matmul(bank[7][:, vc * DC:(vc + 1) * DC], otv[:, sc, vc * P:(vc + 1) * P], okw[:, sc, :], start=sc == 0, stop=sc == 1)
                last.then_inc(S["cp_ready"], 1)
                apart(pe)
                pe.wait_ge(S["ns_read"], h + 1)
                for vc in range(2):
                    last = turn(bank[3][:, DC + vc * TS:DC + (vc + 1) * TS], ons[:, vc * P:(vc + 1) * P], TS, P)
                last.then_inc(S["num_ready"], 1)

            with pe.Fori(0, H // 2) as i:
                for k in range(2):
                    pe.wait_ge(S["hs_squared"], i * 2 + (k + 1))
                    pe.wait_ge(S["hs_read"], i * 2 + (k + 1))
                    for vc in range(2):
                        last = pe.matmul(bank[5 + k][:, 0:NT], ones[:, :], hT[:, bass.ds(i * 4 + (2 * k + vc), 1), :].rearrange("p a t -> p (a t)"), start=vc == 0, stop=vc == 1)
                    last.then_inc(S["hs_summed"], 1)
            pe.wait_ge(S["den_read"], H + 1)
            for dc in range(2):
                turn(bank[4][0:64, dc * P:(dc + 1) * P], nnew[:, dc, :], P, 64)
                last = turn(bank[2][0:H, dc * P:(dc + 1) * P], nprm[:, dc, :], P, H)
            last.then_inc(S["n_turned"], 1)

            pe.wait_ge(S["hs_done"], H)
            pe.wait_ge(S["hs_rstd"], 2)
            with pe.Fori(0, TRIPS["out"]) as i:
                for j in range(2):
                    product("out1", "out", i, j, yT, NT)
            sum_squares("post1")

            pe.wait_ge(S["post1_done"], 1)
            for k in range(12):
                tc, f = k // 4, k % 4
                rows_ = P if tc < 2 else TS
                if k >= 2:
                    pe.wait_ge(S["y_read"], k - 1)
                for c in range(4):
                    last = turn(bank[5 + k % 2][0:rows_, c * P:(c + 1) * P], xT[:, 4 * f + c, tc * P:tc * P + rows_], P, rows_)
                last.then_inc(S["y_turned"], 1)

        @block.scalar
        def _(eng):
            A1 = AO.link

            def evacuate(phase, kind, i, j, outs):
                per, n = len(SLOTS_FOR[kind]), first[phase] + j
                for mt in range(2):
                    act.wait_ge(proj_ready, i * (2 * per) + (2 * n + mt + 1))
                    outs(mt, proj[mt])

            def squares(key, src, dst):
                for q in range(4):
                    A1(act.activation(dst[:, 4 * q:4 * q + 4, :], src[:, 4 * q:4 * q + 4, :], ACT.Square), S[f"{key}_squared"])

            def root(key, summed, n):
                act.wait_ge(S[f"{key}_summed"], 1)
                A1(act.activation(rstd[:, :], summed, ACT.Ln, bias=eps, scale=1.0 / n))
                A1(act.activation(rstd[:, :], rstd[:, :], ACT.Exp, scale=-0.5), S[f"{key}_rstd"])

            act.dma_start(cin[0:1, :], A["c_prompt"]).then_inc(small_loaded, 16)
            act.dma_start(cin[1:NC, :], A["c_sample"]).then_inc(small_loaded, 16)
            act.dma_start(cst[:, :], A["constants"]).then_inc(small_loaded, 16)
            act.dma_start(xin[:, :, :], A["x_prompt"][0].rearrange("(c p) d -> p c d", p=P)).then_inc(small_loaded, 16)
            act.dma_start(xsin[:, :], A["x_sample"].rearrange("b t d -> (b t) d")).then_inc(small_loaded, 16)
            act.dma_start(prow[0:96, 0, :], A["ada_b"].rearrange("l (c p) -> (l c) p", p=P)).then_inc(small_loaded, 16)
            act.dma_start(prow[0:32, 1, :], A["norm_pre"].rearrange("l (c p) -> (l c) p", p=P)).then_inc(small_loaded, 16)
            act.dma_start(prow[32:64, 1, :], A["norm_post"].rearrange("l (c p) -> (l c) p", p=P)).then_inc(small_loaded, 16)
            act.dma_start(prow[64:72, 1, :], A["pool_scale"].rearrange("l (c p) -> (l c) p", p=P)).then_inc(small_loaded, 16)
            act.dma_start(prow[72:88, 1, :], A["head_norm"].rearrange("l (c p) -> (l c) p", p=P)).then_inc(small_loaded, 16)
            act.dma_start(bif[:, 0:1], A["b_igate"].rearrange("a h -> h a")).then_inc(small_loaded, 16)
            act.dma_start(bif[:, 1:2], A["b_fgate"].rearrange("a h -> h a")).then_inc(small_loaded, 16)
            act.dma_start(ptab[:, :], A["page_table"].rearrange("b (g a) -> a (b g)", a=1)).then_inc(ptab_loaded, 16)
            for s, n in ((proj_free, 2), (S["kt_read_act"], 1), (S["cp_read"], 1), (S["hs_read"], 2)):
                AO.credit(s, n)
            act.wait_ge(small_loaded, 16 * N_SMALL)
            A1(act.activation(cexp[:, :], cin[:, :], ACT.Exp, scale=-1.0), S["c_exp"])
            act.wait_ge(S["x_read"], KC)
            squares("pre0", xT, yT)
            root("pre0", bank[4][:, 0:NT], D)

            def read_mod(phase, layer, i, j):
                def outs(mt, b):
                    A1(act.activation(mod_rows[layer][:, bass.ds(i * (6 * P) + (2 * j + mt) * P, P)], b[0:NC, 0:P], ACT.Copy), proj_free)
                evacuate(phase, "ada", i, j, outs)

            with AO.turns(0, TRIPS["ada"], proj_free=6) as i:
                for j in range(3):
                    read_mod("ada0", 0, i, j)
            act.sem_inc(phase_met, 1)

            act.wait_ge(phase_met, 3)

            def into(z):
                return lambda mt, b: A1(act.activation(z[:, mt, :], b[:, 0:NT], ACT.Copy), proj_free)

            kout = OUT["k_prompt"][0, 0].rearrange("(c p) h d -> p c (h d)", p=P)
            vout = OUT["v_prompt"][0, 0].rearrange("(c p) h d -> p c (h d)", p=P)
            with AO.turns(0, TRIPS["even"], proj_free=12, ktok_read=1, vtok_read=1, ga_exp=1, gb_exp=1, p_exp=2, pt_read=2, act_order=8) as g:
                act.wait_ge(S["qk_kept"], g + 1)
                evacuate("even", "even", g, 0, into(zq))
                evacuate("even", "even", g, 1, into(zk))
                evacuate("even", "even", g, 2, into(zv))

                def tokens(tok, tok_s, turned, read, out):
                    act.wait_ge(S[turned], g + 1)
                    act.wait_ge(stored, g * 32 + (16 if tok is ktok else 32))
                    A1(act.activation(tok[:, :, :].rearrange("p a n -> p (a n)"), bank[4][:, :], ACT.Copy))
                    A1(act.activation(tok_s[:, bass.ds(g * GW, GW)], bank[5][0:TS, 0:GW], ACT.Copy), S[read])
                    act.dma_start(out[:, :, bass.ds(g * GW, GW)], tok[:, :, :]).then_inc(stored, 16)

                tokens(ktok, ktok_s, "ktok_turned", "ktok_read", kout)
                act.wait_ge(S["att_read"], g + 1)

                def gate_a(mt, b):
                    A1(act.activation(zga[:, mt, :], b[:, 0:NT], ACT.Copy))
                    A1(act.activation(ega[:, mt, :], b[:, 0:NT], ACT.Exp, scale=-1.0), proj_free)

                evacuate("even", "even", g, 3, gate_a)
                act.sem_inc(S["ga_exp"], 1)
                AO.count(S["ga_exp"]).k += 1
                for hh in range(2):
                    act.wait_ge(S["x_max"], g * 2 + (hh + 1))
                    for c, (a, b) in enumerate(((0, P), (P, 384))):
                        A1(act.activation(xs[hh][:, a:b], xs[hh][:, a:b], ACT.Exp, bias=stat[:, 2 * hh + c, 1:2], scale=SCALE,
                                          accum_out=stat[:, 2 * hh + c, 2:3]), S["p_exp"] if c else None)
                tokens(vtok, vtok_s, "vtok_turned", "vtok_read", vout)
                evacuate("even", "even", g, 4, lambda mt, b: A1(act.activation(
                    yT[:, bass.ds(g * 2 + (8 + mt), 1), :].rearrange("p a t -> p (a t)"), b[:, 0:NT], ACT.Copy), proj_free))
                for hh in range(2):
                    act.wait_ge(S["pt_turned"], g * 2 + (hh + 1))
                    A1(act.activation(pts[hh][:, :], bank[6 + hh][:, 0:384], ACT.Copy), S["pt_read"])
                act.wait_ge(S["silu_gb"], g + 1)

                def gate_b(mt, b):
                    A1(act.activation(gbs[:, bass.ds(g * 2 + mt, 1), :].rearrange("p a t -> p (a t)"), b[:, 0:NT], ACT.Copy))
                    A1(act.activation(egb[:, mt, :], b[:, 0:NT], ACT.Exp, scale=-1.0), proj_free)

                evacuate("even", "even", g, 5, gate_b)
                act.sem_inc(S["gb_exp"], 1)
                AO.count(S["gb_exp"]).k += 1
            even_stored = 16 * 2 * TRIPS["even"] + 16
            act.wait_ge(stored, even_stored)
            for name, tok in (("k_sample", ktok_s), ("v_sample", vtok_s)):
                store(OUT[name][0].rearrange("b t h d -> (b t) (h d)"), tok[:, :])
            act.wait_ge(stored, even_stored + 32)
            act.sem_inc(phase_met, 1)

            act.wait_ge(phase_met, 6)
            act.dma_start(hist[:, :], A["state_pool"][0].rearrange("b j c -> (b j) c")).then_inc(S["pool_loaded"], 16)
            act.dma_start(pw[:, :, :], A["pool_w"][0].rearrange("g (c p) d -> p (g c) d", p=P)).then_inc(S["pool_loaded"], 16)
            store(OUT["pool_sample"][0][:, 0:HIST - ST, :], A["state_pool"][0][:, ST:HIST, :])
            act.wait_ge(S["u_turned"], 1)
            A1(act.activation(utok[:, :], pair[0][0:HIST, :], ACT.Copy))
            A1(act.activation(ustok[:, :], pair[1][0:TS, :], ACT.Copy), S["u_read"])
            store(OUT["pool_prompt"][0, 0], utok[:, :])
            for b in range(SB):
                store(OUT["pool_sample"][0][b, HIST - ST:HIST, :], ustok[b * ST:(b + 1) * ST, :])
            act.wait_ge(stored, even_stored + 32 + 16 * (2 + SB))
            act.sem_inc(phase_met, 1)

            act.wait_ge(phase_met, 9)
            def halves(b):
                for j in range(PAGES):
                    act.wait_ge(S["kt_turned"], b * (2 * PAGES) + (2 * j + 1))
                    A1(act.activation(ktp[j % 2][:, 0, :], bank[0][:, :], ACT.Copy), S["kt_read_act"])

            def softmax(b):
                act.wait_ge(S["s_max"], b + 1)
                A1(act.activation(sx[0][:, :], sx[0][:, :], ACT.Exp, bias=sstat[:, 1:2], scale=SCALE, accum_out=sstat[:, 2:3]), S["s_exp"])

            def values_out(b):
                act.wait_ge(S["s_rows"], b + 1)
                A1(act.activation(so[:, :], pair[1][0:TS, :], ACT.Copy), S["s_rows_read"])

            halves(0)
            softmax(0)
            with AO.turns(1, SB, kt_read_act=PAGES, s_exp=1, s_rows_read=1) as b:
                halves(b)
                softmax(b)
                values_out(b - 1)
            values_out(SB - 1)
            act.sem_inc(phase_met, 1)

            act.wait_ge(phase_met, 12)
            act.dma_start(wg[:, :, :], w_odd[:, :, 5 * D:5 * D + 2 * H]).then_inc(S["wg_loaded"], 16)
            act.dma_start(snin[:, :], A["state_n"][0].rearrange("b h d -> (b h) d")).then_inc(S["sn_loaded"], 16)
            act.dma_start(gr["w"][:, 0:SB], A["state_m"][0].rearrange("b h -> h b"), allow_slow_non_contiguous=True).then_inc(S["m0_loaded"], 16)

            def read_mix(phase):
                def outs(mt, b):
                    A1(act.activation(hT[:, bass.ds(i * 4 + (2 * j + mt), 1), :].rearrange("p a t -> p (a t)"), b[:, 0:NT], ACT.Copy), proj_free)
                with AO.turns(0, TRIPS["out"], proj_free=4) as i:
                    for j in range(2):
                        evacuate(phase, "out", i, j, outs)

            read_mix("out0")
            squares("post0", hT, yT)
            root("post0", bank[4][:, 0:NT], D)
            with AO.turns(0, TRIPS["ada"] // 2, proj_free=6) as i:
                for j in range(3):
                    read_mod("ada1", 1, i, j)
            act.wait_ge(S["post0_done"], 1)
            squares("pre1", xT, yT)
            root("pre1", bank[4][:, 0:NT], D)
            with AO.turns(TRIPS["ada"] // 2, TRIPS["ada"], proj_free=6) as i:
                for j in range(3):
                    read_mod("ada1", 1, i, j)

            act.wait_ge(S["gx"], 1)
            A1(act.activation(gr["w"][:, :], gr["M"][:, :], ACT.Exp, scale=-1.0))
            A1(act.activation(gr["w"][:, :], gr["w"][:, :], ACT.Ln, bias=1.0), S["g_ln"])
            act.wait_ge(S["gl_ready"], 1)
            A1(act.activation(rows[:, NT:3 * NT], rows[:, NT:3 * NT], ACT.Exp))
            A1(act.activation(gr["w"][:, :], gr["w"][:, :], ACT.Exp), S["rows_ready"])
            store(OUT["m_prompt"][0].rearrange("a h -> h a"), gr["t1"][:, TP - 1:TP])
            store(OUT["m_sample"][0].rearrange("b h -> h b"), gr["t1"][:, TP:NT].rearrange("h (b t) -> h b t", t=ST)[:, :, ST - 1], slow=True)
            act.wait_ge(stored, even_stored + 16 * n_store[0])

            cp_stored = S["cp_stored"]
            with AO.turns(0, H, proj_free=10, kt_r=1, vt_r=1, e_exp=1, bc2_r=1, smp_r=1, ct_r=SB, ns_read=1, cp_read=1, act_order=4) as h:
                for j, z in enumerate((oz["q"], oz["k"])):
                    evacuate("odd", "odd", h, j, lambda mt, b: A1(act.activation(z[:, mt, :], b[:, 0:NT], ACT.Copy, scale=KSCALE if j else 1.0), proj_free))
                act.wait_ge(S["kt_t"], h + 1)
                A1(act.activation(otk[:, :, :].rearrange("p a n -> p (a n)"), bank[5][:, :], ACT.Copy), S["kt_r"])
                act.wait_ge(S["e_in"], h + 1)
                A1(act.activation(oe[:, 0:384], oe[:, 0:384], ACT.Exp))
                A1(act.activation(oe[0:TS, 384:384 + TS], oe[0:TS, 384:384 + TS], ACT.Exp), S["e_exp"])
                evacuate("odd", "odd", h, 2, into(ozv))
                act.wait_ge(S["vt_t"], h + 1)
                A1(act.activation(otv[:, :, :].rearrange("p a n -> p (a n)"), bank[5][:, :], ACT.Copy), S["vt_r"])
                act.wait_ge(S["bc2"], h + 1)
                act.wait_ge(S["den_read"], h + 1)
                A1(act.activation(obc[:, :], bank[6][:, 0:NT + TS], ACT.Copy), S["bc2_r"])
                act.wait_ge(S["num_read"], h + 1)
                evacuate("odd", "odd", h, 3, lambda mt, b: A1(act.activation(oz["eo"][:, mt, :], b[:, 0:NT], ACT.Exp, scale=-1.0), proj_free))
                act.wait_ge(S["smp_t"], h + 1)
                A1(act.activation(otks[:, :], bank[5][0:TS, 0:DC], ACT.Copy))
                A1(act.activation(otvs[:, :], bank[5][0:TS, DC:2 * DC], ACT.Copy), S["smp_r"])
                act.wait_ge(S["gate_done"], h + 1)

                def gate(mt, b):
                    A1(act.activation(oz["g"][:, mt, :], b[:, 0:NT], ACT.Copy))
                    A1(act.activation(oz["eg"][:, mt, :], b[:, 0:NT], ACT.Exp, scale=-1.0), proj_free)

                evacuate("odd", "odd", h, 4, gate)
                for b in range(SB):
                    act.wait_ge(S["ct_t"], h * SB + (b + 1))
                    A1(act.activation(oct_[b % 2][:, :, :].rearrange("p a n -> p (a n)"), bank[5 + b % 2][:, :], ACT.Copy), S["ct_r"])
                act.wait_ge(S["ns_ready"], h + 1)
                A1(act.activation(ons[:, :], bank[2][0:TS, DC:2 * DC], ACT.Copy), S["ns_read"])
                act.wait_ge(S["cp_ready"], h + 1)
                act.wait_ge(cp_stored, h * 16 + 16)
                A1(act.activation(ocp[:, :], bank[7][:, :], ACT.Copy), S["cp_read"])
                act.dma_start(OUT["C_prompt"][0, 0, bass.ds(h, 1), :, :].rearrange("h (v p) d -> p (h v) d", p=P),
                              ocp[:, :].rearrange("p (v d) -> p v d", v=2)).then_inc(cp_stored, 16)

            act.wait_ge(S["num_read"], H + 1)
            for q in range(H):
                A1(act.activation(hT[:, 2 * q:2 * q + 2, :], yT[:, 2 * q:2 * q + 2, :], ACT.Square), S["hs_squared"])
            for half in range(2):
                for k in range(4 * half, 4 * half + 4):
                    act.wait_ge(S["hs_summed"], k + 1)
                    A1(act.activation(hT[:, 2 * k, :], bank[5 + k % 2][:, 0:NT], ACT.Ln, bias=eps, scale=1.0 / DC), S["hs_read"])
                r = hT[:, 8 * half:8 * half + 8, :].rearrange("p (k a) t -> p k a t", a=2)[:, :, 0, :]
                A1(act.activation(r, r, ACT.Exp, scale=-0.5), S["hs_rstd"])
            act.wait_ge(S["n_turned"], 1)
            A1(act.activation(nout[:, :, :].rearrange("p a n -> p (a n)"), bank[4][0:64, 0:DC], ACT.Copy))
            A1(act.activation(npout[:, :, :].rearrange("p a n -> p (a n)"), bank[2][0:H, 0:DC], ACT.Copy), S["n_read"])
            store(OUT["n_sample"][0].rearrange("b h d -> (b h) d"), nout[:, :, :].rearrange("p a n -> p (a n)"))
            store(OUT["n_prompt"][0, 0], npout[:, :, :].rearrange("p a n -> p (a n)"))

            act.wait_ge(S["hs_done"], H)
            read_mix("out1")
            squares("post1", hT, yT)
            root("post1", bank[4][:, 0:NT], D)
            act.wait_ge(S["post1_done"], 1)
            yout = [OUT["y_prompt"][0, 0:P, :], OUT["y_prompt"][0, P:TP, :], OUT["y_sample"].rearrange("b t d -> (b t) d")]
            flat = [t[:, :, :].rearrange("p a t -> p (a t)") for t in (hT, yT)]
            for k in range(12):
                tc, f = k // 4, k % 4
                n = P if tc < 2 else TS
                stage = flat[k // 8][0:n, (k % 8) * 512:(k % 8 + 1) * 512]
                act.wait_ge(S["y_turned"], k + 1)
                A1(act.activation(stage, bank[5 + k % 2][0:n, :], ACT.Copy), S["y_read"])
                store(yout[tc][:, f * 512:(f + 1) * 512], stage)
            act.wait_ge(stored, even_stored + 16 * n_store[0])
            act.wait_ge(cp_stored, 16 * H + 16)

        @block.vector
        def _(eng):
            V1 = VO.link

            def wide(ap, n):
                return ap.unsqueeze(2).broadcast_to([ap.shape[0], ap.shape[1], n])

            def over(ap, n):
                return ap.unsqueeze(1).broadcast_to([ap.shape[0], n, ap.shape[1]])

            def batches(t):
                return t[:, :, TP:NT].rearrange("p c (b t) -> p c b t", t=ST)

            def by_batch(m):
                return m[:, :, 1:NC].unsqueeze(3).broadcast_to([P, KC, SB, ST])

            def prepare(l):
                dve.wait_ge(S[f"mod_turned{l}"], 1)
                m = modT[:, 48 * l:48 * (l + 1), :]
                V1(dve.tensor_tensor(m, bank[2][:, 0:48 * NC].rearrange("p (c n) -> p c n", n=NC), wide(adab[:, 48 * l:48 * (l + 1)], NC), ALU.add),
                   S["mod_read"])
                V1(dve.scalar_tensor_tensor(out=m[:, 16:32, :], in0=m[:, 16:32, :], scalar=1.0, in1=wide(npre[:, 16 * l:16 * l + 16], NC),
                                            op0=ALU.add, op1=ALU.mult))
                V1(dve.tensor_tensor(m[:, 32:48, :], m[:, 32:48, :], wide(npost[:, 16 * l:16 * l + 16], NC), ALU.mult))

            def pre_norm(l):
                m = modT[:, 48 * l:48 * (l + 1), :]
                dve.wait_ge(S[f"pre{l}_rstd"], 1)
                V1(dve.tensor_tensor(hT[:, :, :], xT[:, :, :], over(rstd[:, :], KC), ALU.mult))
                prepare(l)
                for c in range(KC):
                    V1(dve.tensor_scalar(hT[:, c, 0:TP], hT[:, c, 0:TP], m[:, 16 + c, 0:1], m[:, c, 0:1], ALU.mult, ALU.add))
                V1(dve.tensor_tensor(batches(hT), batches(hT), by_batch(m[:, 16:32, :]), ALU.mult))
                V1(dve.tensor_tensor(batches(hT), batches(hT), by_batch(m[:, 0:16, :]), ALU.add), S[f"pre{l}_done"])

            def post_norm(l):
                m = modT[:, 48 * l:48 * (l + 1), :]
                dve.wait_ge(S[f"post{l}_rstd"], 1)
                V1(dve.tensor_tensor(hT[:, :, :], hT[:, :, :], over(rstd[:, :], KC), ALU.mult))
                for c in range(KC):
                    V1(dve.scalar_tensor_tensor(out=xT[:, c, 0:TP], in0=hT[:, c, 0:TP], scalar=m[:, 32 + c, 0:1], in1=xT[:, c, 0:TP],
                                                op0=ALU.mult, op1=ALU.add))
                V1(dve.tensor_tensor(batches(hT), batches(hT), by_batch(m[:, 32:48, :]), ALU.mult))
                V1(dve.tensor_tensor(batches(xT), batches(xT), batches(hT), ALU.add), S[f"post{l}_done"])

            for s, n in ((S["att_read"], 1), (S["qk_kept"], 1), (S["silu_gb"], 1), (S["kt_read_dve"], 1), (S["s_read"], 1), (S["s_out_read"], 1),
                         (S["num_read"], 1), (S["den_read"], 1), (S["gate_done"], 1), (stored, 16), (S["cp_stored"], 16)):
                VO.credit(s, n)
            V1(dve.memset(ones[:, :], 1.0), S["ones_set"])
            dve.wait_ge(S["prm_turned"], 1)
            V1(dve.tensor_copy(prm[:, :], bank[5][:, 0:184]))
            dve.wait_ge(S["c_exp"], 1)
            V1(dve.tensor_scalar(cexp[:, :], cexp[:, :], 1.0, None, ALU.add))
            V1(dve.reciprocal(cexp[:, :], cexp[:, :]))
            V1(dve.tensor_tensor(cin[:, :], cin[:, :], cexp[:, :], ALU.mult), S["c_silu"])
            for c in range(KC):
                dve.wait_ge(S["x_turned"], c + 1)
                V1(dve.tensor_copy(xT[:, c, :], bank[6 + c % 2][:, 0:NT]), S["x_read"])
            dve.wait_ge(S["c_turned"], 1)
            V1(dve.tensor_copy(scT[:, :, :].rearrange("p a n -> p (a n)"), bank[2][:, 0:KC * NC]), S["c_read"])
            dve.sem_inc(phase_met, 1)
            pre_norm(0)

            dve.wait_ge(phase_met, 3)
            with VO.turns(0, TRIPS["even"], qk_kept=1, scores_read=2, x_max=2, p_ready=2, silu_gb=1, att_read=1, dve_order=15) as g:
                dve.wait_ge(proj_free, g * 12 + (2 * first["even"] + 6))
                V1(dve.tensor_copy(qTs[:, bass.ds(g * 2, 2), :], zq[:, :, TP:NT]))
                V1(dve.tensor_copy(kTs[:, bass.ds(g * 2, 2), :], zk[:, :, TP:NT]), S["qk_kept"])
                for hh in range(2):
                    dve.wait_ge(S["scores"], g * 2 + (hh + 1))
                    V1(dve.scalar_tensor_tensor(out=xs[hh][:, :], in0=const("dist"), scalar=const("slope")[:, bass.ds(g * 2 + hh, 1)],
                                                in1=bank[2 + hh][:, 0:384], op0=ALU.mult, op1=ALU.add), S["scores_read"])
                    V1(dve.reduce_max(stat[:, 2 * hh, 0:1], xs[hh][:, 0:P], AX.X))
                    V1(dve.reduce_max(stat[:, 2 * hh + 1, 0:1], xs[hh][:, P:384], AX.X))
                    V1(dve.tensor_scalar(stat[:, 2 * hh:2 * hh + 2, 1], stat[:, 2 * hh:2 * hh + 2, 0], -SCALE, None, ALU.mult), S["x_max"])
                dve.wait_ge(S["ga_exp"], g + 1)
                V1(dve.tensor_scalar(ega[:, :, :], ega[:, :, :], 1.0, None, ALU.add))
                V1(dve.reciprocal(ega[:, :, :], ega[:, :, :]))
                V1(dve.tensor_tensor(ega[:, :, :], ega[:, :, :], zga[:, :, :], ALU.mult))
                V1(dve.tensor_copy(gas[:, bass.ds(g * 2, 2), :], ega[:, :, TP:NT]))
                for hh in range(2):
                    dve.wait_ge(S["p_exp"], g * 2 + (hh + 1))
                    V1(dve.reciprocal(stat[:, 2 * hh:2 * hh + 2, 3], stat[:, 2 * hh:2 * hh + 2, 2]))
                    V1(dve.tensor_scalar(xs[hh][:, 0:P], xs[hh][:, 0:P], stat[:, 2 * hh, 3:4], None, ALU.mult))
                    V1(dve.tensor_scalar(xs[hh][:, P:384], xs[hh][:, P:384], stat[:, 2 * hh + 1, 3:4], None, ALU.mult), S["p_ready"])
                dve.wait_ge(S["gb_exp"], g + 1)
                V1(dve.tensor_scalar(egb[:, :, :], egb[:, :, :], 1.0, None, ALU.add))
                V1(dve.reciprocal(egb[:, :, :], egb[:, :, :]))
                gb = gbs[:, bass.ds(g * 2, 2), :]
                V1(dve.tensor_tensor(gb, gb, egb[:, :, :], ALU.mult), S["silu_gb"])
                dve.wait_ge(S["att_out"], g + 1)
                V1(dve.tensor_tensor(yT[:, bass.ds(g * 2, 2), 0:TP], bank[2][:, :].rearrange("p (a t) -> p a t", a=2), ega[:, :, 0:TP], ALU.mult), S["att_read"])
            dve.sem_inc(phase_met, 1)

            dve.wait_ge(phase_met, 6)
            for t in uext:
                V1(dve.memset(t[:, :, 0:16], 0.0))
            sv = sext.rearrange("p c (b t) -> p c b t", t=19)
            dve.wait_ge(S["hist_turned"], 1)
            for k in range(2):
                V1(dve.tensor_copy(sv[:, 4 * k:4 * k + 4, :, 0:HIST], bank[2 + k][:, 0:480].rearrange("p (c b j) -> p c b j", c=4, b=SB)), S["hist_read"])
            V1(dve.tensor_copy(sv[:, :, :, HIST:19], yT[:, 8:16, TP:NT].rearrange("p c (b t) -> p c b t", t=ST)))

            def pool_read(g):
                dve.wait_ge(S["pool_out"], g + 1)
                for mt in range(2):
                    V1(dve.scalar_tensor_tensor(out=yT[:, 8 + 2 * g + mt, :], in0=bank[2 + 2 * (g % 2) + mt][:, 0:NT], scalar=pscale[:, 2 * g + mt:2 * g + mt + 1],
                                                in1=gbs[:, 2 * g + mt, :], op0=ALU.mult, op1=ALU.mult), S["pool_read"])

            for g, w in enumerate(WINDOWS):
                u = yT[:, 8 + 2 * g:10 + 2 * g, :]
                V1(dve.tensor_copy(uext[0][:, :, 16:], u[:, :, 0:TP]))
                se = sext[:, 2 * g:2 * g + 2, :].rearrange("p c (b t) -> p (c b) t", t=19)
                ssrc = se
                for k in range(g + 1):
                    d = 1 << k
                    a, b = uext[k % 2], uext[(k + 1) % 2]
                    V1(dve.tensor_tensor(b[:, :, 16:], a[:, :, 16:], a[:, :, 16 - d:16 + TP - d], ALU.add))
                    lo = 2 * d - 1
                    V1(dve.tensor_tensor(swin[k % 2][:, :, lo:19], ssrc[:, :, lo:19], ssrc[:, :, lo - d:19 - d], ALU.add))
                    ssrc = swin[k % 2]
                win = uext[(g + 1) % 2]
                if g:
                    dve.wait_ge(S["pool_out"], g)
                V1(dve.scalar_tensor_tensor(out=dT[:, :, 0:TP], in0=win[:, :, 16:], scalar=1.0 / w, in1=u[:, :, 0:TP], op0=ALU.mult, op1=ALU.subtract))
                V1(dve.tensor_tensor(dT[:, :, 0:16], win[:, :, 16:32], over(const("invcnt")[:, 16 * g:16 * g + 16], 2), ALU.mult))
                V1(dve.tensor_tensor(dT[:, :, 0:16], dT[:, :, 0:16], u[:, :, 0:16], ALU.subtract))
                for cc in range(2):
                    V1(dve.scalar_tensor_tensor(out=dT[:, cc, TP:NT].rearrange("p (b t) -> p b t", t=ST), in0=ssrc[:, SB * cc:SB * (cc + 1), HIST:19],
                                                scalar=1.0 / w, in1=se[:, SB * cc:SB * (cc + 1), HIST:19], op0=ALU.mult, op1=ALU.subtract),
                       S["d_ready"] if cc else None)
                if g == 0:
                    dve.wait_ge(S["u_turned"], 1)
                else:
                    pool_read(g - 1)
            pool_read(3)
            dve.sem_inc(phase_met, 1)

            dve.wait_ge(phase_met, 9)
            V1(dve.memset(qm[0][:, 0:288], 0.0))
            heads_q = qm[0][:, 0:288].rearrange("p (h x) -> p h x", x=TS + ST)[:, :, 0:ST]
            x = sx[0]
            x4 = x[:, 0:PAST].rearrange("p (n k) -> p n k", n=NB)
            gates, least, rank, drop = sstat[:, 4:8], sstat[:, 8:9], sstat[:, 9:13], sstat[:, 13:14]

            def scores_of(b, first_turn):
                if not first_turn:
                    dve.wait_ge(S["s_scores"], b)
                V1(dve.tensor_copy(heads_q, qTs[:, :, bass.ds(b * ST, ST)]), S["qm_ready"])
                for j in range(PAGES):
                    dve.wait_ge(S["kt_turned"], b * (2 * PAGES) + (2 * j + 2))
                    V1(dve.tensor_copy(ktp[j % 2][:, 1, :], bank[1][:, :]), S["kt_read_dve"])

            def weights_of(b):
                dve.wait_ge(S["s_scores"], b + 1)
                V1(dve.tensor_tensor(x[:, 0:PAST], pair[0][0:TS, :], const("sbias", TS), ALU.add))
                V1(dve.tensor_tensor(x[:, PAST:XW], bank[2][0:TS, 0:TS], const("own", TS)[:, bass.ds(b * TS, TS)], ALU.add))
                V1(dve.tensor_reduce(gates, pair[0][0:TS, :].rearrange("p (n k) -> p n k", n=NB), AX.X, ALU.add), S["s_read"])
                V1(dve.tensor_reduce(least, gates, AX.X, ALU.min))
                V1(dve.scalar_tensor_tensor(out=rank, in0=gates, scalar=least, in1=const("rank", TS), op0=ALU.is_equal, op1=ALU.mult))
                V1(dve.reduce_max(drop, rank, AX.X))
                V1(dve.tensor_scalar(rank, const("rank", TS), drop, -BIG, ALU.is_equal, ALU.mult))
                V1(dve.tensor_tensor(x4, x4, wide(rank, BLOCK), ALU.add))
                V1(dve.reduce_max(sstat[:, 0:1], x, AX.X))
                V1(dve.tensor_scalar(sstat[:, 1:2], sstat[:, 0:1], -SCALE, None, ALU.mult), S["s_max"])
                dve.wait_ge(S["s_exp"], b + 1)
                V1(dve.reciprocal(sstat[:, 3:4], sstat[:, 2:3]))
                V1(dve.tensor_scalar(x, x, sstat[:, 3:4], None, ALU.mult), S["s_ready"])

            def turned_weights(b):
                dve.wait_ge(S["s_turned"], b + 1)
                V1(dve.tensor_copy(pT[:, 0:PAGES * TS], bank[3][:, 0:PAGES * TS]))
                V1(dve.tensor_copy(pT[0:TS, PAGES * TS:(PAGES + 1) * TS], bank[3][0:TS, PAGES * TS:(PAGES + 1) * TS]), S["s_pt"])

            def output_of(b):
                dve.wait_ge(S["s_out"], b + 1)
                V1(dve.tensor_tensor(yT[:, 0:H, bass.ds(b * ST + TP, ST)], bank[3][:, 0:H * (TS + ST)].rearrange("p (h x) -> p h x", x=TS + ST)[:, :, 0:ST],
                                     gas[:, :, bass.ds(b * ST, ST)], ALU.mult), S["s_out_read"])

            scores_of(0, True)
            weights_of(0)
            with VO.turns(1, SB, qm_ready=1, kt_read_dve=PAGES, s_read=1, s_max=1, s_ready=1, s_pt=1, s_out_read=1, dve_order=10) as b:
                scores_of(b, False)
                turned_weights(b - 1)
                weights_of(b)
                output_of(b - 1)
            turned_weights(SB - 1)
            output_of(SB - 1)
            dve.sem_inc(phase_met, 1)

            dve.wait_ge(phase_met, 12)
            dve.wait_ge(S["m0_loaded"], 16)
            V1(dve.memset(m0[:, 0:TP], 0.0))
            V1(dve.tensor_copy(m0[:, TP:NT].rearrange("h (b t) -> h b t", t=ST), wide(gr["w"][:, 0:SB], ST)))
            post_norm(0)
            pre_norm(1)

            dve.wait_ge(S["gate_sums"], 1)
            V1(dve.tensor_scalar(gr["ig"][:, :], bank[2][0:H, 0:NT], bif[:, 0:1], None, ALU.add))
            V1(dve.tensor_scalar(gr["t1"][:, :], bank[3][0:H, 0:NT], bif[:, 1:2], None, ALU.add))
            V1(dve.scalar_tensor_tensor(out=gr["M"][:, :], in0=gr["t1"][:, :], scalar=-1.0, in1=gr["t1"][:, :], op0=ALU.mult, op1=ALU.max), S["gx"])
            dve.wait_ge(S["g_ln"], 1)
            V1(dve.scalar_tensor_tensor(out=gr["lf"][:, :], in0=gr["t1"][:, :], scalar=0.0, in1=gr["w"][:, :], op0=ALU.min, op1=ALU.subtract))
            V1(dve.tensor_tensor_scan(gr["b"][:, :], const("keep", H), gr["lf"][:, :], 0.0, ALU.mult, ALU.add))
            V1(dve.tensor_tensor(gr["c"][:, :], gr["ig"][:, :], gr["b"][:, :], ALU.subtract))
            V1(dve.tensor_tensor_scan(gr["M"][:, :], const("cut", H), gr["c"][:, :], 0.0, ALU.add, ALU.max))
            V1(dve.tensor_tensor(gr["M"][:, :], gr["M"][:, :], m0[:, :], ALU.max))
            V1(dve.tensor_tensor(gr["t1"][:, :], gr["b"][:, :], gr["M"][:, :], ALU.add))
            V1(dve.tensor_scalar(rows[:, 0:NT], gr["M"][:, :], -1.0, None, ALU.mult))
            V1(dve.tensor_scalar(rows[:, NT:2 * NT], gr["t1"][:, :], -1.0, None, ALU.mult))
            V1(dve.tensor_tensor(rows[:, 2 * NT:3 * NT], m0[:, :], gr["M"][:, :], ALU.subtract))
            V1(dve.tensor_scalar(gr["w"][:, 0:TP], gr["c"][:, 0:TP], gr["M"][:, TP - 1:TP], None, ALU.subtract))
            end = gr["M"][:, TP:NT].rearrange("h (b t) -> h b t", t=ST)[:, :, ST - 1]
            V1(dve.tensor_tensor(gr["w"][:, TP:NT].rearrange("h (b t) -> h b t", t=ST), gr["c"][:, TP:NT].rearrange("h (b t) -> h b t", t=ST),
                                 wide(end, ST), ALU.subtract), S["gl_ready"])
            dve.wait_ge(S["cw_turned"], 1)
            for k, t in enumerate((cT, wT)):
                V1(dve.tensor_copy(t[:, 0:2, :], bank[5][:, 24 * k:24 * k + 16].rearrange("p (a h) -> p a h", a=2)))
                V1(dve.tensor_copy(t[0:TS, 2, :], bank[5][0:TS, 24 * k + 16:24 * k + 24]))
            V1(dve.tensor_copy(nT[:, :, :].rearrange("p a n -> p (a n)"), bank[4][:, 0:128]), S["cw_read"])

            V1(dve.memset(oqm[:, :, :], 0.0))
            diag = oqm.rearrange("p d (b x) -> p d b x", x=TS + ST)[:, :, :, 0:ST]
            n_bh = nT.rearrange("p d (b h) -> p d b h", h=H)
            nn_bh = nnew.rearrange("p d (b h) -> p d b h", h=H)
            with VO.turns(0, H, rm=1, wc_ready=1, e_in=1, kw_ready=1, w_ready=1, qi_ready=1, km_ready=1, ws_ready=1, c_new=SB,
                          den_read=1, num_read=1, gate_done=1, dve_order=17) as h:
                def head(ap):
                    return ap[:, :, bass.ds(h, 1)]

                V1(dve.tensor_scalar(rsel[:, :], ones[0:H, :], ident[0:H, bass.ds(h, 1)], None, ALU.mult), S["rm"])
                V1(dve.tensor_copy(wcol[:, :].unsqueeze(2), head(wT[:, 0:2, :])))
                V1(dve.tensor_scalar(wm[:, :], const("bsel", TS), wT[0:TS, 2, bass.ds(h, 1)], None, ALU.mult), S["wc_ready"])
                dve.wait_ge(S["nm_bc"], h + 1)
                V1(dve.scalar_tensor_tensor(out=oe[:, 0:TP], in0=bank[6][:, 0:TP], scalar=cT[:, 0, bass.ds(h, 1)], in1=const("cneg")[:, 0:TP],
                                            op0=ALU.add, op1=ALU.add))
                V1(dve.scalar_tensor_tensor(out=oe[:, TP:384], in0=bank[6][:, P:TP], scalar=cT[:, 1, bass.ds(h, 1)], in1=const("cneg")[:, TP:384],
                                            op0=ALU.add, op1=ALU.add))
                V1(dve.scalar_tensor_tensor(out=oe[0:TS, 384:384 + TS], in0=bank[6][0:TS, TP:NT], scalar=cT[0:TS, 2, bass.ds(h, 1)], in1=const("sneg", TS),
                                            op0=ALU.add, op1=ALU.add), S["e_in"])
                dve.wait_ge(S["kt_r"], h + 1)
                for sc in range(2):
                    V1(dve.tensor_scalar(okw[:, sc, :], otk[:, sc, :], wcol[:, sc:sc + 1], None, ALU.mult), S["kw_ready"] if sc else None)
                dve.wait_ge(S["st"], h + 1)
                dve.wait_ge(S["e_exp"], h + 1)
                V1(dve.tensor_tensor(ow[:, 0:384], bank[7][:, 0:384], oe[:, 0:384], ALU.mult), S["w_ready"])
                dve.wait_ge(S["bc2_r"], h + 1)
                V1(dve.tensor_tensor(oqi[:, :, :], oz["q"][:, :, TP:NT], over(obc[:, NT:NT + TS], 2), ALU.mult))
                V1(dve.tensor_copy(diag, oqi.rearrange("p d (b t) -> p d b t", t=ST)))
                V1(dve.tensor_tensor(onq.rearrange("p d (b t) -> p d b t", t=ST), oqi.rearrange("p d (b t) -> p d b t", t=ST),
                                     n_bh[:, :, :, bass.ds(h, 1)].broadcast_to([P, 2, SB, ST]), ALU.mult), S["qi_ready"])
                dve.wait_ge(S["sst"], h + 1)
                V1(dve.tensor_tensor(ow[0:TS, 384:384 + TS], bank[7][0:TS, 0:TS], oe[0:TS, 384:384 + TS], ALU.mult), S["ws_ready"])
                dve.wait_ge(S["smp_r"], h + 1)
                V1(dve.tensor_tensor(okm[:, :, :], over(otks[:, :], SB), wide(wm[:, :], DC), ALU.mult), S["km_ready"])
                carried = obc[:, NT:NT + TS].rearrange("p (b t) -> p b t", t=ST)[:, :, ST - 1]
                dve.wait_ge(S["den_ready"], h + 1)
                V1(dve.scalar_tensor_tensor(out=odd_[:, :], in0=bank[4][:, 0:NT], scalar=-1.0, in1=obc[:, 0:NT], op0=ALU.mult, op1=ALU.max))
                V1(dve.tensor_tensor(odd_[:, :], odd_[:, :], bank[4][:, 0:NT], ALU.max))
                new = nn_bh[:, :, :, bass.ds(h, 1)].rearrange("p d b h -> p d (b h)")
                V1(dve.tensor_tensor(new, n_bh[:, :, :, bass.ds(h, 1)].rearrange("p d b h -> p d (b h)"), over(carried, 2), ALU.mult))
                V1(dve.tensor_tensor(new, new, bank[4][:, 320:336].rearrange("p (d b) -> p d b", d=2), ALU.add))
                V1(dve.tensor_copy(head(nprm), bank[4][:, 336:338].unsqueeze(2)))
                for b in range(SB):
                    dve.wait_ge(S["outer"], h * SB + (b + 1))
                    V1(dve.scalar_tensor_tensor(out=cring[:, b, :], in0=cring[:, b, :], scalar=obc[:, NT + ST * b + ST - 1:NT + ST * b + ST], in1=bank[7][:, :],
                                                op0=ALU.mult, op1=ALU.add), S["c_new"])
                dve.wait_ge(proj_free, h * 10 + (2 * first["odd"] + 10))
                V1(dve.scalar_tensor_tensor(out=ort[:, :, :], in0=oz["eo"][:, :, :], scalar=1.0, in1=over(odd_[:, :], 2), op0=ALU.add, op1=ALU.mult), S["den_read"])
                V1(dve.reciprocal(ort[:, :, :], ort[:, :, :]))
                dve.wait_ge(S["num_ready"], h + 1)
                for vc in range(2):
                    V1(dve.tensor_tensor(yT[:, bass.ds(h * 2 + vc, 1), 0:TP].rearrange("p a t -> p (a t)"), bank[2 + vc][:, 0:TP], ort[:, vc, 0:TP], ALU.mult))
                V1(dve.tensor_tensor(yT[:, bass.ds(h * 2, 2), TP:NT], bank[3][:, DC:DC + 2 * TS].rearrange("p (a t) -> p a t", a=2), ort[:, :, TP:NT], ALU.mult),
                   S["num_read"])
                dve.wait_ge(proj_free, h * 10 + (2 * first["odd"] + 12))
                V1(dve.tensor_scalar(oz["eg"][:, :, :], oz["eg"][:, :, :], 1.0, None, ALU.add))
                V1(dve.reciprocal(oz["eg"][:, :, :], oz["eg"][:, :, :]))
                for mt in range(2):
                    V1(dve.scalar_tensor_tensor(out=ogain[:, bass.ds(h * 2 + mt, 1), :].rearrange("p a t -> p (a t)"), in0=oz["eg"][:, mt, :],
                                                scalar=hgain[:, bass.ds(h * 2 + mt, 1)], in1=oz["g"][:, mt, :], op0=ALU.mult, op1=ALU.mult),
                       S["gate_done"] if mt else None)

            dve.wait_ge(S["hs_rstd"], 2)
            with VO.turns(0, H // 2, hs_done=2, dve_order=2) as i:
                for k in range(2):
                    y = yT[:, bass.ds(i * 4 + 2 * k, 2), :]
                    V1(dve.tensor_tensor(y, y, ogain[:, bass.ds(i * 4 + 2 * k, 2), :], ALU.mult))
                    V1(dve.tensor_tensor(y, y, hT[:, bass.ds(i * 4 + 2 * k, 1), :].broadcast_to([P, 2, NT]), ALU.mult), S["hs_done"])
            post_norm(1)


def shape_constants():
    import numpy as np
    c = np.zeros((P, CW), np.float32)

    def put(name, a):
        lo, hi = CONST[name]
        c[0:a.shape[0], lo:hi] = a.reshape(a.shape[0], -1)

    p = np.arange(P)[:, None]
    s = np.arange(TP)[None, :]
    slopes = 2.0 ** (-8.0 * np.arange(1, H + 1) / H)
    put("ident", np.eye(P))
    put("dist", np.concatenate([np.where(s[:, :P] <= p, s[:, :P] - p, -BIG), np.where(s <= p + P, s - p - P, -BIG)], 1))
    put("slope", np.broadcast_to(slopes / SCALE, (P, H)))
    put("cneg", np.concatenate([np.where(s >= p, 0, -BIG), np.where(s[:, :P] >= p, 0, -BIG)], 1))
    r = np.arange(TS)
    hr, tr = r // ST, r % ST
    put("sbias", -slopes[hr][:, None] / SCALE * (PAST + tr[:, None] - np.arange(PAST)[None, :]))
    own = np.full((TS, SB, SB, ST), -BIG)
    for b in range(SB):
        for t in range(ST):
            own[tr >= t, b, b, t] = (-slopes[hr] / SCALE * (tr - t))[tr >= t]
    put("own", own.reshape(TS, -1))
    bt = r // ST
    put("sneg", np.where((bt[:, None] == bt[None, :]) & (tr[:, None] <= tr[None, :]), 0, -BIG))
    put("bsel", (bt[:, None] == np.arange(SB)[None, :]).astype(float))
    put("eps", np.full((P, 1), EPS))
    start = np.zeros(NT, bool)
    start[0] = True
    start[TP::ST] = True
    put("keep", np.broadcast_to(np.where(start, 0.0, 1.0), (H, NT)))
    put("cut", np.broadcast_to(np.where(start, -BIG, 0.0), (H, NT)))
    put("invcnt", np.broadcast_to(np.stack([1.0 / np.minimum(w, np.arange(16) + 1) for w in WINDOWS]).reshape(-1), (P, 64)))
    put("rank", np.broadcast_to(np.arange(1, NB + 1), (P, NB)))
    return c


IN_NAMES = ['x_prompt', 'x_sample', 'cache_k', 'cache_v', 'state_pool', 'state_C', 'state_n', 'state_m', 'page_table', 'c_prompt',
            'c_sample', 'ada_w', 'ada_b', 'norm_pre', 'norm_post', 'w_in_even', 'pool_w', 'pool_scale', 'w_out_even', 'w_in_odd',
            'b_igate', 'b_fgate', 'head_norm', 'w_out_odd']
OUT_SHAPES = [("y_prompt", (1, TP, D)), ("y_sample", (SB, ST, D)), ("k_prompt", (1, 1, TP, H, DH)), ("v_prompt", (1, 1, TP, H, DH)),
              ("k_sample", (1, SB, ST, H, DH)), ("v_sample", (1, SB, ST, H, DH)), ("pool_prompt", (1, 1, HIST, WA)),
              ("pool_sample", (1, SB, HIST, WA)), ("C_prompt", (1, 1, H, DC, DC)), ("n_prompt", (1, 1, H, DC)), ("m_prompt", (1, 1, H)),
              ("C_sample", (1, SB, H, DC, DC)), ("n_sample", (1, SB, H, DC)), ("m_sample", (1, SB, H))]


def kernel(**inputs):
    import numpy as np
    import concourse.bacc as bacc
    from concourse.bass_utils import run_bass_kernel_spmd

    nc = bacc.Bacc("TRN2", target_bir_lowering=False, num_devices=1)
    arrays = {name: np.ascontiguousarray(inputs[name]) for name in IN_NAMES}
    arrays["constants"] = shape_constants()
    ins = {name: nc.dram_tensor(name, a.shape, mybir.dt.from_np(a.dtype), kind="ExternalInput").ap() for name, a in arrays.items()}
    outs = {name: nc.dram_tensor("out_" + name, shape, F32, kind="ExternalOutput").ap() for name, shape in OUT_SHAPES}
    trunk_kernel(nc, ins, outs)
    r = run_bass_kernel_spmd(nc, [arrays], core_ids=[0])
    return tuple(r.results[0]["out_" + name] for name, _ in OUT_SHAPES)
```

```python
import math
from contextlib import ExitStack, contextmanager

import concourse.bass as bass
from concourse import mybir

F32 = mybir.dt.float32
F32R = mybir.dt.float32r
I32 = mybir.dt.int32
ALU = mybir.AluOpType
ACT = mybir.ActivationFunctionType
AX = mybir.AxisListType

P = 128
D = 2048
KC = D // P
TP, SB, ST = 256, 8, 4
TS = SB * ST
NT = TP + TS
NC = 1 + SB
H = 8
DH = 128
WA = H * DH
PAGES, PAGE = 8, 128
PAST = PAGES * PAGE
BLOCK = 256
NB = PAST // BLOCK
WINDOWS = (2, 4, 8, 16)
HIST = 15
GW = 256
DC = 256
EPS = 1e-6
BIG = 1e30
SCALE = DH ** -0.5
KSCALE = DC ** -0.5
KD, VD = 4, 4
PF = 4
N_SMALL = 10
SLOTS_FOR = dict(ada=(0, 1), even=(0, 1, 0, 1, 0, 1), out=(0, 1), odd=(0, 1, 0, 1, 0))
TRIPS = dict(ada=12, even=4, out=4, odd=8)
PHASES = (("ada0", "ada"), ("even", "even"), ("out0", "out"), ("ada1", "ada"), ("odd", "odd"), ("out1", "out"))
CONST = {}
_at = 0
for _n, _w in (("ident", P), ("dist", 384), ("slope", H), ("cneg", 384), ("sbias", PAST), ("own", SB * TS), ("sneg", TS),
               ("bsel", SB), ("eps", 1), ("keep", NT), ("cut", NT), ("invcnt", 64), ("rank", NB), ("colsel", 9 * H)):
    CONST[_n] = (_at, _at + _w)
    _at += _w
CW = _at


def slab_plan():
    first, slot, uses, before = {}, [], [], []
    last, count = {}, {}
    for name, kind in PHASES:
        first[name] = len(slot)
        for s in SLOTS_FOR[kind] * TRIPS[kind]:
            count[s] = count.get(s, 0) + 1
            slot.append(s)
            uses.append(count[s])
            before.append(last.get(s))
            last[s] = len(slot) - 1
    return first, slot, uses, before


class Count:

    def __init__(self, sem):
        self.sem, self.base, self.k, self.i, self.per = sem, 0, 0, None, 0

    def inc(self, ins):
        self.k += 1
        return ins.then_inc(self.sem, 1)

    def value(self):
        return self.base + self.k if self.i is None else self.i * self.per + (self.base + self.k)

    def enter(self, i, per):
        self.base, self.k, self.i, self.per = self.base + self.k, 0, i, per

    def leave(self, trips):
        assert self.k == self.per, f"{self.k} increments a turn, {self.per} said"
        self.base, self.k, self.i = self.base + trips * self.per, 0, None


def trunk_kernel(nc, A, OUT):
    first, slot, uses, before = slab_plan()
    ctx = ExitStack()
    with ctx:
        def sb(name, shape, dt=F32):
            return ctx.enter_context(nc.sbuf_tensor(name, shape, dt))

        def sem(name):
            return ctx.enter_context(nc.semaphore(name))

        wbuf = sb("wbuf", [P, 2, KC, GW])
        w_hi = sb("w_hi", [P, 4, 4, GW], F32R)
        w_lo = sb("w_lo", [P, 4, 4, GW], F32R)
        h_hi = sb("h_hi", [P, KC, NT], F32R)
        h_lo = sb("h_lo", [P, KC, NT], F32R)
        xT = sb("xT", [P, KC, NT])
        yT = sb("yT", [P, KC, NT])
        modT = sb("modT", [P, 2 * 48, NC])
        cst = sb("cst", [P, CW])
        ones = sb("ones", [P, P])
        prm = sb("prm", [P, 96 + 88])
        scT = sb("scT", [P, KC, NC])
        rstd = sb("rstd", [P, NT])
        bif = sb("bif", [H, 2])
        m0 = sb("m0", [H, NT])
        ptab = sb("ptab", [1, SB * PAGES], I32)
        arena_words = 13470
        arena = sb("arena", [P, arena_words])

        def const(name, rows=P):
            a, b = CONST[name]
            return cst[0:rows, a:b]

        ident = const("ident")
        eps = const("eps")
        adab = prm[:, 0:96]
        npre, npost = prm[:, 96:128], prm[:, 128:160]
        pscale, hgain = prm[:, 160:168], prm[:, 168:184]

        class Arena:

            def __init__(self):
                self.at = 0

            def take(self, rows, *dims):
                n = math.prod(dims)
                ap = arena[0:rows, self.at:self.at + n]
                self.at += n
                assert self.at <= arena_words, self.at
                if len(dims) == 2:
                    return ap.rearrange("p (a b) -> p a b", b=dims[1])
                if len(dims) == 3:
                    return ap.rearrange("p (a b c) -> p a b c", b=dims[1], c=dims[2])
                return ap

        bank = [ctx.enter_context(nc.psum_tensor(f"bank{i}", [P, 512], F32)) for i in range(4)]
        pair = [ctx.enter_context(nc.psum_tensor(f"pair{i}", [P, 1024], F32)) for i in range(2)]
        bank += [pair[0][:, 0:512], pair[0][:, 512:1024], pair[1][:, 0:512], pair[1][:, 512:1024]]
        proj = bank[0:2]

        w_loaded = [[sem(f"w_loaded{s}{half}") for half in "ab"] for s in range(2)]
        hi_ready = sem("hi_ready")
        lo_ready = sem("lo_ready")
        unit_used = sem("unit_used")
        h_hi_ready, h_lo_ready = sem("h_hi_ready"), sem("h_lo_ready")
        proj_ready = sem("proj_ready")
        proj_free = sem("proj_free")
        act_order, dve_order = sem("act_order"), sem("dve_order")
        phase_met = sem("phase_met")
        small_loaded = sem("small_loaded")
        ptab_loaded = sem("ptab_loaded")
        stored = sem("stored")
        block = ctx.enter_context(nc.Block())

        pe, act, dve, pool, sp = nc.tensor, nc.scalar, nc.vector, nc.gpsimd, nc.sync

        class Own:

            def __init__(self, eng, order):
                self.eng, self.order, self.counts, self.turn = eng, order, {}, None

            def count(self, s):
                if s.name not in self.counts:
                    self.counts[s.name] = Count(s)
                    if self.turn:
                        self.counts[s.name].enter(*self.turn_of(s.name))
                return self.counts[s.name]

            def turn_of(self, name):
                i, per = self.turn
                return i, per.get(name, 0)

            def credit(self, s, n):
                c = self.count(s)
                c.k += n
                self.eng.sem_inc(s, n)

            def link(self, ins, s=None):
                c = self.count(self.order if s is None else s)
                c.inc(ins)
                self.eng.wait_ge(c.sem, c.value())

            @contextmanager
            def turns(self, start, end, **per):
                with self.eng.Fori(start, end) as i:
                    self.turn = ((i - start) if start else i, per)
                    for name, c in self.counts.items():
                        c.enter(*self.turn_of(name))
                    yield i
                    did = {n: c.k for n, c in self.counts.items() if c.k}
                    assert did == per, f"a turn raises {did}"
                    for c in self.counts.values():
                        c.leave(end - start)
                    self.turn = None

        AO, VO = Own(act, act_order), Own(dve, dve_order)
        def apart(eng):
            eng.wait_ge(small_loaded, 16 * N_SMALL)

        n_store = [0]

        def store(out, in_, slow=False):
            n_store[0] += 1
            act.dma_start(out, in_, allow_slow_non_contiguous=slow).then_inc(stored, 16)

        S = {}

        def signals(*names):
            for n in names:
                S[n] = sem(n)

        signals("x_loaded", "c_exp", "c_silu", "c_turned", "c_read", "prm_turned", "x_turned", "x_read", "ones_set")
        signals("x_squared", "x_summed", "x_rstd", "norm_done")
        norm = dict(pre0=0, post0=1, pre1=2, post1=3)
        signals("mod_turned")
        signals("ga_exp", "gb_exp", "scores", "x_max", "p_exp", "p_ready", "pt_turned",
                "pt_read", "ktok_turned", "ktok_read", "vtok_turned", "vtok_read", "att_out", "att_read")
        signals("hist_turned", "hist_read", "u_turned", "u_read", "d_ready", "pool_out", "pool_read", "pool_loaded")
        signals("qk_kept", "silu_gb", "gate_done", "cp_stored", "kt_turned", "kt_read_act", "kt_read_dve", "s_scores", "s_read", "s_max", "s_exp", "s_ready", "s_turned", "s_pt", "s_out", "s_out_read", "qm_ready", "v_used", "s_rows", "s_rows_read")
        k_loaded = [sem(f"k_loaded{s}") for s in range(KD)]
        v_loaded = [sem(f"v_loaded{s}") for s in range(VD)]
        signals("gate_sums", "g_ln", "gl_ready", "rows_ready", "cw_turned", "cw_read", "wg_loaded", "sn_loaded",
                "m0_loaded", "gx")
        signals("rm", "nm_bc", "kt_t", "kt_r", "vt_t", "vt_r", "st", "e_in", "e_exp", "w_ready", "bc2", "bc2_r",
                "smp_t", "smp_r", "sst", "ws_ready", "kw_ready", "qi_ready", "km_ready", "wc_ready", "ct_t", "ct_r", "outer", "c_new", "num_ready", "ns_ready", "ns_read", "num_read", "den_ready", "den_read", "cp_ready", "cp_read",
                "hs_squared", "hs_summed", "hs_read", "hs_rstd", "hs_spread", "hs_done", "sel_ready", "n_turned")
        c_loaded = [sem(f"c_loaded{s}") for s in range(8)]
        c_stored = [sem(f"c_stored{s}") for s in range(8)]
        signals("y_turned", "y_read")

        def wview(w):
            return w.rearrange("(kc p) n -> p kc n", p=P)

        w_ada = [wview(A["ada_w"][l, :, :]) for l in range(2)]
        w_even = wview(A["w_in_even"][0, :, :])
        w_out = [wview(A["w_out_even"][0, :, :]), wview(A["w_out_odd"][0, :, :])]
        w_odd = wview(A["w_in_odd"][0, :, :])
        kpage = A["cache_k"][0].rearrange("g t h d -> t g (h d)")
        vpage = A["cache_v"][0].rearrange("g t h d -> t g (h d)")
        stateC = A["state_C"][0].rearrange("b h (v p) d -> p b h v d", p=P)
        outC = OUT["C_sample"][0].rearrange("b h (v p) d -> p b h v d", p=P)

        EVEN_COL = [j * WA for j in range(6)]
        ODD_COL = [0, D, 2 * D, 3 * D, 4 * D]

        ar = Arena()
        xin = ar.take(P, 2, D)
        xsin = ar.take(TS, D)
        rows_at = ar.at
        mod_rows = [ar.take(NC, 3 * D)]
        prow = ar.take(P, 2, P)
        ar.at = rows_at
        cin = ar.take(NC, D)
        cexp = ar.take(NC, D)
        mod_at = 4096 + 576
        ar.at = mod_at
        mod_rows.append(ar.take(NC, 3 * D))
        early_at = ar.at
        ar.at = mod_at
        sq = ar.take(P, KC, NT)

        ar = Arena()
        qTs = ar.take(P, H, TS)
        kTs = ar.take(P, H, TS)
        gas = ar.take(P, H, TS)
        vtok_s = ar.take(TS, WA)
        sample_at = ar.at
        gbs = ar.take(P, 8, NT)
        even_common = ar.at
        ktok_s = ar.take(TS, WA)
        zq = ar.take(P, 2, NT)
        zk = ar.take(P, 2, NT)
        zv = ar.take(P, 2, NT)
        zga = ar.take(P, 2, NT)
        ega = ar.take(P, 2, NT)
        egb = ar.take(P, 2, NT)
        xs = [ar.take(P, 384) for _ in range(2)]
        pts = [ar.take(P, 384) for _ in range(2)]
        vtok = ar.take(P, 2, GW)
        ktok = ar.take(P, 2, GW)
        stat = ar.take(P, 4, 4)
        ar.at = even_common
        hist = ar.take(120, WA)
        uext = [ar.take(P, 2, 16 + TP) for _ in range(2)]
        sext = ar.take(P, 8, SB * 19)
        swin = [ar.take(P, 2 * SB, 19) for _ in range(2)]
        dT = ar.take(P, 2, NT)
        pw = ar.take(P, 8, GW)
        utok = ar.take(HIST, WA)
        ustok = ar.take(TS, WA)
        ar.at = sample_at
        kring = wbuf[:, 1, :, :].rearrange("p k n -> p (k n)").rearrange("p (a b) -> p a b", a=KD)
        vring = ar.take(P, VD, WA)
        ktp = [ar.take(P, 2, 512) for _ in range(2)]
        qm = [ar.take(P, H * (TS + ST))]
        XW = PAST + TS
        sx = [ar.take(TS, XW)]
        pT = ar.take(P, 9 * TS)
        so = ar.take(TS, WA)
        sstat = ar.take(TS, 16)

        ar = Arena()
        cring = ar.take(P, 8, 2 * DC)
        oz = {n: ar.take(P, 2, NT) for n in ("k", "q", "eo", "g", "eg")}
        ozv = ar.take(P, 2, NT)
        otk = ar.take(P, 2, DC)
        otv = ar.take(P, 2, DC)
        otks = ar.take(TS, DC)
        otvs = ar.take(TS, DC)
        okm = [ar.take(TS, DC) for _ in range(2)]
        oct_ = [ar.take(P, 2, DC) for _ in range(2)]
        e_at = ar.at
        oe = ar.take(P, 384 + TS)
        obc = ar.take(P, NT + TS)
        odd_ = obc[:, 0:NT]
        oqi = ar.take(P, 2, TS)
        oqm = ar.take(P, 2, SB * (TS + ST))
        onq = ar.take(P, 2, TS)
        rows = ar.take(H, 3 * NT)
        rsel = ar.take(H, P)
        csel = ar.take(P, H)
        cT = ar.take(P, 3, H)
        wT = ar.take(P, 3, H)
        wcol = ar.take(P, 2)
        wm = ar.take(TS, SB)
        nT = ar.take(P, 2, SB * H)
        nnew = ar.take(P, 2, SB * H)
        nprm = ar.take(P, 2, H)
        ow = oe
        ort = oz["eo"]
        hsq = oz["eo"]
        ocp = oct_[0].rearrange("p a n -> p (a n)")
        ons = otks
        hsum = m0
        ar.at = early_at
        wg = ar.take(P, KC, 2 * H)
        snin = ar.take(SB * H, DC)
        gr = {"w": ar.take(H, NT)}
        ar.at = mod_at
        gr.update({n: ar.take(H, NT) for n in ("ig", "lf", "t1", "b", "c", "M")})
        ar.at = e_at
        rsel8 = ar.take(H, H, P)
        nout = ar.take(SB * H, 2, P)
        npout = ar.take(H, 2, P)

        KINDS = dict(PHASES)
        split_before, split_first, n_split = [], {}, 0
        for name, kind in PHASES:
            split_first[name] = n_split
            for _ in range(len(SLOTS_FOR[kind]) * TRIPS[kind]):
                split_before.append(n_split)
                n_split += kind != "ada"
        kind_of = [kind for _, kind in PHASES for _ in range(len(SLOTS_FOR[kind]) * TRIPS[kind])]
        in_phase = {name: k for k, name in enumerate(("even", "out0", "odd", "out1"))}

        def quarter(phase, i, j, q):
            return i * (4 * len(SLOTS_FOR[KINDS[phase]])) + (4 * (split_first[phase] + j) + q + 1)

        def load_slab(n, src, turns=0):
            for half in range(2):
                b = before[n]
                if b is not None and kind_of[b] == "ada":
                    sp.wait_ge(proj_ready, turns * 4 + (2 * b + half + 1))
                elif b is not None:
                    sp.wait_ge(lo_ready, turns * (4 * len(SLOTS_FOR[kind_of[b]])) + (4 * split_before[b] + 2 * (half + 1)))
                sp.dma_start(wbuf[:, slot[n], 8 * half:8 * half + 8, :], src[:, 8 * half:8 * half + 8, :]).then_inc(w_loaded[slot[n]][half], 16)

        def load_first(name, source):
            for j in range(len(SLOTS_FOR[KINDS[name]])):
                load_slab(first[name] + j, source(0, j))

        def load_rest(name, source):
            per = len(SLOTS_FOR[KINDS[name]])
            with sp.Fori(1, TRIPS[KINDS[name]]) as i:
                for j in range(per):
                    load_slab(first[name] + per + j, source(i, j), i - 1)

        def load_phase(name, source):
            load_first(name, source)
            load_rest(name, source)

        def cols(view, start):
            return view[:, :, bass.ds(start, GW)]

        def load_odd():
            base, per = first["odd"], 5
            for j in range(per):
                load_slab(base + j, cols(w_odd, ODD_COL[j]))
                if j == 2:
                    sp.wait_ge(phase_met, 12)
                    for b in range(SB):
                        sp.dma_start(cring[:, b, :].rearrange("p (v d) -> p v d", v=2), stateC[:, b, 0, :, :]).then_inc(c_loaded[b], 16)
            with sp.Fori(1, H) as h:
                for j in range(per):
                    load_slab(base + per + j, cols(w_odd, h * GW + ODD_COL[j]), h - 1)
                    if j == 3:
                        for b in range(SB):
                            sp.wait_ge(c_stored[b], h * 16)
                            sp.dma_start(cring[:, b, :].rearrange("p (v d) -> p v d", v=2),
                                         stateC[:, b, bass.ds(h, 1), :, :].rearrange("p h v d -> p (h v) d")).then_inc(c_loaded[b], 16)

        @block.sync
        def _(eng):
            load_phase("ada0", lambda i, j: cols(w_ada[0], i * (2 * GW) + j * GW))
            load_phase("even", lambda i, j: cols(w_even, i * GW + EVEN_COL[j]))
            out0_source = lambda i, j: cols(w_out[0], i * (2 * GW) + j * GW)
            load_slab(first["out0"], out0_source(0, 0))
            sp.wait_ge(lo_ready, 4 * split_before[first["out0"]])
            sp.wait_ge(ptab_loaded, 16)

            def load_pages(b, ring, depth, cache, loaded, freed, per_page, first_turn):
                for j in range(PAGES):
                    if not (first_turn and j < depth):
                        sp.wait_ge(freed, b * (PAGES * per_page) + (j + 1 - depth) * per_page)
                    page = sp.value_load(ptab[0:1, bass.ds(b * PAGES + j, 1)], min_val=0, max_val=79)
                    sp.dma_start(ring[:, j % depth, :], cache[:, bass.ds(page, 1), :].rearrange("t g x -> t (g x)"))\
                      .then_inc(loaded[j % depth], 16)

            load_pages(0, kring, KD, kpage, k_loaded, S["kt_turned"], 2, True)
            load_pages(1, kring, KD, kpage, k_loaded, S["kt_turned"], 2, False)
            sp.wait_ge(phase_met, 9)
            load_pages(0, vring, VD, vpage, v_loaded, S["v_used"], 1, True)
            with sp.Fori(2, SB) as b:
                load_pages(b, kring, KD, kpage, k_loaded, S["kt_turned"], 2, False)
                load_pages(b - 1, vring, VD, vpage, v_loaded, S["v_used"], 1, False)
            load_pages(SB - 1, vring, VD, vpage, v_loaded, S["v_used"], 1, False)
            sp.wait_ge(S["kt_turned"], 2 * PAGES * SB)
            load_slab(first["out0"] + 1, out0_source(0, 1))
            load_rest("out0", out0_source)
            load_phase("ada1", lambda i, j: cols(w_ada[1], i * (2 * GW) + j * GW))
            load_odd()
            load_phase("out1", lambda i, j: cols(w_out[1], i * (2 * GW) + j * GW))

        @block.gpsimd
        def _(eng):
            with pool.Fori(0, H) as h:
                for b in range(SB):
                    pool.wait_ge(S["c_new"], h * SB + (b + 1))
                    pool.dma_start(outC[:, b, bass.ds(h, 1), :, :].rearrange("p h v d -> p (h v) d"),
                                   cring[:, b, :].rearrange("p (v d) -> p v d", v=2)).then_inc(c_stored[b], 16)
            for b in range(SB):
                pool.wait_ge(c_stored[b], 16 * H)

        def slab_count(n0, i, per_phase, j):
            return i * per_phase + (n0 + j)

        def turn(out, in_, rows, width):
            return pe.transpose(out, in_, ident[0:rows, 0:rows])

        @block.tensor
        def _(eng):
            def product(phase, i, j):
                per, n = len(SLOTS_FOR[KINDS[phase]]), first[phase] + j
                for q in range(4):
                    pe.wait_ge(h_lo_ready, 4 * in_phase[phase] + q + 1)
                    pe.wait_ge(lo_ready, quarter(phase, i, j, q))
                    for mt in range(2):
                        if q == 0:
                            pe.wait_ge(proj_free, i * (2 * per) + (2 * n + mt + PF - 1))
                        cols_ = slice(mt * P, (mt + 1) * P)
                        for c in range(4):
                            for k, (w, h) in enumerate(((w_hi, h_hi), (w_hi, h_lo), (w_lo, h_hi))):
                                last = pe.matmul(proj[mt][:, 0:NT], w[:, q, c, cols_], h[:, 4 * q + c, :], start=q + c + k == 0, stop=q + c == 6 and k == 2)
                        if q == 3:
                            last.then_inc(proj_ready, 1)
                    if q < 3:
                        last.then_inc(unit_used, 1)
                pe.wait_ge(proj_ready, i * (2 * per) + (2 * n + 2))
                pe.sem_inc(unit_used, 1)

            def product_c(phase, i, j):
                n = first[phase] + j
                s = slot[n]
                for kc in range(KC):
                    if kc % 8 == 0:
                        pe.wait_ge(w_loaded[s][kc // 8], i * 16 + 16 * uses[n])
                    if kc == 0:
                        pe.wait_ge(proj_free, i * 4 + (2 * n + PF - 2))
                    last = pe.matmul(proj[j][0:NC, 0:GW], scT[:, kc, :], wbuf[:, s, kc, :], start=kc == 0, stop=kc == KC - 1)
                    if kc % 8 == 7:
                        last.then_inc(proj_ready, 1)

            def turn_mod(l):
                pe.wait_ge(proj_free, 2 * (first[f"ada{l}"] + 2 * TRIPS["ada"]) + PF)
                for c in range(48):
                    last = turn(bank[2][:, c * NC:(c + 1) * NC], mod_rows[l][:, c * P:(c + 1) * P], NC, P)
                last.then_inc(S["mod_turned"], 1)

            def wait_read(phase, i, j):
                pe.wait_ge(proj_free, i * (2 * len(SLOTS_FOR[KINDS[phase]])) + (2 * (first[phase] + j) + 2 + PF))

            def sum_squares(key, t):
                for q in range(4):
                    pe.wait_ge(S["x_squared"], 4 * norm[key] + q + 1)
                    for c in range(4 * q, 4 * q + 4):
                        last = pe.matmul(bank[4][:, 0:NT], ones[:, :], t[:, c, :], start=c == 0, stop=c == KC - 1)
                last.then_inc(S["x_summed"], 1)

            def meet(own_last, value):
                pe.wait_ge(own_last, value)
                pe.sem_inc(phase_met, 1)

            pe.wait_ge(small_loaded, 16 * N_SMALL)
            turn(bank[5][:, 0:96], prow[0:96, 0, :], 96, P)
            turn(bank[5][:, 96:184], prow[0:88, 1, :], 88, P).then_inc(S["prm_turned"], 1)
            pe.wait_ge(S["c_silu"], 1)
            for c in range(KC):
                last = turn(bank[2][:, c * NC:(c + 1) * NC], cin[:, c * P:(c + 1) * P], NC, P)
            last.then_inc(S["c_turned"], 1)
            pe.wait_ge(S["c_read"], 1)
            with pe.Fori(0, TRIPS["ada"] // 2) as i:
                for j in range(2):
                    product_c("ada0", i, j)
            pe.wait_ge(S["x_loaded"], 32)
            for c in range(KC):
                if c >= 2:
                    pe.wait_ge(S["x_read"], c - 1)
                b = bank[6 + c % 2]
                turn(b[:, 0:P], xin[:, 0, c * P:(c + 1) * P], P, P)
                turn(b[:, P:2 * P], xin[:, 1, c * P:(c + 1) * P], P, P)
                turn(b[:, TP:NT], xsin[:, c * P:(c + 1) * P], TS, P).then_inc(S["x_turned"], 1)
            pe.wait_ge(S["ones_set"], 1)
            with pe.Fori(TRIPS["ada"] // 2, TRIPS["ada"] - 2) as i:
                for j in range(2):
                    product_c("ada0", i, j)
            sum_squares("pre0", yT)
            with pe.Fori(TRIPS["ada"] - 2, TRIPS["ada"]) as i:
                for j in range(2):
                    product_c("ada0", i, j)

            turn_mod(0)
            meet(S["mod_turned"], 1)

            pe.wait_ge(phase_met, 3)
            with pe.Fori(0, TRIPS["even"]) as g:
                product("even", g, 0)
                product("even", g, 1)
                product("even", g, 2)
                wait_read("even", g, 1)
                pe.wait_ge(S["att_read"], g + 1)
                for hh in range(2):
                    pe.matmul(bank[2 + hh][:, 0:P], zq[:, hh, 0:P], zk[:, hh, 0:P], start=True, stop=True)
                    pe.matmul(bank[2 + hh][:, P:384], zq[:, hh, P:TP], zk[:, hh, 0:TP], start=True, stop=True)\
                      .then_inc(S["scores"], 1)
                for z, turned in ((zk, "ktok_turned"), (zv, "vtok_turned")):
                    if z is zv:
                        product("even", g, 3)
                        pe.wait_ge(S["ktok_read"], g + 1)
                    for hh in range(2):
                        for tc in range(2):
                            turn(bank[4][:, tc * GW + hh * P:tc * GW + (hh + 1) * P], z[:, hh, tc * P:(tc + 1) * P], P, P)
                        last = turn(bank[5][0:TS, hh * P:(hh + 1) * P], z[:, hh, TP:NT], P, TS)
                    last.then_inc(S[turned], 1)
                product("even", g, 4)
                for hh in range(2):
                    pe.wait_ge(S["p_ready"], g * 2 + (hh + 1))
                    for k in range(3):
                        last = turn(bank[6 + hh][:, k * P:(k + 1) * P], xs[hh][:, k * P:(k + 1) * P], P, P)
                    last.then_inc(S["pt_turned"], 1)
                product("even", g, 5)
                pe.wait_ge(S["vtok_read"], g + 1)
                for hh in range(2):
                    pe.wait_ge(S["pt_read"], g * 2 + (hh + 1))
                    v = vtok[:, :, hh * P:(hh + 1) * P]
                    pe.matmul(bank[2][:, hh * TP:(hh + 1) * TP], v[:, 0, :], pts[hh][:, 0:TP], start=True, stop=True)
                    last = pe.matmul(bank[2][:, hh * TP + P:(hh + 1) * TP], v[:, 1, :], pts[hh][:, TP:384], start=False, stop=True,
                                     skip_group_check=True)
                last.then_inc(S["att_out"], 1)
            meet(S["att_out"], TRIPS["even"])

            pe.wait_ge(phase_met, 6)
            for c in range(8):
                turn(pair[0][0:HIST, c * P:(c + 1) * P], yT[:, 8 + c, TP - HIST:TP], P, HIST)
                last = turn(pair[1][0:TS, c * P:(c + 1) * P], yT[:, 8 + c, TP:NT], P, TS)
            last.then_inc(S["u_turned"], 1)
            pe.wait_ge(S["pool_loaded"], 32)
            for c in range(8):
                b = bank[2 + c // 4]
                last = turn(b[:, (c % 4) * 120:(c % 4 + 1) * 120], hist[:, c * P:(c + 1) * P], 120, P)
            last.then_inc(S["hist_turned"], 1)
            for g in range(4):
                pe.wait_ge(S["d_ready"], g + 1)
                if g == 0:
                    pe.wait_ge(S["hist_read"], 2)
                if g == 1:
                    pe.wait_ge(S["u_read"], 1)
                if g >= 2:
                    pe.wait_ge(S["pool_read"], 2 * (g - 1))
                for mt in range(2):
                    for cc in range(2):
                        last = pe.matmul(bank[2 + 2 * (g % 2) + mt][:, 0:NT], pw[:, 2 * g + cc, mt * P:(mt + 1) * P], dT[:, cc, :],
                                         start=cc == 0, stop=cc == 1)
                last.then_inc(S["pool_out"], 1)
            meet(S["pool_out"], 4)

            pe.wait_ge(phase_met, 9)

            def turn_page(b, j):
                pe.wait_ge(k_loaded[j % KD], b * (16 * PAGES // KD) + 16 * (j // KD + 1))
                pe.wait_ge(S["kt_read_act"], b * PAGES + (j + 1))
                pe.wait_ge(S["kt_read_dve"], b * PAGES + (j + 1))
                for hh in range(2):
                    for h in range(4):
                        last = turn(bank[hh][:, h * P:(h + 1) * P], kring[:, j % KD, (4 * hh + h) * P:(4 * hh + h + 1) * P], P, P)
                    last.then_inc(S["kt_turned"], 1)

            def sample_scores(b):
                turn_page(b, 0)
                pe.wait_ge(S["qm_ready"], b + 1)
                pe.wait_ge(S["s_read"], b + 1)
                for j in range(PAGES):
                    pe.wait_ge(S["kt_read_act"], b * PAGES + (j + 2))
                    pe.wait_ge(S["kt_read_dve"], b * PAGES + (j + 2))
                    if j + 1 < PAGES:
                        turn_page(b, j + 1)
                    for h in range(H):
                        pe.matmul(pair[0][0:TS, j * PAGE:(j + 1) * PAGE], qm[0][:, h * TS:(h + 1) * TS],
                                  ktp[j % 2][:, h // 4, (h % 4) * P:(h % 4 + 1) * P], start=h == 0, stop=h == H - 1)
                for h in range(H):
                    last = pe.matmul(bank[2][0:TS, 0:TS], qm[0][:, h * TS:(h + 1) * TS], kTs[:, h, :], start=h == 0, stop=h == H - 1)
                last.then_inc(S["s_scores"], 1)

            def sample_values(b):
                apart(pe)
                pe.wait_ge(S["s_ready"], b + 1)
                pe.wait_ge(S["s_out_read"], b + 1)
                for j in range(PAGES):
                    turn(bank[3][:, j * TS:(j + 1) * TS], sx[0][:, j * PAGE:(j + 1) * PAGE], TS, P)
                turn(bank[3][0:TS, PAGES * TS:(PAGES + 1) * TS], sx[0][:, PAST:XW], TS, TS).then_inc(S["s_turned"], 1)
                pe.wait_ge(S["s_pt"], b + 1)
                for j in range(PAGES):
                    pe.wait_ge(v_loaded[j % VD], b * (16 * PAGES // VD) + 16 * (j // VD + 1))
                    for half in range(2):
                        last = pe.matmul(pair[1][0:TS, half * 512:(half + 1) * 512], pT[:, j * TS:(j + 1) * TS],
                                         vring[:, j % VD, half * 512:(half + 1) * 512], start=j == 0, stop=False)
                    last.then_inc(S["v_used"], 1)
                for half in range(2):
                    last = pe.matmul(pair[1][0:TS, half * 512:(half + 1) * 512], pT[0:TS, PAGES * TS:(PAGES + 1) * TS],
                                     vtok_s[:, half * 512:(half + 1) * 512], start=False, stop=True)
                last.then_inc(S["s_rows"], 1)
                apart(pe)
                pe.wait_ge(S["s_rows_read"], b + 1)
                for h in range(H):
                    last = turn(bank[3][:, h * TS:(h + 1) * TS], so[:, h * P:(h + 1) * P], TS, P)
                last.then_inc(S["s_out"], 1)

            sample_scores(0)
            with pe.Fori(1, SB) as b:
                sample_scores(b)
                sample_values(b - 1)
            sample_values(SB - 1)
            meet(S["s_out"], SB)

            pe.wait_ge(phase_met, 12)
            with pe.Fori(0, TRIPS["out"]) as i:
                for j in range(2):
                    product("out0", i, j)
            sum_squares("post0", sq)
            pe.wait_ge(proj_free, 2 * first["ada1"] + PF)
            with pe.Fori(0, TRIPS["ada"] // 2) as i:
                for j in range(2):
                    product_c("ada1", i, j)
            sum_squares("pre1", yT)
            with pe.Fori(TRIPS["ada"] // 2, TRIPS["ada"]) as i:
                for j in range(2):
                    product_c("ada1", i, j)

            turn_mod(1)

            pe.wait_ge(S["wg_loaded"], 16)
            pe.wait_ge(S["sn_loaded"], 16)
            for dc in range(2):
                last = turn(bank[4][:, dc * 64:(dc + 1) * 64], snin[:, dc * P:(dc + 1) * P], 64, P)
            last
            for kc in range(KC):
                if kc % 4 == 0:
                    pe.wait_ge(S["norm_done"], 4 * norm["pre1"] + kc // 4 + 1)
                for k in range(2):
                    last = pe.matmul(bank[2 + k][0:H, 0:NT], wg[:, kc, k * H:(k + 1) * H], yT[:, kc, :], start=kc == 0, stop=kc == KC - 1)
            last.then_inc(S["gate_sums"], 1)
            pe.wait_ge(S["rows_ready"], 1)
            for k, r in enumerate((gr["c"], gr["w"])):
                for s in range(3):
                    n = P if s < 2 else TS
                    last = turn(bank[5][0:n, 24 * k + 8 * s:24 * k + 8 * s + 8], r[:, s * P:s * P + n], H, n)
            last.then_inc(S["cw_turned"], 1)
            pe.wait_ge(S["cw_read"], 1)

            with pe.Fori(0, H) as h:
                product("odd", h, 0)
                pe.wait_ge(S["rm"], h + 1)
                pe.wait_ge(S["hs_squared"], h + 1)
                for vc in range(2):
                    last = pe.matmul(bank[4][0:H, 0:NT], csel[:, :], hsq[:, vc, :], start=vc == 0, stop=vc == 1)
                last.then_inc(S["hs_summed"], 1)
                product("odd", h, 1)
                wait_read("odd", h, 1)
                for tc in range(2):
                    for dc in range(2):
                        last = turn(bank[5][:, tc * DC + dc * P:tc * DC + (dc + 1) * P], oz["k"][:, dc, tc * P:(tc + 1) * P], P, P)
                last.then_inc(S["kt_t"], 1)
                pe.matmul(bank[6][:, 0:NT], rsel[:, :], rows[:, 0:NT], start=True, stop=True).then_inc(S["nm_bc"], 1)
                product("odd", h, 2)
                pe.wait_ge(S["cp_read"], h + 1)
                for dc in range(2):
                    pe.matmul(bank[7][:, 0:TP], oz["k"][:, dc, 0:P], oz["q"][:, dc, 0:TP], start=dc == 0, stop=dc == 1)
                for dc in range(2):
                    last = pe.matmul(bank[7][:, TP:384], oz["k"][:, dc, P:TP], oz["q"][:, dc, P:TP], start=dc == 0, stop=dc == 1)
                last.then_inc(S["st"], 1)
                pe.wait_ge(S["kt_r"], h + 1)
                wait_read("odd", h, 2)
                for tc in range(2):
                    for dc in range(2):
                        last = turn(bank[5][:, tc * DC + dc * P:tc * DC + (dc + 1) * P], ozv[:, dc, tc * P:(tc + 1) * P], P, P)
                last.then_inc(S["vt_t"], 1)
                pe.wait_ge(S["e_in"], h + 1)
                pe.matmul(bank[6][:, 0:NT], rsel[:, :], rows[:, NT:2 * NT], start=True, stop=True)
                pe.matmul(bank[6][:, NT:NT + TS], rsel[:, :], rows[:, 2 * NT + TP:3 * NT], start=True, stop=True).then_inc(S["bc2"], 1)
                product("odd", h, 3)
                pe.wait_ge(S["vt_r"], h + 1)
                for k, z in enumerate((oz["k"], ozv)):
                    for dc in range(2):
                        last = turn(bank[5][0:TS, k * DC + dc * P:k * DC + (dc + 1) * P], z[:, dc, TP:NT], P, TS)
                last.then_inc(S["smp_t"], 1)
                pe.wait_ge(S["w_ready"], h + 1)
                pe.wait_ge(S["num_read"], h + 1)
                for vc in range(2):
                    pe.matmul(bank[2 + vc][:, 0:TP], otv[:, 0, vc * P:(vc + 1) * P], ow[:, 0:TP], start=True, stop=True)
                    pe.matmul(bank[2 + vc][:, P:TP], otv[:, 1, vc * P:(vc + 1) * P], ow[:, TP:384], start=False, stop=True, skip_group_check=True)
                for dc in range(2):
                    last = pe.matmul(bank[7][0:TS, 0:TS], oz["k"][:, dc, TP:NT], oz["q"][:, dc, TP:NT], start=dc == 0, stop=dc == 1)
                last.then_inc(S["sst"], 1)
                product("odd", h, 4)
                apart(pe)
                pe.wait_ge(S["smp_r"], h + 1)
                pe.wait_ge(S["ws_ready"], h + 1)
                pe.matmul(bank[2][0:TS, DC:2 * DC], ow[0:TS, 384:384 + TS], otvs[:, :], start=True, stop=False)
                pe.wait_ge(S["den_read"], h + 1)
                pe.wait_ge(S["hs_read"], h + 1)
                pe.wait_ge(S["wc_ready"], h + 1)
                pe.wait_ge(S["kw_ready"], h + 1)
                pe.wait_ge(S["qi_ready"], h + 1)
                pe.matmul(bank[4][:, 0:TP], ones[:, :], ow[:, 0:TP], start=True, stop=True)
                pe.matmul(bank[4][:, P:TP], ones[:, :], ow[:, TP:384], start=False, stop=True, skip_group_check=True)
                pe.matmul(bank[4][:, TP:NT], ones[0:TS, :], ow[0:TS, 384:384 + TS], start=True, stop=False)
                for dc in range(2):
                    pe.matmul(bank[4][:, TP:NT], ones[:, :], onq[:, dc, :], start=False, stop=dc == 1)
                for dc in range(2):
                    pe.matmul(bank[4][:, 320 + SB * dc:320 + SB * (dc + 1)], otks[:, dc * P:(dc + 1) * P], wm[:, :], start=True, stop=True)
                for dc in range(2):
                    for sc in range(2):
                        last = pe.matmul(bank[4][:, 336 + dc:337 + dc], otk[:, sc, dc * P:(dc + 1) * P], ones[:, 0:1], start=sc == 0, stop=sc == 1)
                last.then_inc(S["den_ready"], 1)
                pe.wait_ge(S["bc2_r"], h + 1)

                def turn_state(b):
                    pe.wait_ge(c_loaded[b], h * 16 + 16)
                    for dc in range(2):
                        for vc in range(2):
                            last = turn(bank[5 + b % 2][:, dc * DC + vc * P:dc * DC + (vc + 1) * P],
                                        cring[:, b, vc * DC + dc * P:vc * DC + (dc + 1) * P], P, P)
                    last.then_inc(S["ct_t"], 1)

                turn_state(0)
                for b in range(SB):
                    if b + 1 < SB:
                        turn_state(b + 1)
                    if b:
                        pe.wait_ge(S["c_new"], h * SB + b)
                    pe.wait_ge(S["km_ready"], h * SB + (b + 1))
                    for vc in range(2):
                        last = pe.matmul(bank[7][:, vc * DC:(vc + 1) * DC], otvs[:, vc * P:(vc + 1) * P], okm[b % 2], start=True, stop=True)
                    last.then_inc(S["outer"], 1)
                    pe.wait_ge(S["ct_r"], h * SB + (b + 1))
                    for dc in range(2):
                        last = pe.matmul(bank[2][0:TS, DC:2 * DC], oqm[:, dc, b * TS:(b + 1) * TS], oct_[b % 2][:, dc, :],
                                         start=False, stop=b == SB - 1 and dc == 1)
                last.then_inc(S["ns_ready"], 1)
                pe.wait_ge(S["c_new"], h * SB + SB)
                for vc in range(2):
                    for sc in range(2):
                        last = pe.matmul(bank[7][:, vc * DC:(vc + 1) * DC], otv[:, sc, vc * P:(vc + 1) * P], otk[:, sc, :], start=sc == 0, stop=sc == 1)
                last.then_inc(S["cp_ready"], 1)
                apart(pe)
                pe.wait_ge(S["ns_read"], h + 1)
                for vc in range(2):
                    last = turn(bank[3][:, DC + vc * TS:DC + (vc + 1) * TS], ons[:, vc * P:(vc + 1) * P], TS, P)
                last.then_inc(S["num_ready"], 1)

            pe.wait_ge(S["hs_squared"], H + 1)
            for vc in range(2):
                last = pe.matmul(bank[4][0:H, 0:NT], const("colsel")[:, H * H:(H + 1) * H], hsq[:, vc, :], start=vc == 0, stop=vc == 1)
            last.then_inc(S["hs_summed"], 1)
            pe.wait_ge(S["sel_ready"], 1)
            for k in range(H):
                pe.wait_ge(S["hs_rstd"], 1)
                if k >= 2:
                    pe.wait_ge(S["hs_done"], k - 1)
                pe.matmul(bank[5 + k % 2][:, 0:NT], rsel8[:, k, :], hsum[:, :], start=True, stop=True).then_inc(S["hs_spread"], 1)
            for dc in range(2):
                turn(bank[4][0:64, dc * P:(dc + 1) * P], nnew[:, dc, :], P, 64)
                last = turn(bank[2][0:H, dc * P:(dc + 1) * P], nprm[:, dc, :], P, H)
            last.then_inc(S["n_turned"], 1)

            with pe.Fori(0, TRIPS["out"]) as i:
                for j in range(2):
                    product("out1", i, j)
            sum_squares("post1", sq)

            for k in range(12):
                f, tc = k // 3, k % 3
                rows_ = P if tc < 2 else TS
                pe.wait_ge(S["norm_done"], 4 * norm["post1"] + f + 1)
                if k >= 2:
                    pe.wait_ge(S["y_read"], k - 1)
                for c in range(4):
                    last = turn(bank[5 + k % 2][0:rows_, c * P:(c + 1) * P], xT[:, 4 * f + c, tc * P:tc * P + rows_], P, rows_)
                last.then_inc(S["y_turned"], 1)

        @block.scalar
        def _(eng):
            A1 = AO.link

            def high(phase, i, j, quarters):
                n = first[phase] + j
                s = slot[n]
                for q in quarters:
                    act.wait_ge(w_loaded[s][q // 2], i * (16 * SLOTS_FOR[KINDS[phase]].count(s)) + 16 * uses[n])
                    act.wait_ge(unit_used, quarter(phase, i, j, q))
                    A1(act.activation(w_hi[:, q, :, :], wbuf[:, s, 4 * q:4 * q + 4, :], ACT.Copy), hi_ready)

            def evacuate(phase, i, j, outs, more=True):
                per, n = len(SLOTS_FOR[KINDS[phase]]), first[phase] + j
                nxt = (i, j + 1) if j + 1 < per else (i + 1, 0)
                if more:
                    high(phase, *nxt, range(3))
                for mt in range(2):
                    act.wait_ge(proj_ready, i * (2 * per) + (2 * n + mt + 1))
                    outs(mt, proj[mt])
                if more:
                    high(phase, *nxt, range(3, 4))

            def high_h(phase, ready=None):
                for q in range(4):
                    if ready:
                        ready(q)
                    A1(act.activation(h_hi[:, 4 * q:4 * q + 4, :], yT[:, 4 * q:4 * q + 4, :], ACT.Copy), h_hi_ready)

            def squares(key, src, dst):
                for q in range(4):
                    A1(act.activation(dst[:, 4 * q:4 * q + 4, :], src[:, 4 * q:4 * q + 4, :], ACT.Square), S["x_squared"])

            def root(key, summed, n):
                act.wait_ge(S["x_summed"], norm[key] + 1)
                A1(act.activation(rstd[:, :], summed, ACT.Ln, bias=eps, scale=1.0 / n))
                A1(act.activation(rstd[:, :], rstd[:, :], ACT.Exp, scale=-0.5), S["x_rstd"])

            act.dma_start(cin[0:1, :], A["c_prompt"]).then_inc(small_loaded, 16)
            act.dma_start(cin[1:NC, :], A["c_sample"]).then_inc(small_loaded, 16)
            act.dma_start(cst[:, :], A["constants"]).then_inc(small_loaded, 16)
            act.dma_start(prow[0:96, 0, :], A["ada_b"].rearrange("l (c p) -> (l c) p", p=P)).then_inc(small_loaded, 16)
            act.dma_start(prow[0:32, 1, :], A["norm_pre"].rearrange("l (c p) -> (l c) p", p=P)).then_inc(small_loaded, 16)
            act.dma_start(prow[32:64, 1, :], A["norm_post"].rearrange("l (c p) -> (l c) p", p=P)).then_inc(small_loaded, 16)
            act.dma_start(prow[64:72, 1, :], A["pool_scale"].rearrange("l (c p) -> (l c) p", p=P)).then_inc(small_loaded, 16)
            act.dma_start(prow[72:88, 1, :], A["head_norm"].rearrange("l (c p) -> (l c) p", p=P)).then_inc(small_loaded, 16)
            act.dma_start(bif[:, 0:1], A["b_igate"].rearrange("a h -> h a")).then_inc(small_loaded, 16)
            act.dma_start(bif[:, 1:2], A["b_fgate"].rearrange("a h -> h a")).then_inc(small_loaded, 16)
            act.dma_start(xin[:, :, :], A["x_prompt"][0].rearrange("(c p) d -> p c d", p=P)).then_inc(S["x_loaded"], 16)
            act.dma_start(xsin[:, :], A["x_sample"].rearrange("b t d -> (b t) d")).then_inc(S["x_loaded"], 16)
            act.dma_start(ptab[:, :], A["page_table"].rearrange("b (g a) -> a (b g)", a=1)).then_inc(ptab_loaded, 16)
            for s, n in ((proj_free, PF), (S["kt_read_act"], 1), (S["cp_read"], 1), (S["hs_squared"], 1)):
                AO.credit(s, n)
            act.sem_inc(unit_used, 4)
            act.wait_ge(small_loaded, 16 * N_SMALL)
            A1(act.activation(cexp[:, :], cin[:, :], ACT.Exp, scale=-1.0), S["c_exp"])

            def read_mod(phase, layer, i, j):
                n = first[phase] + j
                act.wait_ge(proj_ready, i * 4 + (2 * n + 2))
                for mt in range(2):
                    A1(act.activation(mod_rows[layer][:, bass.ds(i * (4 * P) + (2 * j + mt) * P, P)], proj[j][0:NC, mt * P:(mt + 1) * P], ACT.Copy),
                       proj_free)

            half = TRIPS["ada"] // 2
            with AO.turns(0, half, proj_free=4) as i:
                for j in range(2):
                    read_mod("ada0", 0, i, j)
            act.wait_ge(S["x_read"], KC)
            squares("pre0", xT, yT)
            with AO.turns(half, TRIPS["ada"] - 2, proj_free=4) as i:
                for j in range(2):
                    read_mod("ada0", 0, i, j)
            root("pre0", bank[4][:, 0:NT], D)
            with AO.turns(TRIPS["ada"] - 2, TRIPS["ada"], proj_free=4) as i:
                for j in range(2):
                    read_mod("ada0", 0, i, j)
            act.sem_inc(phase_met, 1)
            high("even", 0, 0, range(4))
            high_h("even", lambda q: act.wait_ge(S["norm_done"], 4 * norm["pre0"] + q + 1))

            act.wait_ge(phase_met, 3)

            def into(z):
                return lambda mt, b: A1(act.activation(z[:, mt, :], b[:, 0:NT], ACT.Copy), proj_free)

            kout = OUT["k_prompt"][0, 0].rearrange("(c p) h d -> p c (h d)", p=P)
            vout = OUT["v_prompt"][0, 0].rearrange("(c p) h d -> p c (h d)", p=P)
            with AO.turns(0, TRIPS["even"], hi_ready=24, proj_free=12, ktok_read=1, vtok_read=1, ga_exp=1, gb_exp=1, p_exp=2, pt_read=2, act_order=8) as g:
                act.wait_ge(S["qk_kept"], g + 1)
                evacuate("even", g, 0, into(zq))
                evacuate("even", g, 1, into(zk))
                evacuate("even", g, 2, into(zv))

                def tokens(tok, tok_s, turned, read, out):
                    act.wait_ge(S[turned], g + 1)
                    act.wait_ge(stored, g * 32 + (16 if tok is ktok else 32))
                    A1(act.activation(tok[:, :, :].rearrange("p a n -> p (a n)"), bank[4][:, :], ACT.Copy))
                    A1(act.activation(tok_s[:, bass.ds(g * GW, GW)], bank[5][0:TS, 0:GW], ACT.Copy), S[read])
                    act.dma_start(out[:, :, bass.ds(g * GW, GW)], tok[:, :, :]).then_inc(stored, 16)

                tokens(ktok, ktok_s, "ktok_turned", "ktok_read", kout)
                act.wait_ge(S["att_read"], g + 1)

                def gate_a(mt, b):
                    A1(act.activation(zga[:, mt, :], b[:, 0:NT], ACT.Copy))
                    A1(act.activation(ega[:, mt, :], b[:, 0:NT], ACT.Exp, scale=-1.0), proj_free)

                evacuate("even", g, 3, gate_a)
                act.sem_inc(S["ga_exp"], 1)
                AO.count(S["ga_exp"]).k += 1
                for hh in range(2):
                    act.wait_ge(S["x_max"], g * 2 + (hh + 1))
                    for c, (a, b) in enumerate(((0, P), (P, 384))):
                        A1(act.activation(xs[hh][:, a:b], xs[hh][:, a:b], ACT.Exp, bias=stat[:, 2 * hh + c, 1:2], scale=SCALE,
                                          accum_out=stat[:, 2 * hh + c, 2:3]), S["p_exp"] if c else None)
                tokens(vtok, vtok_s, "vtok_turned", "vtok_read", vout)
                evacuate("even", g, 4, lambda mt, b: A1(act.activation(
                    yT[:, bass.ds(g * 2 + (8 + mt), 1), :].rearrange("p a t -> p (a t)"), b[:, 0:NT], ACT.Copy), proj_free))
                for hh in range(2):
                    act.wait_ge(S["pt_turned"], g * 2 + (hh + 1))
                    A1(act.activation(pts[hh][:, :], bank[6 + hh][:, 0:384], ACT.Copy), S["pt_read"])
                act.wait_ge(S["silu_gb"], g + 1)

                def gate_b(mt, b):
                    A1(act.activation(gbs[:, bass.ds(g * 2 + mt, 1), :].rearrange("p a t -> p (a t)"), b[:, 0:NT], ACT.Copy))
                    A1(act.activation(egb[:, mt, :], b[:, 0:NT], ACT.Exp, scale=-1.0), proj_free)

                evacuate("even", g, 5, gate_b)
                act.sem_inc(S["gb_exp"], 1)
                AO.count(S["gb_exp"]).k += 1
            even_stored = 16 * 2 * TRIPS["even"] + 16
            act.wait_ge(stored, even_stored)
            for name, tok in (("k_sample", ktok_s), ("v_sample", vtok_s)):
                store(OUT[name][0].rearrange("b t h d -> (b t) (h d)"), tok[:, :])
            act.wait_ge(stored, even_stored + 32)
            act.sem_inc(phase_met, 1)

            act.wait_ge(phase_met, 6)
            act.dma_start(hist[:, :], A["state_pool"][0].rearrange("b j c -> (b j) c")).then_inc(S["pool_loaded"], 16)
            act.dma_start(pw[:, :, :], A["pool_w"][0].rearrange("g (c p) d -> p (g c) d", p=P)).then_inc(S["pool_loaded"], 16)
            store(OUT["pool_sample"][0][:, 0:HIST - ST, :], A["state_pool"][0][:, ST:HIST, :])
            act.wait_ge(S["u_turned"], 1)
            A1(act.activation(utok[:, :], pair[0][0:HIST, :], ACT.Copy))
            A1(act.activation(ustok[:, :], pair[1][0:TS, :], ACT.Copy), S["u_read"])
            store(OUT["pool_prompt"][0, 0], utok[:, :])
            for b in range(SB):
                store(OUT["pool_sample"][0][b, HIST - ST:HIST, :], ustok[b * ST:(b + 1) * ST, :])
            act.wait_ge(stored, even_stored + 32 + 16 * (2 + SB))
            act.sem_inc(phase_met, 1)

            act.wait_ge(phase_met, 9)
            def halves(b):
                for j in range(PAGES):
                    act.wait_ge(S["kt_turned"], b * (2 * PAGES) + (2 * j + 1))
                    A1(act.activation(ktp[j % 2][:, 0, :], bank[0][:, :], ACT.Copy), S["kt_read_act"])

            def softmax(b):
                act.wait_ge(S["s_max"], b + 1)
                A1(act.activation(sx[0][:, :], sx[0][:, :], ACT.Exp, bias=sstat[:, 1:2], scale=SCALE, accum_out=sstat[:, 2:3]), S["s_exp"])

            def values_out(b):
                act.wait_ge(S["s_rows"], b + 1)
                A1(act.activation(so[:, :], pair[1][0:TS, :], ACT.Copy), S["s_rows_read"])

            halves(0)
            softmax(0)
            with AO.turns(1, SB, kt_read_act=PAGES, s_exp=1, s_rows_read=1) as b:
                halves(b)
                softmax(b)
                values_out(b - 1)
            values_out(SB - 1)
            act.sem_inc(phase_met, 1)

            act.wait_ge(phase_met, 12)
            act.dma_start(wg[:, :, :], w_odd[:, :, 5 * D:5 * D + 2 * H]).then_inc(S["wg_loaded"], 16)
            act.dma_start(snin[:, :], A["state_n"][0].rearrange("b h d -> (b h) d")).then_inc(S["sn_loaded"], 16)
            act.dma_start(gr["w"][:, 0:SB], A["state_m"][0].rearrange("b h -> h b"), allow_slow_non_contiguous=True).then_inc(S["m0_loaded"], 16)

            def read_mix(phase):
                def outs(i, j):
                    return lambda mt, b: A1(act.activation(yT[:, bass.ds(i * 4 + (2 * j + mt), 1), :].rearrange("p a t -> p (a t)"), b[:, 0:NT], ACT.Copy), proj_free)
                with AO.turns(0, TRIPS["out"] - 1, proj_free=4, hi_ready=8) as i:
                    for j in range(2):
                        evacuate(phase, i, j, outs(i, j))
                i = TRIPS["out"] - 1
                for j in range(2):
                    evacuate(phase, i, j, outs(i, j), more=j == 0)

            high_h("out0")
            read_mix("out0")
            squares("post0", yT, sq)
            root("post0", bank[4][:, 0:NT], D)
            with AO.turns(0, TRIPS["ada"] // 2, proj_free=4) as i:
                for j in range(2):
                    read_mod("ada1", 1, i, j)
            act.wait_ge(S["norm_done"], 4 * norm["post0"] + 4)
            squares("pre1", xT, yT)
            root("pre1", bank[4][:, 0:NT], D)
            with AO.turns(TRIPS["ada"] // 2, TRIPS["ada"], proj_free=4) as i:
                for j in range(2):
                    read_mod("ada1", 1, i, j)
            high("odd", 0, 0, range(4))
            high_h("odd", lambda q: act.wait_ge(S["norm_done"], 4 * norm["pre1"] + q + 1))

            act.wait_ge(S["gx"], 1)
            A1(act.activation(gr["w"][:, :], gr["M"][:, :], ACT.Exp, scale=-1.0))
            A1(act.activation(gr["w"][:, :], gr["w"][:, :], ACT.Ln, bias=1.0), S["g_ln"])
            act.wait_ge(S["gl_ready"], 1)
            A1(act.activation(rows[:, NT:3 * NT], rows[:, NT:3 * NT], ACT.Exp))
            A1(act.activation(gr["w"][:, :], gr["w"][:, :], ACT.Exp), S["rows_ready"])
            store(OUT["m_prompt"][0].rearrange("a h -> h a"), gr["t1"][:, TP - 1:TP])
            store(OUT["m_sample"][0].rearrange("b h -> h b"), gr["t1"][:, TP:NT].rearrange("h (b t) -> h b t", t=ST)[:, :, ST - 1], slow=True)
            act.wait_ge(stored, even_stored + 16 * n_store[0])
            n_store.append(even_stored + 16 * n_store[0])

            cp_stored = S["cp_stored"]
            with AO.turns(0, H, hi_ready=20, hs_squared=1, proj_free=10, kt_r=1, vt_r=1, e_exp=1, bc2_r=1, smp_r=1, ct_r=SB, ns_read=1, cp_read=1, act_order=4) as h:
                for j, z in enumerate((oz["q"], oz["k"])):
                    evacuate("odd", h, j, lambda mt, b: A1(act.activation(z[:, mt, :], b[:, 0:NT], ACT.Copy, scale=KSCALE if j else 1.0), proj_free))
                act.wait_ge(S["kt_t"], h + 1)
                A1(act.activation(otk[:, :, :].rearrange("p a n -> p (a n)"), bank[5][:, :], ACT.Copy), S["kt_r"])
                act.wait_ge(S["e_in"], h + 1)
                A1(act.activation(oe[:, 0:384], oe[:, 0:384], ACT.Exp))
                A1(act.activation(oe[0:TS, 384:384 + TS], oe[0:TS, 384:384 + TS], ACT.Exp), S["e_exp"])
                evacuate("odd", h, 2, into(ozv))
                act.wait_ge(S["vt_t"], h + 1)
                A1(act.activation(otv[:, :, :].rearrange("p a n -> p (a n)"), bank[5][:, :], ACT.Copy), S["vt_r"])
                act.wait_ge(S["bc2"], h + 1)
                act.wait_ge(S["den_read"], h + 1)
                A1(act.activation(obc[:, :], bank[6][:, 0:NT + TS], ACT.Copy), S["bc2_r"])
                act.wait_ge(S["num_read"], h + 1)
                evacuate("odd", h, 3, lambda mt, b: A1(act.activation(oz["eo"][:, mt, :], b[:, 0:NT], ACT.Exp, scale=-1.0), proj_free))
                act.wait_ge(S["smp_t"], h + 1)
                A1(act.activation(otks[:, :], bank[5][0:TS, 0:DC], ACT.Copy))
                A1(act.activation(otvs[:, :], bank[5][0:TS, DC:2 * DC], ACT.Copy), S["smp_r"])
                act.wait_ge(S["gate_done"], h + 1)

                def gate(mt, b):
                    A1(act.activation(oz["g"][:, mt, :], b[:, 0:NT], ACT.Copy))
                    A1(act.activation(oz["eg"][:, mt, :], b[:, 0:NT], ACT.Exp, scale=-1.0), proj_free)

                evacuate("odd", h, 4, gate)
                act.wait_ge(cp_stored, h * 16 + 16)
                for b in range(SB):
                    act.wait_ge(S["ct_t"], h * SB + (b + 1))
                    A1(act.activation(oct_[b % 2][:, :, :].rearrange("p a n -> p (a n)"), bank[5 + b % 2][:, :], ACT.Copy), S["ct_r"])
                act.wait_ge(S["ns_ready"], h + 1)
                A1(act.activation(ons[:, :], bank[2][0:TS, DC:2 * DC], ACT.Copy), S["ns_read"])
                act.wait_ge(S["cp_ready"], h + 1)
                A1(act.activation(ocp[:, :], bank[7][:, :], ACT.Copy), S["cp_read"])
                act.dma_start(OUT["C_prompt"][0, 0, bass.ds(h, 1), :, :].rearrange("h (v p) d -> p (h v) d", p=P),
                              ocp[:, :].rearrange("p (v d) -> p v d", v=2)).then_inc(cp_stored, 16)
                act.wait_ge(S["num_read"], h + 2)
                A1(act.activation(hsq[:, :, :], yT[:, bass.ds(h * 2, 2), :], ACT.Square), S["hs_squared"])

            act.wait_ge(S["hs_read"], H + 1)
            A1(act.activation(hsum[:, :], hsum[:, :], ACT.Ln, bias=eps[0:H, :], scale=1.0 / DC))
            A1(act.activation(hsum[:, :], hsum[:, :], ACT.Exp, scale=-0.5), S["hs_rstd"])
            high_h("out1", lambda q: act.wait_ge(S["hs_done"], 2 * q + 2))
            act.wait_ge(S["n_turned"], 1)
            A1(act.activation(nout[:, :, :].rearrange("p a n -> p (a n)"), bank[4][0:64, 0:DC], ACT.Copy))
            A1(act.activation(npout[:, :, :].rearrange("p a n -> p (a n)"), bank[2][0:H, 0:DC], ACT.Copy))
            store(OUT["n_sample"][0].rearrange("b h d -> (b h) d"), nout[:, :, :].rearrange("p a n -> p (a n)"))
            store(OUT["n_prompt"][0, 0], npout[:, :, :].rearrange("p a n -> p (a n)"))

            read_mix("out1")
            squares("post1", yT, sq)
            root("post1", bank[4][:, 0:NT], D)
            yout = [OUT["y_prompt"][0, 0:P, :], OUT["y_prompt"][0, P:TP, :], OUT["y_sample"].rearrange("b t d -> (b t) d")]
            for k in range(12):
                f, tc = k // 3, k % 3
                n = P if tc < 2 else TS
                if k < 9:
                    stage = sq.rearrange("p a t -> p (a t)")[0:n, k * 512:(k + 1) * 512]
                else:
                    stage = cring[0:n, k - 9, :]
                    act.wait_ge(c_stored[k - 9], 16 * H)
                act.wait_ge(S["y_turned"], k + 1)
                A1(act.activation(stage, bank[5 + k % 2][0:n, :], ACT.Copy), S["y_read"])
                store(yout[tc][:, f * 512:(f + 1) * 512], stage)
            act.wait_ge(stored, even_stored + 16 * n_store[0])
            act.wait_ge(cp_stored, 16 * H + 16)

        @block.vector
        def _(eng):
            V1 = VO.link

            def wide(ap, n):
                return ap.unsqueeze(2).broadcast_to([ap.shape[0], ap.shape[1], n])

            def over(ap, n):
                return ap.unsqueeze(1).broadcast_to([ap.shape[0], n, ap.shape[1]])

            def batches(t):
                return t[:, :, TP:NT].rearrange("p c (b t) -> p c b t", t=ST)

            def by_batch(m):
                return m[:, :, 1:NC].unsqueeze(3).broadcast_to([P, m.shape[1], SB, ST])

            def low(phase, i, j):
                s = slot[first[phase] + j]
                for q in range(4):
                    dve.wait_ge(hi_ready, quarter(phase, i, j, q))
                    V1(dve.tensor_tensor(w_lo[:, q, :, :], wbuf[:, s, 4 * q:4 * q + 4, :], w_hi[:, q, :, :].bitcast(F32), ALU.subtract), lo_ready)

            def low_h(phase, q):
                dve.wait_ge(h_hi_ready, 4 * in_phase[phase] + q + 1)
                c = slice(4 * q, 4 * q + 4)
                V1(dve.tensor_tensor(h_lo[:, c, :], yT[:, c, :], h_hi[:, c, :].bitcast(F32), ALU.subtract), h_lo_ready)

            def low_mix_rest(phase):
                with VO.turns(0, TRIPS["out"] - 1, lo_ready=8) as i:
                    low(phase, i, 1)
                    low(phase, i + 1, 0)
                low(phase, TRIPS["out"] - 1, 1)

            def prepare(l):
                dve.wait_ge(S["mod_turned"], l + 1)
                m = modT[:, 48 * l:48 * (l + 1), :]
                V1(dve.tensor_tensor(m, bank[2][:, 0:48 * NC].rearrange("p (c n) -> p c n", n=NC), wide(adab[:, 48 * l:48 * (l + 1)], NC), ALU.add))
                V1(dve.scalar_tensor_tensor(out=m[:, 16:32, :], in0=m[:, 16:32, :], scalar=1.0, in1=wide(npre[:, 16 * l:16 * l + 16], NC),
                                            op0=ALU.add, op1=ALU.mult))
                V1(dve.tensor_tensor(m[:, 32:48, :], m[:, 32:48, :], wide(npost[:, 16 * l:16 * l + 16], NC), ALU.mult))

            def pre_norm(l, phase):
                m = modT[:, 48 * l:48 * (l + 1), :]
                dve.wait_ge(S["x_rstd"], norm[f"pre{l}"] + 1)
                V1(dve.tensor_tensor(yT[:, :, :], xT[:, :, :], over(rstd[:, :], KC), ALU.mult))
                low(phase, 0, 0)
                prepare(l)
                for q in range(4):
                    y = yT[:, 4 * q:4 * q + 4, :]
                    for c in range(4 * q, 4 * q + 4):
                        V1(dve.tensor_scalar(yT[:, c, 0:TP], yT[:, c, 0:TP], m[:, 16 + c, 0:1], m[:, c, 0:1], ALU.mult, ALU.add))
                    V1(dve.tensor_tensor(batches(y), batches(y), by_batch(m[:, 16 + 4 * q:20 + 4 * q, :]), ALU.mult))
                    V1(dve.tensor_tensor(batches(y), batches(y), by_batch(m[:, 4 * q:4 * q + 4, :]), ALU.add), S["norm_done"])
                    if q:
                        low_h(phase, q - 1)
                low_h(phase, 3)

            def post_norm(l):
                m = modT[:, 48 * l:48 * (l + 1), :]
                dve.wait_ge(S["x_rstd"], norm[f"post{l}"] + 1)
                for q in range(4):
                    c4 = slice(4 * q, 4 * q + 4)
                    y, x = yT[:, c4, :], xT[:, c4, :]
                    V1(dve.tensor_tensor(y, y, over(rstd[:, :], 4), ALU.mult))
                    for c in range(4 * q, 4 * q + 4):
                        V1(dve.scalar_tensor_tensor(out=xT[:, c, 0:TP], in0=yT[:, c, 0:TP], scalar=m[:, 32 + c, 0:1], in1=xT[:, c, 0:TP],
                                                    op0=ALU.mult, op1=ALU.add))
                    V1(dve.tensor_tensor(batches(y), batches(y), by_batch(m[:, 32 + 4 * q:36 + 4 * q, :]), ALU.mult))
                    V1(dve.tensor_tensor(batches(x), batches(x), batches(y), ALU.add), S["norm_done"])

            for s, n in ((S["att_read"], 1), (S["qk_kept"], 1), (S["silu_gb"], 1), (S["kt_read_dve"], 1), (S["s_read"], 1), (S["s_out_read"], 1),
                         (S["num_read"], 1), (S["den_read"], 1), (S["gate_done"], 1), (stored, 16), (S["cp_stored"], 16)):
                VO.credit(s, n)
            V1(dve.memset(ones[:, :], 1.0), S["ones_set"])
            dve.wait_ge(S["prm_turned"], 1)
            V1(dve.tensor_copy(prm[:, :], bank[5][:, 0:184]))
            dve.wait_ge(S["c_exp"], 1)
            V1(dve.tensor_scalar(cexp[:, :], cexp[:, :], 1.0, None, ALU.add))
            V1(dve.reciprocal(cexp[:, :], cexp[:, :]))
            V1(dve.tensor_tensor(cin[:, :], cin[:, :], cexp[:, :], ALU.mult), S["c_silu"])
            dve.wait_ge(S["c_turned"], 1)
            V1(dve.tensor_copy(scT[:, :, :].rearrange("p a n -> p (a n)"), bank[2][:, 0:KC * NC]), S["c_read"])
            for c in range(KC):
                dve.wait_ge(S["x_turned"], c + 1)
                V1(dve.tensor_copy(xT[:, c, :], bank[6 + c % 2][:, 0:NT]), S["x_read"])
            dve.sem_inc(phase_met, 1)
            pre_norm(0, "even")

            dve.wait_ge(phase_met, 3)
            with VO.turns(0, TRIPS["even"], lo_ready=24, qk_kept=1, x_max=2, p_ready=2, silu_gb=1, att_read=1, dve_order=17) as g:
                low("even", g, 1)
                low("even", g, 2)
                dve.wait_ge(proj_free, g * 12 + (2 * first["even"] + 4 + PF))
                V1(dve.tensor_copy(qTs[:, bass.ds(g * 2, 2), :], zq[:, :, TP:NT]))
                V1(dve.tensor_copy(kTs[:, bass.ds(g * 2, 2), :], zk[:, :, TP:NT]), S["qk_kept"])
                low("even", g, 3)
                for hh in range(2):
                    dve.wait_ge(S["scores"], g * 2 + (hh + 1))
                    V1(dve.scalar_tensor_tensor(out=xs[hh][:, :], in0=const("dist"), scalar=const("slope")[:, bass.ds(g * 2 + hh, 1)],
                                                in1=bank[2 + hh][:, 0:384], op0=ALU.mult, op1=ALU.add))
                    V1(dve.reduce_max(stat[:, 2 * hh, 0:1], xs[hh][:, 0:P], AX.X))
                    V1(dve.reduce_max(stat[:, 2 * hh + 1, 0:1], xs[hh][:, P:384], AX.X))
                    V1(dve.tensor_scalar(stat[:, 2 * hh:2 * hh + 2, 1], stat[:, 2 * hh:2 * hh + 2, 0], -SCALE, None, ALU.mult), S["x_max"])
                low("even", g, 4)
                dve.wait_ge(S["ga_exp"], g + 1)
                V1(dve.tensor_scalar(ega[:, :, :], ega[:, :, :], 1.0, None, ALU.add))
                V1(dve.reciprocal(ega[:, :, :], ega[:, :, :]))
                V1(dve.tensor_tensor(ega[:, :, :], ega[:, :, :], zga[:, :, :], ALU.mult))
                V1(dve.tensor_copy(gas[:, bass.ds(g * 2, 2), :], ega[:, :, TP:NT]))
                for hh in range(2):
                    dve.wait_ge(S["p_exp"], g * 2 + (hh + 1))
                    V1(dve.reciprocal(stat[:, 2 * hh:2 * hh + 2, 3], stat[:, 2 * hh:2 * hh + 2, 2]))
                    V1(dve.tensor_scalar(xs[hh][:, 0:P], xs[hh][:, 0:P], stat[:, 2 * hh, 3:4], None, ALU.mult))
                    V1(dve.tensor_scalar(xs[hh][:, P:384], xs[hh][:, P:384], stat[:, 2 * hh + 1, 3:4], None, ALU.mult), S["p_ready"])
                low("even", g, 5)
                low("even", g + 1, 0)
                dve.wait_ge(S["gb_exp"], g + 1)
                V1(dve.tensor_scalar(egb[:, :, :], egb[:, :, :], 1.0, None, ALU.add))
                V1(dve.reciprocal(egb[:, :, :], egb[:, :, :]))
                gb = gbs[:, bass.ds(g * 2, 2), :]
                V1(dve.tensor_tensor(gb, gb, egb[:, :, :], ALU.mult), S["silu_gb"])
                dve.wait_ge(S["att_out"], g + 1)
                V1(dve.tensor_tensor(yT[:, bass.ds(g * 2, 2), 0:TP], bank[2][:, :].rearrange("p (a t) -> p a t", a=2), ega[:, :, 0:TP], ALU.mult), S["att_read"])
            dve.sem_inc(phase_met, 1)

            dve.wait_ge(phase_met, 6)
            for t in uext:
                V1(dve.memset(t[:, :, 0:16], 0.0))
            sv = sext.rearrange("p c (b t) -> p c b t", t=19)
            dve.wait_ge(S["hist_turned"], 1)
            for k in range(2):
                V1(dve.tensor_copy(sv[:, 4 * k:4 * k + 4, :, 0:HIST], bank[2 + k][:, 0:480].rearrange("p (c b j) -> p c b j", c=4, b=SB)), S["hist_read"])
            V1(dve.tensor_copy(sv[:, :, :, HIST:19], yT[:, 8:16, TP:NT].rearrange("p c (b t) -> p c b t", t=ST)))

            def pool_read(g):
                dve.wait_ge(S["pool_out"], g + 1)
                for mt in range(2):
                    V1(dve.scalar_tensor_tensor(out=yT[:, 8 + 2 * g + mt, :], in0=bank[2 + 2 * (g % 2) + mt][:, 0:NT], scalar=pscale[:, 2 * g + mt:2 * g + mt + 1],
                                                in1=gbs[:, 2 * g + mt, :], op0=ALU.mult, op1=ALU.mult), S["pool_read"])

            for g, w in enumerate(WINDOWS):
                u = yT[:, 8 + 2 * g:10 + 2 * g, :]
                V1(dve.tensor_copy(uext[0][:, :, 16:], u[:, :, 0:TP]))
                se = sext[:, 2 * g:2 * g + 2, :].rearrange("p c (b t) -> p (c b) t", t=19)
                ssrc = se
                for k in range(g + 1):
                    d = 1 << k
                    a, b = uext[k % 2], uext[(k + 1) % 2]
                    V1(dve.tensor_tensor(b[:, :, 16:], a[:, :, 16:], a[:, :, 16 - d:16 + TP - d], ALU.add))
                    lo = 2 * d - 1
                    V1(dve.tensor_tensor(swin[k % 2][:, :, lo:19], ssrc[:, :, lo:19], ssrc[:, :, lo - d:19 - d], ALU.add))
                    ssrc = swin[k % 2]
                win = uext[(g + 1) % 2]
                if g:
                    dve.wait_ge(S["pool_out"], g)
                V1(dve.scalar_tensor_tensor(out=dT[:, :, 0:TP], in0=win[:, :, 16:], scalar=1.0 / w, in1=u[:, :, 0:TP], op0=ALU.mult, op1=ALU.subtract))
                V1(dve.tensor_tensor(dT[:, :, 0:16], win[:, :, 16:32], over(const("invcnt")[:, 16 * g:16 * g + 16], 2), ALU.mult))
                V1(dve.tensor_tensor(dT[:, :, 0:16], dT[:, :, 0:16], u[:, :, 0:16], ALU.subtract))
                for cc in range(2):
                    V1(dve.scalar_tensor_tensor(out=dT[:, cc, TP:NT].rearrange("p (b t) -> p b t", t=ST), in0=ssrc[:, SB * cc:SB * (cc + 1), HIST:19],
                                                scalar=1.0 / w, in1=se[:, SB * cc:SB * (cc + 1), HIST:19], op0=ALU.mult, op1=ALU.subtract),
                       S["d_ready"] if cc else None)
                if g == 0:
                    dve.wait_ge(S["u_turned"], 1)
                else:
                    pool_read(g - 1)
            pool_read(3)
            dve.sem_inc(phase_met, 1)

            dve.wait_ge(phase_met, 9)
            V1(dve.memset(qm[0][:, 0:288], 0.0))
            heads_q = qm[0][:, 0:288].rearrange("p (h x) -> p h x", x=TS + ST)[:, :, 0:ST]
            x = sx[0]
            x4 = x[:, 0:PAST].rearrange("p (n k) -> p n k", n=NB)
            gates, least, rank, drop = sstat[:, 4:8], sstat[:, 8:9], sstat[:, 9:13], sstat[:, 13:14]

            def scores_of(b, first_turn):
                if not first_turn:
                    dve.wait_ge(S["s_scores"], b)
                V1(dve.tensor_copy(heads_q, qTs[:, :, bass.ds(b * ST, ST)]), S["qm_ready"])
                for j in range(PAGES):
                    dve.wait_ge(S["kt_turned"], b * (2 * PAGES) + (2 * j + 2))
                    V1(dve.tensor_copy(ktp[j % 2][:, 1, :], bank[1][:, :]), S["kt_read_dve"])

            def weights_of(b):
                dve.wait_ge(S["s_scores"], b + 1)
                V1(dve.tensor_tensor(x[:, 0:PAST], pair[0][0:TS, :], const("sbias", TS), ALU.add))
                V1(dve.tensor_tensor(x[:, PAST:XW], bank[2][0:TS, 0:TS], const("own", TS)[:, bass.ds(b * TS, TS)], ALU.add))
                V1(dve.tensor_reduce(gates, pair[0][0:TS, :].rearrange("p (n k) -> p n k", n=NB), AX.X, ALU.add), S["s_read"])
                V1(dve.tensor_reduce(least, gates, AX.X, ALU.min))
                V1(dve.scalar_tensor_tensor(out=rank, in0=gates, scalar=least, in1=const("rank", TS), op0=ALU.is_equal, op1=ALU.mult))
                V1(dve.reduce_max(drop, rank, AX.X))
                V1(dve.tensor_scalar(rank, const("rank", TS), drop, -BIG, ALU.is_equal, ALU.mult))
                V1(dve.tensor_tensor(x4, x4, wide(rank, BLOCK), ALU.add))
                V1(dve.reduce_max(sstat[:, 0:1], x, AX.X))
                V1(dve.tensor_scalar(sstat[:, 1:2], sstat[:, 0:1], -SCALE, None, ALU.mult), S["s_max"])
                dve.wait_ge(S["s_exp"], b + 1)
                V1(dve.reciprocal(sstat[:, 3:4], sstat[:, 2:3]))
                V1(dve.tensor_scalar(x, x, sstat[:, 3:4], None, ALU.mult), S["s_ready"])

            def turned_weights(b):
                dve.wait_ge(S["s_turned"], b + 1)
                V1(dve.tensor_copy(pT[:, 0:PAGES * TS], bank[3][:, 0:PAGES * TS]))
                V1(dve.tensor_copy(pT[0:TS, PAGES * TS:(PAGES + 1) * TS], bank[3][0:TS, PAGES * TS:(PAGES + 1) * TS]), S["s_pt"])

            def output_of(b):
                dve.wait_ge(S["s_out"], b + 1)
                V1(dve.tensor_tensor(yT[:, 0:H, bass.ds(b * ST + TP, ST)], bank[3][:, 0:H * (TS + ST)].rearrange("p (h x) -> p h x", x=TS + ST)[:, :, 0:ST],
                                     gas[:, :, bass.ds(b * ST, ST)], ALU.mult), S["s_out_read"])

            scores_of(0, True)
            weights_of(0)
            with VO.turns(1, SB, qm_ready=1, kt_read_dve=PAGES, s_read=1, s_max=1, s_ready=1, s_pt=1, s_out_read=1, dve_order=10) as b:
                scores_of(b, False)
                turned_weights(b - 1)
                weights_of(b)
                output_of(b - 1)
            turned_weights(SB - 1)
            output_of(SB - 1)
            dve.sem_inc(phase_met, 1)

            dve.wait_ge(phase_met, 12)
            dve.wait_ge(S["m0_loaded"], 16)
            V1(dve.memset(m0[:, 0:TP], 0.0))
            V1(dve.tensor_copy(m0[:, TP:NT].rearrange("h (b t) -> h b t", t=ST), wide(gr["w"][:, 0:SB], ST)))
            for q in range(4):
                low_h("out0", q)
            low_mix_rest("out0")
            post_norm(0)
            pre_norm(1, "odd")

            dve.wait_ge(S["gate_sums"], 1)
            V1(dve.tensor_scalar(gr["ig"][:, :], bank[2][0:H, 0:NT], bif[:, 0:1], None, ALU.add))
            V1(dve.tensor_scalar(gr["t1"][:, :], bank[3][0:H, 0:NT], bif[:, 1:2], None, ALU.add))
            V1(dve.scalar_tensor_tensor(out=gr["M"][:, :], in0=gr["t1"][:, :], scalar=-1.0, in1=gr["t1"][:, :], op0=ALU.mult, op1=ALU.max), S["gx"])
            dve.wait_ge(S["g_ln"], 1)
            V1(dve.scalar_tensor_tensor(out=gr["lf"][:, :], in0=gr["t1"][:, :], scalar=0.0, in1=gr["w"][:, :], op0=ALU.min, op1=ALU.subtract))
            V1(dve.tensor_tensor_scan(gr["b"][:, :], const("keep", H), gr["lf"][:, :], 0.0, ALU.mult, ALU.add))
            V1(dve.tensor_tensor(gr["c"][:, :], gr["ig"][:, :], gr["b"][:, :], ALU.subtract))
            V1(dve.tensor_tensor_scan(gr["M"][:, :], const("cut", H), gr["c"][:, :], 0.0, ALU.add, ALU.max))
            V1(dve.tensor_tensor(gr["M"][:, :], gr["M"][:, :], m0[:, :], ALU.max))
            V1(dve.tensor_tensor(gr["t1"][:, :], gr["b"][:, :], gr["M"][:, :], ALU.add))
            V1(dve.tensor_scalar(rows[:, 0:NT], gr["M"][:, :], -1.0, None, ALU.mult))
            V1(dve.tensor_scalar(rows[:, NT:2 * NT], gr["t1"][:, :], -1.0, None, ALU.mult))
            V1(dve.tensor_tensor(rows[:, 2 * NT:3 * NT], m0[:, :], gr["M"][:, :], ALU.subtract))
            V1(dve.tensor_scalar(gr["w"][:, 0:TP], gr["c"][:, 0:TP], gr["M"][:, TP - 1:TP], None, ALU.subtract))
            end = gr["M"][:, TP:NT].rearrange("h (b t) -> h b t", t=ST)[:, :, ST - 1]
            V1(dve.tensor_tensor(gr["w"][:, TP:NT].rearrange("h (b t) -> h b t", t=ST), gr["c"][:, TP:NT].rearrange("h (b t) -> h b t", t=ST),
                                 wide(end, ST), ALU.subtract), S["gl_ready"])
            dve.wait_ge(S["cw_turned"], 1)
            for k, t in enumerate((cT, wT)):
                V1(dve.tensor_copy(t[:, 0:2, :], bank[5][:, 24 * k:24 * k + 16].rearrange("p (a h) -> p a h", a=2)))
                V1(dve.tensor_copy(t[0:TS, 2, :], bank[5][0:TS, 24 * k + 16:24 * k + 24]))
            V1(dve.tensor_copy(nT[:, :, :].rearrange("p a n -> p (a n)"), bank[4][:, 0:128]), S["cw_read"])

            V1(dve.memset(oqm[:, :, :], 0.0))
            dve.wait_ge(stored, n_store[1])
            V1(dve.memset(hsq[:, :, :], 0.0))
            V1(dve.memset(hsum[:, :], 0.0))
            diag = oqm.rearrange("p d (b x) -> p d b x", x=TS + ST)[:, :, :, 0:ST]
            n_bh = nT.rearrange("p d (b h) -> p d b h", h=H)
            nn_bh = nnew.rearrange("p d (b h) -> p d b h", h=H)

            def add_squares(h):
                dve.wait_ge(S["hs_summed"], h + 1)
                V1(dve.tensor_tensor(hsum[:, :], hsum[:, :], bank[4][0:H, 0:NT], ALU.add), S["hs_read"])

            def weighted_keys(b):
                V1(dve.tensor_scalar(okm[b % 2], otks[:, :], wm[:, b:b + 1], None, ALU.mult), S["km_ready"])

            with VO.turns(0, H, lo_ready=20, hs_read=1, rm=1, wc_ready=1, e_in=1, kw_ready=1, w_ready=1, qi_ready=1, km_ready=SB, ws_ready=1, c_new=SB,
                          den_read=1, num_read=1, gate_done=1, dve_order=19) as h:
                def head(ap):
                    return ap[:, :, bass.ds(h, 1)]

                V1(dve.tensor_copy(csel[:, :], const("colsel")[:, bass.ds(h * H, H)]))
                V1(dve.tensor_scalar(rsel[:, :], ones[0:H, :], ident[0:H, bass.ds(h, 1)], None, ALU.mult), S["rm"])
                V1(dve.tensor_copy(wcol[:, :].unsqueeze(2), head(wT[:, 0:2, :])))
                V1(dve.tensor_scalar(wm[:, :], const("bsel", TS), wT[0:TS, 2, bass.ds(h, 1)], None, ALU.mult), S["wc_ready"])
                low("odd", h, 1)
                add_squares(h)
                low("odd", h, 2)
                dve.wait_ge(S["nm_bc"], h + 1)
                V1(dve.scalar_tensor_tensor(out=oe[:, 0:TP], in0=bank[6][:, 0:TP], scalar=cT[:, 0, bass.ds(h, 1)], in1=const("cneg")[:, 0:TP],
                                            op0=ALU.add, op1=ALU.add))
                V1(dve.scalar_tensor_tensor(out=oe[:, TP:384], in0=bank[6][:, P:TP], scalar=cT[:, 1, bass.ds(h, 1)], in1=const("cneg")[:, TP:384],
                                            op0=ALU.add, op1=ALU.add))
                V1(dve.scalar_tensor_tensor(out=oe[0:TS, 384:384 + TS], in0=bank[6][0:TS, TP:NT], scalar=cT[0:TS, 2, bass.ds(h, 1)], in1=const("sneg", TS),
                                            op0=ALU.add, op1=ALU.add), S["e_in"])
                dve.wait_ge(S["kt_r"], h + 1)
                for sc in range(2):
                    V1(dve.tensor_scalar(otk[:, sc, :], otk[:, sc, :], wcol[:, sc:sc + 1], None, ALU.mult), S["kw_ready"] if sc else None)
                low("odd", h, 3)
                dve.wait_ge(S["st"], h + 1)
                dve.wait_ge(S["e_exp"], h + 1)
                V1(dve.tensor_tensor(ow[:, 0:384], bank[7][:, 0:384], oe[:, 0:384], ALU.mult), S["w_ready"])
                dve.wait_ge(S["bc2_r"], h + 1)
                V1(dve.tensor_tensor(oqi[:, :, :], oz["q"][:, :, TP:NT], over(obc[:, NT:NT + TS], 2), ALU.mult))
                V1(dve.tensor_copy(diag, oqi.rearrange("p d (b t) -> p d b t", t=ST)))
                V1(dve.tensor_tensor(onq.rearrange("p d (b t) -> p d b t", t=ST), oqi.rearrange("p d (b t) -> p d b t", t=ST),
                                     n_bh[:, :, :, bass.ds(h, 1)].broadcast_to([P, 2, SB, ST]), ALU.mult), S["qi_ready"])
                low("odd", h, 4)
                dve.wait_ge(S["sst"], h + 1)
                V1(dve.tensor_tensor(ow[0:TS, 384:384 + TS], bank[7][0:TS, 0:TS], oe[0:TS, 384:384 + TS], ALU.mult), S["ws_ready"])
                dve.wait_ge(S["smp_r"], h + 1)
                for b in range(2):
                    weighted_keys(b)
                low("odd", h + 1, 0)
                carried = obc[:, NT:NT + TS].rearrange("p (b t) -> p b t", t=ST)[:, :, ST - 1]
                dve.wait_ge(S["den_ready"], h + 1)
                V1(dve.scalar_tensor_tensor(out=odd_[:, :], in0=bank[4][:, 0:NT], scalar=-1.0, in1=obc[:, 0:NT], op0=ALU.mult, op1=ALU.max))
                V1(dve.tensor_tensor(odd_[:, :], odd_[:, :], bank[4][:, 0:NT], ALU.max))
                new = nn_bh[:, :, :, bass.ds(h, 1)].rearrange("p d b h -> p d (b h)")
                V1(dve.tensor_tensor(new, n_bh[:, :, :, bass.ds(h, 1)].rearrange("p d b h -> p d (b h)"), over(carried, 2), ALU.mult))
                V1(dve.tensor_tensor(new, new, bank[4][:, 320:336].rearrange("p (d b) -> p d b", d=2), ALU.add))
                V1(dve.tensor_copy(head(nprm), bank[4][:, 336:338].unsqueeze(2)))
                for b in range(SB):
                    dve.wait_ge(S["outer"], h * SB + (b + 1))
                    V1(dve.scalar_tensor_tensor(out=cring[:, b, :], in0=cring[:, b, :], scalar=obc[:, NT + ST * b + ST - 1:NT + ST * b + ST], in1=bank[7][:, :],
                                                op0=ALU.mult, op1=ALU.add), S["c_new"])
                    if b + 2 < SB:
                        weighted_keys(b + 2)
                dve.wait_ge(proj_free, h * 10 + (2 * first["odd"] + 8 + PF))
                V1(dve.scalar_tensor_tensor(out=ort[:, :, :], in0=oz["eo"][:, :, :], scalar=1.0, in1=over(odd_[:, :], 2), op0=ALU.add, op1=ALU.mult), S["den_read"])
                V1(dve.reciprocal(ort[:, :, :], ort[:, :, :]))
                dve.wait_ge(S["num_ready"], h + 1)
                for vc in range(2):
                    V1(dve.tensor_tensor(yT[:, bass.ds(h * 2 + vc, 1), 0:TP].rearrange("p a t -> p (a t)"), bank[2 + vc][:, 0:TP], ort[:, vc, 0:TP], ALU.mult))
                V1(dve.tensor_tensor(yT[:, bass.ds(h * 2, 2), TP:NT], bank[3][:, DC:DC + 2 * TS].rearrange("p (a t) -> p a t", a=2), ort[:, :, TP:NT], ALU.mult),
                   S["num_read"])
                dve.wait_ge(proj_free, h * 10 + (2 * first["odd"] + 10 + PF))
                V1(dve.tensor_scalar(oz["eg"][:, :, :], oz["eg"][:, :, :], 1.0, None, ALU.add))
                V1(dve.reciprocal(oz["eg"][:, :, :], oz["eg"][:, :, :]))
                for mt in range(2):
                    V1(dve.scalar_tensor_tensor(out=oz["g"][:, mt, :], in0=oz["eg"][:, mt, :],
                                                scalar=hgain[:, bass.ds(h * 2 + mt, 1)], in1=oz["g"][:, mt, :], op0=ALU.mult, op1=ALU.mult))
                dve.wait_ge(S["hs_squared"], h + 2)
                y = yT[:, bass.ds(h * 2, 2), :]
                V1(dve.tensor_tensor(y, y, oz["g"][:, :, :], ALU.mult), S["gate_done"])

            add_squares(H)
            V1(dve.tensor_copy(rsel8[:, :, :], wide(ident[0:H, 0:H], P)), S["sel_ready"])
            for k in range(H):
                dve.wait_ge(S["hs_spread"], k + 1)
                y = yT[:, 2 * k:2 * k + 2, :]
                V1(dve.tensor_tensor(y, y, over(bank[5 + k % 2][:, 0:NT], 2), ALU.mult), S["hs_done"])
                if k % 2:
                    low_h("out1", k // 2)
            low_mix_rest("out1")
            post_norm(1)


def shape_constants():
    import numpy as np
    c = np.zeros((P, CW), np.float32)

    def put(name, a):
        lo, hi = CONST[name]
        c[0:a.shape[0], lo:hi] = a.reshape(a.shape[0], -1)

    p = np.arange(P)[:, None]
    s = np.arange(TP)[None, :]
    slopes = 2.0 ** (-8.0 * np.arange(1, H + 1) / H)
    put("ident", np.eye(P))
    put("dist", np.concatenate([np.where(s[:, :P] <= p, s[:, :P] - p, -BIG), np.where(s <= p + P, s - p - P, -BIG)], 1))
    put("slope", np.broadcast_to(slopes / SCALE, (P, H)))
    put("cneg", np.concatenate([np.where(s >= p, 0, -BIG), np.where(s[:, :P] >= p, 0, -BIG)], 1))
    r = np.arange(TS)
    hr, tr = r // ST, r % ST
    put("sbias", -slopes[hr][:, None] / SCALE * (PAST + tr[:, None] - np.arange(PAST)[None, :]))
    own = np.full((TS, SB, SB, ST), -BIG)
    for b in range(SB):
        for t in range(ST):
            own[tr >= t, b, b, t] = (-slopes[hr] / SCALE * (tr - t))[tr >= t]
    put("own", own.reshape(TS, -1))
    bt = r // ST
    put("sneg", np.where((bt[:, None] == bt[None, :]) & (tr[:, None] <= tr[None, :]), 0, -BIG))
    put("bsel", (bt[:, None] == np.arange(SB)[None, :]).astype(float))
    put("eps", np.full((P, 1), EPS))
    start = np.zeros(NT, bool)
    start[0] = True
    start[TP::ST] = True
    put("keep", np.broadcast_to(np.where(start, 0.0, 1.0), (H, NT)))
    put("cut", np.broadcast_to(np.where(start, -BIG, 0.0), (H, NT)))
    put("invcnt", np.broadcast_to(np.stack([1.0 / np.minimum(w, np.arange(16) + 1) for w in WINDOWS]).reshape(-1), (P, 64)))
    put("rank", np.broadcast_to(np.arange(1, NB + 1), (P, NB)))
    put("colsel", np.broadcast_to(np.eye(H + 1)[:, 1:].reshape(-1), (P, (H + 1) * H)))
    return c


IN_NAMES = ['x_prompt', 'x_sample', 'cache_k', 'cache_v', 'state_pool', 'state_C', 'state_n', 'state_m', 'page_table', 'c_prompt',
            'c_sample', 'ada_w', 'ada_b', 'norm_pre', 'norm_post', 'w_in_even', 'pool_w', 'pool_scale', 'w_out_even', 'w_in_odd',
            'b_igate', 'b_fgate', 'head_norm', 'w_out_odd']
OUT_SHAPES = [("y_prompt", (1, TP, D)), ("y_sample", (SB, ST, D)), ("k_prompt", (1, 1, TP, H, DH)), ("v_prompt", (1, 1, TP, H, DH)),
              ("k_sample", (1, SB, ST, H, DH)), ("v_sample", (1, SB, ST, H, DH)), ("pool_prompt", (1, 1, HIST, WA)),
              ("pool_sample", (1, SB, HIST, WA)), ("C_prompt", (1, 1, H, DC, DC)), ("n_prompt", (1, 1, H, DC)), ("m_prompt", (1, 1, H)),
              ("C_sample", (1, SB, H, DC, DC)), ("n_sample", (1, SB, H, DC)), ("m_sample", (1, SB, H))]


def kernel(**inputs):
    import numpy as np
    import concourse.bacc as bacc
    from concourse.bass_utils import run_bass_kernel_spmd

    nc = bacc.Bacc("TRN2", target_bir_lowering=False, num_devices=1)
    arrays = {name: np.ascontiguousarray(inputs[name]) for name in IN_NAMES}
    arrays["constants"] = shape_constants()
    ins = {name: nc.dram_tensor(name, a.shape, mybir.dt.from_np(a.dtype), kind="ExternalInput").ap() for name, a in arrays.items()}
    outs = {name: nc.dram_tensor("out_" + name, shape, F32, kind="ExternalOutput").ap() for name, shape in OUT_SHAPES}
    trunk_kernel(nc, ins, outs)
    r = run_bass_kernel_spmd(nc, [arrays], core_ids=[0])
    return tuple(r.results[0]["out_" + name] for name, _ in OUT_SHAPES)
```

```python
import math
from contextlib import ExitStack, contextmanager

import concourse.bass as bass
from concourse import mybir

F32 = mybir.dt.float32
F32R = mybir.dt.float32r
I32 = mybir.dt.int32
ALU = mybir.AluOpType
ACT = mybir.ActivationFunctionType
AX = mybir.AxisListType

P = 128
D = 2048
KC = D // P
TP, SB, ST = 256, 8, 4
TS = SB * ST
NT = TP + TS
NC = 1 + SB
H = 8
DH = 128
WA = H * DH
PAGES, PAGE = 8, 128
PAST = PAGES * PAGE
BLOCK = 256
NB = PAST // BLOCK
WINDOWS = (2, 4, 8, 16)
HIST = 15
GW = 256
DC = 256
EPS = 1e-6
BIG = 1e30
SCALE = DH ** -0.5
KSCALE = DC ** -0.5
KD, VD = 4, 4
PF = 4
N_SMALL = 8
SLOTS_FOR = dict(ada=(0, 1), even=(0, 1, 0, 1, 0, 1), out=(0, 1), odd=(0, 1, 0, 1, 0))
TRIPS = dict(ada=12, even=4, out=4, odd=8)
PHASES = (("ada0", "ada"), ("even", "even"), ("out0", "out"), ("ada1", "ada"), ("odd", "odd"), ("out1", "out"))
CONST = {}
_at = 0
for _n, _w in (("ident", P), ("dist", 384), ("slope", H), ("cneg", 384), ("sbias", PAST), ("own", SB * TS), ("sneg", TS),
               ("bsel", SB), ("eps", 1), ("keep", NT), ("cut", NT), ("invcnt", 64), ("rank", NB), ("colsel", 9 * H)):
    CONST[_n] = (_at, _at + _w)
    _at += _w
CW = _at


def slab_plan():
    first, slot, uses, before = {}, [], [], []
    last, count = {}, {}
    for name, kind in PHASES:
        first[name] = len(slot)
        for s in SLOTS_FOR[kind] * TRIPS[kind]:
            count[s] = count.get(s, 0) + 1
            slot.append(s)
            uses.append(count[s])
            before.append(last.get(s))
            last[s] = len(slot) - 1
    return first, slot, uses, before


class Count:

    def __init__(self, sem):
        self.sem, self.base, self.k, self.i, self.per = sem, 0, 0, None, 0

    def inc(self, ins):
        self.k += 1
        return ins.then_inc(self.sem, 1)

    def value(self):
        return self.base + self.k if self.i is None else self.i * self.per + (self.base + self.k)

    def enter(self, i, per):
        self.base, self.k, self.i, self.per = self.base + self.k, 0, i, per

    def leave(self, trips):
        assert self.k == self.per, f"{self.k} increments a turn, {self.per} said"
        self.base, self.k, self.i = self.base + trips * self.per, 0, None


def trunk_kernel(nc, A, OUT):
    first, slot, uses, before = slab_plan()
    ctx = ExitStack()
    with ctx:
        def sb(name, shape, dt=F32):
            return ctx.enter_context(nc.sbuf_tensor(name, shape, dt))

        def sem(name):
            return ctx.enter_context(nc.semaphore(name))

        wbuf = sb("wbuf", [P, 2, KC, GW])
        w_hi = sb("w_hi", [P, 4, 4, GW], F32R)
        w_lo = sb("w_lo", [P, 4, 4, GW], F32R)
        h_hi = sb("h_hi", [P, KC, NT], F32R)
        h_lo = sb("h_lo", [P, KC, NT], F32R)
        xT = sb("xT", [P, KC, NT])
        yT = sb("yT", [P, KC, NT])
        modT = sb("modT", [P, 2 * 48, NC])
        cst = sb("cst", [P, CW])
        ones = sb("ones", [P, P])
        prm = sb("prm", [P, 96 + 88])
        c_hi = sb("c_hi", [P, KC, NC], F32R)
        c_lo = sb("c_lo", [P, KC, NC], F32R)
        rstd = sb("rstd", [P, NT])
        bif = sb("bif", [H, 2])
        m0 = sb("m0", [H, NT])
        ptab = sb("ptab", [1, SB * PAGES], I32)
        arena_words = 13326
        arena = sb("arena", [P, arena_words])

        def const(name, rows=P):
            a, b = CONST[name]
            return cst[0:rows, a:b]

        ident = const("ident")
        eps = const("eps")
        adab = prm[:, 0:96]
        npre, npost = prm[:, 96:128], prm[:, 128:160]
        pscale, hgain = prm[:, 160:168], prm[:, 168:184]

        class Arena:

            def __init__(self):
                self.at = 0

            def take(self, rows, *dims):
                n = math.prod(dims)
                ap = arena[0:rows, self.at:self.at + n]
                self.at += n
                assert self.at <= arena_words, self.at
                if len(dims) == 2:
                    return ap.rearrange("p (a b) -> p a b", b=dims[1])
                if len(dims) == 3:
                    return ap.rearrange("p (a b c) -> p a b c", b=dims[1], c=dims[2])
                return ap

        bank = [ctx.enter_context(nc.psum_tensor(f"bank{i}", [P, 512], F32)) for i in range(4)]
        pair = [ctx.enter_context(nc.psum_tensor(f"pair{i}", [P, 1024], F32)) for i in range(2)]
        bank += [pair[0][:, 0:512], pair[0][:, 512:1024], pair[1][:, 0:512], pair[1][:, 512:1024]]
        proj = bank[0:2]

        w_loaded = [[sem(f"w_loaded{s}{half}") for half in "ab"] for s in range(2)]
        hi_ready = sem("hi_ready")
        lo_ready = sem("lo_ready")
        unit_used = sem("unit_used")
        h_hi_ready, h_lo_ready = sem("h_hi_ready"), sem("h_lo_ready")
        proj_ready = sem("proj_ready")
        proj_free = sem("proj_free")
        act_order, dve_order = sem("act_order"), sem("dve_order")
        phase_met = sem("phase_met")
        small_loaded = sem("small_loaded")
        ptab_loaded = sem("ptab_loaded")
        stored = sem("stored")
        block = ctx.enter_context(nc.Block())

        pe, act, dve, pool, sp = nc.tensor, nc.scalar, nc.vector, nc.gpsimd, nc.sync

        class Own:

            def __init__(self, eng, order):
                self.eng, self.order, self.counts, self.turn = eng, order, {}, None

            def count(self, s):
                if s.name not in self.counts:
                    self.counts[s.name] = Count(s)
                    if self.turn:
                        self.counts[s.name].enter(*self.turn_of(s.name))
                return self.counts[s.name]

            def turn_of(self, name):
                i, per = self.turn
                return i, per.get(name, 0)

            def credit(self, s, n):
                c = self.count(s)
                c.k += n
                self.eng.sem_inc(s, n)

            def link(self, ins, s=None):
                c = self.count(self.order if s is None else s)
                c.inc(ins)
                self.eng.wait_ge(c.sem, c.value())

            @contextmanager
            def turns(self, start, end, **per):
                with self.eng.Fori(start, end) as i:
                    self.turn = ((i - start) if start else i, per)
                    for name, c in self.counts.items():
                        c.enter(*self.turn_of(name))
                    yield i
                    did = {n: c.k for n, c in self.counts.items() if c.k}
                    assert did == per, f"a turn raises {did}"
                    for c in self.counts.values():
                        c.leave(end - start)
                    self.turn = None

        AO, VO = Own(act, act_order), Own(dve, dve_order)
        def apart(eng):
            eng.wait_ge(small_loaded, 16 * N_SMALL)

        n_store = [0]

        def store(out, in_, slow=False):
            n_store[0] += 1
            act.dma_start(out, in_, allow_slow_non_contiguous=slow).then_inc(stored, 16)

        S = {}

        def signals(*names):
            for n in names:
                S[n] = sem(n)

        signals("first_loaded", "x_loaded", "c_exp", "c_silu", "c_rounded", "c_turned", "c_read", "prm_turned", "x_turned", "x_read", "ones_set")
        signals("x_squared", "x_added", "x_summed", "x_rstd", "norm_done")
        norm = dict(pre0=0, post0=1, pre1=2, post1=3)
        signals("mod_turned")
        signals("ga_exp", "gb_exp", "scores", "x_max", "p_exp", "p_ready", "pt_turned",
                "pt_read", "ktok_turned", "ktok_read", "vtok_turned", "vtok_read", "att_out", "att_read")
        signals("hist_loaded", "hist_turned", "hist_read", "u_turned", "u_read", "d_ready", "pool_out", "pool_read", "pool_loaded")
        signals("qk_kept", "silu_gb", "gate_done", "cp_stored", "kt_turned", "kt_read", "s_scores", "s_read", "s_max", "s_exp", "s_ready", "s_turned", "s_pt", "s_out", "s_out_read", "qm_ready", "v_used", "s_rows", "s_rows_read", "v_high", "v_taken", "p_high")
        k_loaded = [sem(f"k_loaded{s}") for s in range(KD)]
        v_loaded = [sem(f"v_loaded{s}") for s in range(VD)]
        signals("gate_sums", "g_ln", "gl_ready", "rows_ready", "cw_turned", "cw_read", "wg_loaded", "sn_loaded",
                "m0_loaded", "gx")
        signals("rm", "nm_bc", "kt_t", "kt_r", "vt_t", "vt_r", "st", "e_in", "e_exp", "w_ready", "bc2", "bc2_r",
                "smp_t", "smp_r", "sst", "ws_ready", "kw_ready", "qi_ready", "km_ready", "wc_ready", "ct_t", "ct_r", "outer", "c_new", "num_ready", "ns_ready", "ns_read", "num_read", "den_ready", "den_read", "cp_ready", "cp_read",
                "hs_squared", "hs_summed", "hs_read", "hs_rstd", "hs_spread", "hs_done", "sel_ready", "n_turned")
        c_loaded = [sem(f"c_loaded{s}") for s in range(8)]
        c_stored = [sem(f"c_stored{s}") for s in range(8)]
        signals("y_turned", "y_read")

        def wview(w):
            return w.rearrange("(kc p) n -> p kc n", p=P)

        w_ada = [wview(A["ada_w"][l, :, :]) for l in range(2)]
        w_even = wview(A["w_in_even"][0, :, :])
        w_out = [wview(A["w_out_even"][0, :, :]), wview(A["w_out_odd"][0, :, :])]
        w_odd = wview(A["w_in_odd"][0, :, :])
        kpage = A["cache_k"][0].rearrange("g t h d -> t g (h d)")
        vpage = A["cache_v"][0].rearrange("g t h d -> t g (h d)")
        stateC = A["state_C"][0].rearrange("b h (v p) d -> p b h v d", p=P)
        outC = OUT["C_sample"][0].rearrange("b h (v p) d -> p b h v d", p=P)

        EVEN_COL = [j * WA for j in range(6)]
        ODD_COL = [0, D, 2 * D, 3 * D, 4 * D]

        ar = Arena()
        xin = ar.take(P, 2, D)
        xsin = ar.take(TS, D)
        rows_at = ar.at
        mod_rows = [ar.take(NC, 3 * D)]
        prow = ar.take(P, 2, P)
        ar.at = rows_at
        cin = ar.take(NC, D)
        cexp = ar.take(P, KC * NC)
        scT = ar.take(P, KC * NC)
        mod_at = SB * 2 * DC + 2 * NT
        ar.at = mod_at
        mod_rows.append(ar.take(NC, 3 * D))
        early_at = ar.at
        ar.at = mod_at
        sq = ar.take(P, KC, NT)

        ar = Arena()
        qTs = ar.take(P, H, TS)
        kTs = ar.take(P, H, TS)
        gas = ar.take(P, H, TS)
        vtok_s = ar.take(TS, WA)
        sample_at = ar.at
        gbs = ar.take(P, 8, NT)
        even_common = ar.at
        ktok_s = ar.take(TS, WA)
        zq = ar.take(P, 2, NT)
        zk = ar.take(P, 2, NT)
        zv = ar.take(P, 2, NT)
        zga = ar.take(P, 2, NT)
        ega = ar.take(P, 2, NT)
        egb = ar.take(P, 2, NT)
        xs = [ar.take(P, 384) for _ in range(2)]
        pts = [ar.take(P, 384) for _ in range(2)]
        vtok = ar.take(P, 2, GW)
        ktok = ar.take(P, 2, GW)
        stat = ar.take(P, 4, 4)
        hist = ar.take(120, WA)
        ar.at = even_common + WA
        uext = [ar.take(P, 2, 16 + TP) for _ in range(2)]
        sext = ar.take(P, 8, SB * 19)
        swin = [ar.take(P, 2 * SB, 19) for _ in range(2)]
        dT = ar.take(P, 2, NT)
        pw = ar.take(P, 8, GW)
        utok = ar.take(HIST, WA)
        ustok = ar.take(TS, WA)
        ar.at = sample_at
        kring = wbuf[:, 1, :, :].rearrange("p k n -> p (k n)").rearrange("p (a b) -> p a b", a=KD)
        vring = ar.take(P, VD, WA)
        v_hi, v_lo = (t.rearrange("p a t -> p (a t)")[:, 0:KD * WA].rearrange("p (a b) -> p a b", a=KD) for t in (h_hi, h_lo))
        p_hi, p_lo = (t.rearrange("p a t -> p (a t)")[:, KD * WA:KD * WA + PAGES * TS] for t in (h_hi, h_lo))
        ktp = [ar.take(P, 2, 512) for _ in range(2)]
        qm = [ar.take(P, H * (TS + ST))]
        XW = PAST + TS
        sx = [ar.take(TS, XW)]
        pT = ar.take(P, 9 * TS)
        so = ar.take(TS, WA)
        sstat = ar.take(TS, 16)

        ar = Arena()
        cring = ar.take(P, 8, 2 * DC)
        oz = {n: ar.take(P, 2, NT) for n in ("k", "q", "eo", "g", "eg")}
        ozv = ar.take(P, 2, NT)
        otk = ar.take(P, 2, DC)
        otv = ar.take(P, 2, DC)
        otks = ar.take(TS, DC)
        otvs = ar.take(TS, DC)
        okm = [ar.take(TS, DC) for _ in range(2)]
        oct_ = [ar.take(P, 2, DC) for _ in range(2)]
        e_at = ar.at
        oe = ar.take(P, 384 + TS)
        obc = ar.take(P, NT + TS)
        odd_ = obc[:, 0:NT]
        oqi = ar.take(P, 2, TS)
        oqm = ar.take(P, 2, SB * (TS + ST))
        onq = ar.take(P, 2, TS)
        rows = ar.take(H, 2 * NT + TS)
        rsel = ar.take(H, P)
        csel = ar.take(P, H)
        cT = ar.take(P, 3, H)
        wT = ar.take(P, 3, H)
        wcol = ar.take(P, 2)
        wm = ar.take(TS, SB)
        nT = ar.take(P, 2, SB * H)
        nnew = ar.take(P, 2, SB * H)
        nprm = ar.take(P, 2, H)
        ow = oe
        ort = oz["eo"]
        hsq = oz["eo"]
        ocp = oct_[0].rearrange("p a n -> p (a n)")
        ons = otks
        hsum = m0
        ar.at = early_at
        wg = ar.take(P, KC, 2 * H)
        snin = ar.take(SB * H, DC)
        gr = {"w": ar.take(H, NT)}
        ar.at = mod_at
        gr.update({n: ar.take(H, NT) for n in ("ig", "lf", "t1", "b", "c", "M")})
        ar.at = e_at
        rsel8 = ar.take(H, H, P)
        nout = ar.take(SB * H, 2, P)
        npout = ar.take(H, 2, P)

        KINDS = dict(PHASES)
        kind_of = [kind for _, kind in PHASES for _ in range(len(SLOTS_FOR[kind]) * TRIPS[kind])]
        in_phase = {name: k for k, name in enumerate(("even", "out0", "odd", "out1"))}

        def quarter(phase, i, j, q):
            return i * (4 * len(SLOTS_FOR[KINDS[phase]])) + (4 * (first[phase] + j) + q + 1)

        def load_slab(n, src, turns=0):
            for half in range(2):
                b = before[n]
                if b is not None:
                    sp.wait_ge(lo_ready, turns * (4 * len(SLOTS_FOR[kind_of[b]])) + (4 * b + 2 * (half + 1)))
                sp.dma_start(wbuf[:, slot[n], 8 * half:8 * half + 8, :], src[:, 8 * half:8 * half + 8, :]).then_inc(w_loaded[slot[n]][half], 16)

        def load_first(name, source):
            for j in range(len(SLOTS_FOR[KINDS[name]])):
                load_slab(first[name] + j, source(0, j))

        def load_rest(name, source):
            per = len(SLOTS_FOR[KINDS[name]])
            with sp.Fori(1, TRIPS[KINDS[name]]) as i:
                for j in range(per):
                    load_slab(first[name] + per + j, source(i, j), i - 1)

        def load_phase(name, source):
            load_first(name, source)
            load_rest(name, source)

        def cols(view, start):
            return view[:, :, bass.ds(start, GW)]

        def load_odd():
            base, per = first["odd"], 5
            for j in range(per):
                load_slab(base + j, cols(w_odd, ODD_COL[j]))
                if j == 2:
                    sp.wait_ge(phase_met, 12)
                    for b in range(SB):
                        sp.dma_start(cring[:, b, :].rearrange("p (v d) -> p v d", v=2), stateC[:, b, 0, :, :]).then_inc(c_loaded[b], 16)
            with sp.Fori(1, H) as h:
                for j in range(per):
                    load_slab(base + per + j, cols(w_odd, h * GW + ODD_COL[j]), h - 1)
                    if j == 3:
                        for b in range(SB):
                            sp.wait_ge(c_stored[b], h * 16)
                            sp.dma_start(cring[:, b, :].rearrange("p (v d) -> p v d", v=2),
                                         stateC[:, b, bass.ds(h, 1), :, :].rearrange("p h v d -> p (h v) d")).then_inc(c_loaded[b], 16)

        @block.sync
        def _(eng):
            sp.wait_ge(S["first_loaded"], 48)
            load_phase("ada0", lambda i, j: cols(w_ada[0], i * (2 * GW) + j * GW))
            load_phase("even", lambda i, j: cols(w_even, i * GW + EVEN_COL[j]))
            out0_source = lambda i, j: cols(w_out[0], i * (2 * GW) + j * GW)
            load_slab(first["out0"], out0_source(0, 0))
            sp.wait_ge(lo_ready, 4 * first["out0"])
            sp.wait_ge(ptab_loaded, 16)

            def load_pages(b, ring, depth, cache, loaded, freed, per_page, first_turn):
                for j in range(PAGES):
                    if not (first_turn and j < depth):
                        sp.wait_ge(freed, b * (PAGES * per_page) + (j + 1 - depth) * per_page)
                    page = sp.value_load(ptab[0:1, bass.ds(b * PAGES + j, 1)], min_val=0, max_val=79)
                    sp.dma_start(ring[:, j % depth, :], cache[:, bass.ds(page, 1), :].rearrange("t g x -> t (g x)"))\
                      .then_inc(loaded[j % depth], 16)

            load_pages(0, kring, KD, kpage, k_loaded, S["kt_turned"], 2, True)
            load_pages(1, kring, KD, kpage, k_loaded, S["kt_turned"], 2, False)
            sp.wait_ge(phase_met, 9)
            load_pages(0, vring, VD, vpage, v_loaded, S["v_taken"], 1, True)
            with sp.Fori(2, SB) as b:
                load_pages(b, kring, KD, kpage, k_loaded, S["kt_turned"], 2, False)
                load_pages(b - 1, vring, VD, vpage, v_loaded, S["v_taken"], 1, False)
            load_pages(SB - 1, vring, VD, vpage, v_loaded, S["v_taken"], 1, False)
            sp.wait_ge(S["kt_turned"], 2 * PAGES * SB)
            load_slab(first["out0"] + 1, out0_source(0, 1))
            load_rest("out0", out0_source)
            load_phase("ada1", lambda i, j: cols(w_ada[1], i * (2 * GW) + j * GW))
            load_odd()
            load_phase("out1", lambda i, j: cols(w_out[1], i * (2 * GW) + j * GW))

        @block.gpsimd
        def _(eng):
            with pool.Fori(0, H) as h:
                for b in range(SB):
                    pool.wait_ge(S["c_new"], h * SB + (b + 1))
                    pool.dma_start(outC[:, b, bass.ds(h, 1), :, :].rearrange("p h v d -> p (h v) d"),
                                   cring[:, b, :].rearrange("p (v d) -> p v d", v=2)).then_inc(c_stored[b], 16)
            for b in range(SB):
                pool.wait_ge(c_stored[b], 16 * H)

        def slab_count(n0, i, per_phase, j):
            return i * per_phase + (n0 + j)

        def turn(out, in_, rows, width):
            return pe.transpose(out, in_, ident[0:rows, 0:rows])

        @block.tensor
        def _(eng):
            def product(phase, i, j):
                per, n = len(SLOTS_FOR[KINDS[phase]]), first[phase] + j
                for q in range(4):
                    pe.wait_ge(h_lo_ready, 4 * in_phase[phase] + q + 1)
                    pe.wait_ge(lo_ready, quarter(phase, i, j, q))
                    for mt in range(2):
                        if q == 0:
                            pe.wait_ge(proj_free, i * (2 * per) + (2 * n + mt + PF - 1))
                        cols_ = slice(mt * P, (mt + 1) * P)
                        for c in range(4):
                            for k, (w, h) in enumerate(((w_hi, h_hi), (w_hi, h_lo), (w_lo, h_hi))):
                                last = pe.matmul(proj[mt][:, 0:NT], w[:, q, c, cols_], h[:, 4 * q + c, :], start=q + c + k == 0, stop=q + c == 6 and k == 2)
                        if q == 3:
                            last.then_inc(proj_ready, 1)
                    if q < 3:
                        last.then_inc(unit_used, 1)

            def product_c(phase, i, j):
                n = first[phase] + j
                pe.wait_ge(proj_free, i * 4 + (2 * n + PF - 2))
                for q in range(4):
                    pe.wait_ge(lo_ready, quarter(phase, i, j, q))
                    for c in range(4):
                        for k, (w, x) in enumerate(((w_hi, c_hi), (w_lo, c_hi), (w_hi, c_lo))):
                            last = pe.matmul(proj[j][0:NC, 0:GW], x[:, 4 * q + c, :], w[:, q, c, :], start=q + c + k == 0, stop=q + c == 6 and k == 2)
                    if q < 3:
                        last.then_inc(unit_used, 1)
                last.then_inc(proj_ready, 2)

            def turn_mod(l, chunks, turns):
                pe.wait_ge(proj_free, 2 * (first[f"ada{l}"] + 2 * turns) + PF)
                for c in chunks:
                    last = turn(bank[2][:, c * NC:(c + 1) * NC], mod_rows[l][:, c * P:(c + 1) * P], NC, P)
                last.then_inc(S["mod_turned"], 1)

            def wait_read(phase, i, j):
                pe.wait_ge(proj_free, i * (2 * len(SLOTS_FOR[KINDS[phase]])) + (2 * (first[phase] + j) + 2 + PF))

            def sum_squares(key, t):
                for q in range(4):
                    pe.wait_ge(S["x_added"], 4 * norm[key] + q + 1)
                    last = pe.matmul(bank[4][:, 0:NT], ones[:, :], t[:, 4 * q, :], start=q == 0, stop=q == 3)
                last.then_inc(S["x_summed"], 1)

            def meet(own_last, value):
                pe.wait_ge(own_last, value)
                pe.sem_inc(phase_met, 1)

            pe.wait_ge(S["first_loaded"], 48)
            for c in range(KC):
                last = turn(bank[2][:, c * NC:(c + 1) * NC], cin[:, c * P:(c + 1) * P], NC, P)
            last.then_inc(S["c_turned"], 1)
            pe.wait_ge(S["c_read"], 1)
            with pe.Fori(0, TRIPS["ada"] // 2) as i:
                for j in range(2):
                    product_c("ada0", i, j)
            pe.wait_ge(S["x_loaded"], 32)
            pe.wait_ge(small_loaded, 16 * N_SMALL)
            turn(bank[5][:, 0:96], prow[0:96, 0, :], 96, P)
            turn(bank[5][:, 96:184], prow[0:88, 1, :], 88, P).then_inc(S["prm_turned"], 1)
            for c in range(KC):
                if c >= 2:
                    pe.wait_ge(S["x_read"], c - 1)
                b = bank[6 + c % 2]
                turn(b[:, 0:P], xin[:, 0, c * P:(c + 1) * P], P, P)
                turn(b[:, P:2 * P], xin[:, 1, c * P:(c + 1) * P], P, P)
                turn(b[:, TP:NT], xsin[:, c * P:(c + 1) * P], TS, P).then_inc(S["x_turned"], 1)
            pe.wait_ge(S["ones_set"], 1)
            with pe.Fori(TRIPS["ada"] // 2, TRIPS["ada"] - 2) as i:
                for j in range(2):
                    product_c("ada0", i, j)
            sum_squares("pre0", yT)
            turn_mod(0, range(40), TRIPS["ada"] - 2)
            with pe.Fori(TRIPS["ada"] - 2, TRIPS["ada"]) as i:
                for j in range(2):
                    product_c("ada0", i, j)

            turn_mod(0, range(40, 48), TRIPS["ada"])
            meet(S["mod_turned"], 2)

            pe.wait_ge(phase_met, 3)
            with pe.Fori(0, TRIPS["even"]) as g:
                product("even", g, 0)
                product("even", g, 1)
                product("even", g, 2)
                wait_read("even", g, 1)
                pe.wait_ge(S["att_read"], g + 1)
                for hh in range(2):
                    pe.matmul(bank[2 + hh][:, 0:P], zq[:, hh, 0:P], zk[:, hh, 0:P], start=True, stop=True)
                    pe.matmul(bank[2 + hh][:, P:384], zq[:, hh, P:TP], zk[:, hh, 0:TP], start=True, stop=True)\
                      .then_inc(S["scores"], 1)
                for z, turned in ((zk, "ktok_turned"), (zv, "vtok_turned")):
                    if z is zv:
                        product("even", g, 3)
                        pe.wait_ge(S["ktok_read"], g + 1)
                    for hh in range(2):
                        for tc in range(2):
                            turn(bank[4][:, tc * GW + hh * P:tc * GW + (hh + 1) * P], z[:, hh, tc * P:(tc + 1) * P], P, P)
                        last = turn(bank[5][0:TS, hh * P:(hh + 1) * P], z[:, hh, TP:NT], P, TS)
                    last.then_inc(S[turned], 1)
                product("even", g, 4)
                for hh in range(2):
                    pe.wait_ge(S["p_ready"], g * 2 + (hh + 1))
                    for k in range(3):
                        last = turn(bank[6 + hh][:, k * P:(k + 1) * P], xs[hh][:, k * P:(k + 1) * P], P, P)
                    last.then_inc(S["pt_turned"], 1)
                product("even", g, 5)
                pe.wait_ge(S["vtok_read"], g + 1)
                for hh in range(2):
                    pe.wait_ge(S["pt_read"], g * 2 + (hh + 1))
                    v = vtok[:, :, hh * P:(hh + 1) * P]
                    pe.matmul(bank[2][:, hh * TP:(hh + 1) * TP], v[:, 0, :], pts[hh][:, 0:TP], start=True, stop=True)
                    last = pe.matmul(bank[2][:, hh * TP + P:(hh + 1) * TP], v[:, 1, :], pts[hh][:, TP:384], start=False, stop=True,
                                     skip_group_check=True)
                last.then_inc(S["att_out"], 1)
            meet(S["att_out"], TRIPS["even"])

            for c in range(8):
                turn(pair[0][0:HIST, c * P:(c + 1) * P], yT[:, 8 + c, TP - HIST:TP], P, HIST)
                last = turn(pair[1][0:TS, c * P:(c + 1) * P], yT[:, 8 + c, TP:NT], P, TS)
            last.then_inc(S["u_turned"], 1)
            pe.wait_ge(S["att_read"], TRIPS["even"] + 1)
            pe.wait_ge(S["hist_loaded"], 16)
            for c in range(8):
                b = bank[2 + c // 4]
                last = turn(b[:, (c % 4) * 120:(c % 4 + 1) * 120], hist[:, c * P:(c + 1) * P], 120, P)
            last.then_inc(S["hist_turned"], 1)
            pe.wait_ge(S["pool_loaded"], 16)
            for g in range(4):
                pe.wait_ge(S["d_ready"], g + 1)
                if g == 0:
                    pe.wait_ge(S["hist_read"], 2)
                if g == 1:
                    pe.wait_ge(S["u_read"], 1)
                if g >= 2:
                    pe.wait_ge(S["pool_read"], 2 * (g - 1))
                for mt in range(2):
                    for cc in range(2):
                        last = pe.matmul(bank[2 + 2 * (g % 2) + mt][:, 0:NT], pw[:, 2 * g + cc, mt * P:(mt + 1) * P], dT[:, cc, :],
                                         start=cc == 0, stop=cc == 1)
                last.then_inc(S["pool_out"], 1)
            meet(S["pool_out"], 4)

            pe.wait_ge(phase_met, 9)

            def turn_page(b, j):
                pe.wait_ge(k_loaded[j % KD], b * (16 * PAGES // KD) + 16 * (j // KD + 1))
                for hh in range(2):
                    pe.wait_ge(S["kt_read"], b * (2 * PAGES) + (2 * j + hh + 1))
                    for h in range(4):
                        last = turn(bank[hh][:, h * P:(h + 1) * P], kring[:, j % KD, (4 * hh + h) * P:(4 * hh + h + 1) * P], P, P)
                    last.then_inc(S["kt_turned"], 1)

            def sample_scores(b):
                turn_page(b, 0)
                pe.wait_ge(S["qm_ready"], b + 1)
                pe.wait_ge(S["s_read"], b + 1)
                for j in range(PAGES):
                    if j + 1 < PAGES:
                        turn_page(b, j + 1)
                    for h in range(H):
                        if h % 4 == 0:
                            pe.wait_ge(S["kt_read"], b * (2 * PAGES) + (2 * j + h // 4 + 3))
                        pe.matmul(pair[0][0:TS, j * PAGE:(j + 1) * PAGE], qm[0][:, h * TS:(h + 1) * TS],
                                  ktp[j % 2][:, h // 4, (h % 4) * P:(h % 4 + 1) * P], start=h == 0, stop=h == H - 1)
                for h in range(H):
                    last = pe.matmul(bank[2][0:TS, 0:TS], qm[0][:, h * TS:(h + 1) * TS], kTs[:, h, :], start=h == 0, stop=h == H - 1)
                last.then_inc(S["s_scores"], 1)

            def sample_values(b):
                apart(pe)
                pe.wait_ge(S["s_ready"], b + 1)
                pe.wait_ge(S["s_out_read"], b + 1)
                for j in range(PAGES):
                    turn(bank[3][:, j * TS:(j + 1) * TS], sx[0][:, j * PAGE:(j + 1) * PAGE], TS, P)
                turn(bank[3][0:TS, PAGES * TS:(PAGES + 1) * TS], sx[0][:, PAST:XW], TS, TS).then_inc(S["s_turned"], 1)
                pe.wait_ge(S["s_pt"], b + 1)
                for j in range(PAGES):
                    pe.wait_ge(S["v_taken"], b * PAGES + (j + 1))
                    for k, (p, v) in enumerate(((p_hi, v_hi), (p_hi, v_lo), (p_lo, v_hi))):
                        for half in range(2):
                            last = pe.matmul(pair[1][0:TS, half * 512:(half + 1) * 512], p[:, j * TS:(j + 1) * TS],
                                             v[:, j % VD, half * 512:(half + 1) * 512], start=j + k == 0, stop=False)
                    last.then_inc(S["v_used"], 1)
                for half in range(2):
                    last = pe.matmul(pair[1][0:TS, half * 512:(half + 1) * 512], pT[0:TS, PAGES * TS:(PAGES + 1) * TS],
                                     vtok_s[:, half * 512:(half + 1) * 512], start=False, stop=True)
                last.then_inc(S["s_rows"], 1)
                apart(pe)
                pe.wait_ge(S["s_rows_read"], b + 1)
                for h in range(H):
                    last = turn(bank[3][:, h * TS:(h + 1) * TS], so[:, h * P:(h + 1) * P], TS, P)
                last.then_inc(S["s_out"], 1)

            sample_scores(0)
            with pe.Fori(1, SB) as b:
                sample_scores(b)
                sample_values(b - 1)
            sample_values(SB - 1)
            meet(S["s_out"], SB)

            pe.wait_ge(phase_met, 12)
            with pe.Fori(0, TRIPS["out"]) as i:
                for j in range(2):
                    product("out0", i, j)
            sum_squares("post0", sq)
            pe.wait_ge(proj_free, 2 * first["ada1"] + PF)
            with pe.Fori(0, TRIPS["ada"] // 2) as i:
                for j in range(2):
                    product_c("ada1", i, j)
            with pe.Fori(TRIPS["ada"] // 2, TRIPS["ada"] - 2) as i:
                for j in range(2):
                    product_c("ada1", i, j)
            sum_squares("pre1", yT)
            turn_mod(1, range(40), TRIPS["ada"] - 2)
            with pe.Fori(TRIPS["ada"] - 2, TRIPS["ada"]) as i:
                for j in range(2):
                    product_c("ada1", i, j)
            turn_mod(1, range(40, 48), TRIPS["ada"])

            pe.wait_ge(S["wg_loaded"], 16)
            pe.wait_ge(S["sn_loaded"], 16)
            for dc in range(2):
                last = turn(bank[4][:, dc * 64:(dc + 1) * 64], snin[:, dc * P:(dc + 1) * P], 64, P)
            last
            for kc in range(KC):
                if kc % 4 == 0:
                    pe.wait_ge(S["norm_done"], 4 * norm["pre1"] + kc // 4 + 1)
                for k in range(2):
                    last = pe.matmul(bank[2 + k][0:H, 0:NT], wg[:, kc, k * H:(k + 1) * H], yT[:, kc, :], start=kc == 0, stop=kc == KC - 1)
            last.then_inc(S["gate_sums"], 1)
            product("odd", 0, 0)
            pe.wait_ge(S["rows_ready"], 1)
            for k, r in enumerate((gr["c"], gr["w"])):
                for s in range(3):
                    n = P if s < 2 else TS
                    last = turn(bank[5][0:n, 24 * k + 8 * s:24 * k + 8 * s + 8], r[:, s * P:s * P + n], H, n)
            last.then_inc(S["cw_turned"], 1)
            pe.wait_ge(S["cw_read"], 1)

            def head(h):
                pe.wait_ge(S["rm"], h + 1)
                pe.wait_ge(S["hs_squared"], h + 1)
                for vc in range(2):
                    last = pe.matmul(bank[4][0:H, 0:NT], csel[:, :], hsq[:, vc, :], start=vc == 0, stop=vc == 1)
                last.then_inc(S["hs_summed"], 1)
                product("odd", h, 1)
                wait_read("odd", h, 1)
                for tc in range(2):
                    for dc in range(2):
                        last = turn(bank[5][:, tc * DC + dc * P:tc * DC + (dc + 1) * P], oz["k"][:, dc, tc * P:(tc + 1) * P], P, P)
                last.then_inc(S["kt_t"], 1)
                pe.matmul(bank[6][:, 0:NT], rsel[:, :], rows[:, 0:NT], start=True, stop=True).then_inc(S["nm_bc"], 1)
                product("odd", h, 2)
                pe.wait_ge(S["cp_read"], h + 1)
                for dc in range(2):
                    pe.matmul(bank[7][:, 0:TP], oz["k"][:, dc, 0:P], oz["q"][:, dc, 0:TP], start=dc == 0, stop=dc == 1)
                for dc in range(2):
                    last = pe.matmul(bank[7][:, TP:384], oz["k"][:, dc, P:TP], oz["q"][:, dc, P:TP], start=dc == 0, stop=dc == 1)
                last.then_inc(S["st"], 1)
                pe.wait_ge(S["kt_r"], h + 1)
                wait_read("odd", h, 2)
                for tc in range(2):
                    for dc in range(2):
                        last = turn(bank[5][:, tc * DC + dc * P:tc * DC + (dc + 1) * P], ozv[:, dc, tc * P:(tc + 1) * P], P, P)
                last.then_inc(S["vt_t"], 1)
                pe.wait_ge(S["e_in"], h + 1)
                pe.matmul(bank[6][:, 0:NT], rsel[:, :], rows[:, NT:2 * NT], start=True, stop=True)
                pe.matmul(bank[6][:, NT:NT + TS], rsel[:, :], rows[:, 2 * NT:2 * NT + TS], start=True, stop=True).then_inc(S["bc2"], 1)
                product("odd", h, 3)
                pe.wait_ge(S["vt_r"], h + 1)
                for k, z in enumerate((oz["k"], ozv)):
                    for dc in range(2):
                        last = turn(bank[5][0:TS, k * DC + dc * P:k * DC + (dc + 1) * P], z[:, dc, TP:NT], P, TS)
                last.then_inc(S["smp_t"], 1)
                pe.wait_ge(S["w_ready"], h + 1)
                pe.wait_ge(S["num_read"], h + 1)
                for vc in range(2):
                    pe.matmul(bank[2 + vc][:, 0:TP], otv[:, 0, vc * P:(vc + 1) * P], ow[:, 0:TP], start=True, stop=True)
                    pe.matmul(bank[2 + vc][:, P:TP], otv[:, 1, vc * P:(vc + 1) * P], ow[:, TP:384], start=False, stop=True, skip_group_check=True)
                for dc in range(2):
                    last = pe.matmul(bank[7][0:TS, 0:TS], oz["k"][:, dc, TP:NT], oz["q"][:, dc, TP:NT], start=dc == 0, stop=dc == 1)
                last.then_inc(S["sst"], 1)
                product("odd", h, 4)
                apart(pe)
                pe.wait_ge(S["smp_r"], h + 1)
                pe.wait_ge(S["ws_ready"], h + 1)
                pe.matmul(bank[2][0:TS, DC:2 * DC], ow[0:TS, 384:384 + TS], otvs[:, :], start=True, stop=False)
                pe.wait_ge(S["den_read"], h + 1)
                pe.wait_ge(S["hs_read"], h + 1)
                pe.wait_ge(S["wc_ready"], h + 1)
                pe.wait_ge(S["kw_ready"], h + 1)
                pe.wait_ge(S["qi_ready"], h + 1)
                pe.matmul(bank[4][:, 0:TP], ones[:, :], ow[:, 0:TP], start=True, stop=True)
                pe.matmul(bank[4][:, P:TP], ones[:, :], ow[:, TP:384], start=False, stop=True, skip_group_check=True)
                pe.matmul(bank[4][:, TP:NT], ones[0:TS, :], ow[0:TS, 384:384 + TS], start=True, stop=False)
                for dc in range(2):
                    pe.matmul(bank[4][:, TP:NT], ones[:, :], onq[:, dc, :], start=False, stop=dc == 1)
                for dc in range(2):
                    pe.matmul(bank[4][:, 320 + SB * dc:320 + SB * (dc + 1)], otks[:, dc * P:(dc + 1) * P], wm[:, :], start=True, stop=True)
                for dc in range(2):
                    for sc in range(2):
                        last = pe.matmul(bank[4][:, 336 + dc:337 + dc], otk[:, sc, dc * P:(dc + 1) * P], ones[:, 0:1], start=sc == 0, stop=sc == 1)
                last.then_inc(S["den_ready"], 1)
                pe.wait_ge(S["bc2_r"], h + 1)

                def turn_state(b):
                    pe.wait_ge(c_loaded[b], h * 16 + 16)
                    for dc in range(2):
                        for vc in range(2):
                            last = turn(bank[5 + b % 2][:, dc * DC + vc * P:dc * DC + (vc + 1) * P],
                                        cring[:, b, vc * DC + dc * P:vc * DC + (dc + 1) * P], P, P)
                    last.then_inc(S["ct_t"], 1)

                turn_state(0)
                for b in range(SB):
                    if b + 1 < SB:
                        turn_state(b + 1)
                    if b:
                        pe.wait_ge(S["c_new"], h * SB + b)
                    pe.wait_ge(S["km_ready"], h * SB + (b + 1))
                    for vc in range(2):
                        last = pe.matmul(bank[7][:, vc * DC:(vc + 1) * DC], otvs[:, vc * P:(vc + 1) * P], okm[b % 2], start=True, stop=True)
                    last.then_inc(S["outer"], 1)
                    pe.wait_ge(S["ct_r"], h * SB + (b + 1))
                    for dc in range(2):
                        last = pe.matmul(bank[2][0:TS, DC:2 * DC], oqm[:, dc, b * TS:(b + 1) * TS], oct_[b % 2][:, dc, :],
                                         start=False, stop=b == SB - 1 and dc == 1)
                last.then_inc(S["ns_ready"], 1)
                pe.wait_ge(S["c_new"], h * SB + SB)
                for vc in range(2):
                    for sc in range(2):
                        last = pe.matmul(bank[7][:, vc * DC:(vc + 1) * DC], otv[:, sc, vc * P:(vc + 1) * P], otk[:, sc, :], start=sc == 0, stop=sc == 1)
                last.then_inc(S["cp_ready"], 1)
                apart(pe)
                pe.wait_ge(S["ns_read"], h + 1)
                for vc in range(2):
                    last = turn(bank[3][:, DC + vc * TS:DC + (vc + 1) * TS], ons[:, vc * P:(vc + 1) * P], TS, P)
                last.then_inc(S["num_ready"], 1)

            with pe.Fori(0, H - 1) as h:
                head(h)
                product("odd", h + 1, 0)
            head(H - 1)

            pe.wait_ge(S["hs_squared"], H + 1)
            for vc in range(2):
                last = pe.matmul(bank[4][0:H, 0:NT], const("colsel")[:, H * H:(H + 1) * H], hsq[:, vc, :], start=vc == 0, stop=vc == 1)
            last.then_inc(S["hs_summed"], 1)
            pe.wait_ge(S["sel_ready"], 1)
            for k in range(H):
                pe.wait_ge(S["hs_rstd"], 1)
                if k >= 2:
                    pe.wait_ge(S["hs_done"], k - 1)
                pe.matmul(bank[5 + k % 2][:, 0:NT], rsel8[:, k, :], hsum[:, :], start=True, stop=True).then_inc(S["hs_spread"], 1)
            for dc in range(2):
                turn(bank[4][0:64, dc * P:(dc + 1) * P], nnew[:, dc, :], P, 64)
                last = turn(bank[2][0:H, dc * P:(dc + 1) * P], nprm[:, dc, :], P, H)
            last.then_inc(S["n_turned"], 1)

            with pe.Fori(0, TRIPS["out"]) as i:
                for j in range(2):
                    product("out1", i, j)
            sum_squares("post1", sq)

            for k in range(12):
                f, tc = k // 3, k % 3
                rows_ = P if tc < 2 else TS
                pe.wait_ge(S["norm_done"], 4 * norm["post1"] + f + 1)
                if k >= 2:
                    pe.wait_ge(S["y_read"], k - 1)
                for c in range(4):
                    last = turn(bank[5 + k % 2][0:rows_, c * P:(c + 1) * P], xT[:, 4 * f + c, tc * P:tc * P + rows_], P, rows_)
                last.then_inc(S["y_turned"], 1)

        @block.scalar
        def _(eng):
            A1 = AO.link

            def high(phase, i, j, quarters):
                n = first[phase] + j
                s = slot[n]
                for q in quarters:
                    act.wait_ge(w_loaded[s][q // 2], i * (16 * SLOTS_FOR[KINDS[phase]].count(s)) + 16 * uses[n])
                    per = len(SLOTS_FOR[KINDS[phase]])
                    if q < 3:
                        act.wait_ge(unit_used, i * (3 * per) + (3 * n + q + 1))
                    elif n:
                        act.wait_ge(proj_ready, i * (2 * per) + 2 * n)
                    A1(act.activation(w_hi[:, q, :, :], wbuf[:, s, 4 * q:4 * q + 4, :], ACT.Copy), hi_ready)

            def evacuate(phase, i, j, outs, more=True):
                per, n = len(SLOTS_FOR[KINDS[phase]]), first[phase] + j
                nxt = (i, j + 1) if j + 1 < per else (i + 1, 0)
                if more:
                    high(phase, *nxt, range(3))
                for mt in range(2):
                    act.wait_ge(proj_ready, i * (2 * per) + (2 * n + mt + 1))
                    outs(mt, proj[mt])
                if more:
                    high(phase, *nxt, range(3, 4))

            def high_h(phase, ready=None):
                for q in range(4):
                    if ready:
                        ready(q)
                    A1(act.activation(h_hi[:, 4 * q:4 * q + 4, :], yT[:, 4 * q:4 * q + 4, :], ACT.Copy), h_hi_ready)

            def squares(key, src, dst):
                for q in range(4):
                    A1(act.activation(dst[:, 4 * q:4 * q + 4, :], src[:, 4 * q:4 * q + 4, :], ACT.Square), S["x_squared"])

            def root(key, summed, n):
                act.wait_ge(S["x_summed"], norm[key] + 1)
                A1(act.activation(rstd[:, :], summed, ACT.Ln, bias=eps, scale=1.0 / n))
                A1(act.activation(rstd[:, :], rstd[:, :], ACT.Exp, scale=-0.5), S["x_rstd"])

            act.dma_start(cin[0:1, :], A["c_prompt"]).then_inc(S["first_loaded"], 16)
            act.dma_start(cin[1:NC, :], A["c_sample"]).then_inc(S["first_loaded"], 16)
            act.dma_start(cst[:, 0:P], A["constants"][:, 0:P]).then_inc(S["first_loaded"], 16)
            act.dma_start(cst[:, P:CW], A["constants"][:, P:CW]).then_inc(small_loaded, 16)
            act.dma_start(prow[0:96, 0, :], A["ada_b"].rearrange("l (c p) -> (l c) p", p=P)).then_inc(small_loaded, 16)
            act.dma_start(prow[0:32, 1, :], A["norm_pre"].rearrange("l (c p) -> (l c) p", p=P)).then_inc(small_loaded, 16)
            act.dma_start(prow[32:64, 1, :], A["norm_post"].rearrange("l (c p) -> (l c) p", p=P)).then_inc(small_loaded, 16)
            act.dma_start(prow[64:72, 1, :], A["pool_scale"].rearrange("l (c p) -> (l c) p", p=P)).then_inc(small_loaded, 16)
            act.dma_start(prow[72:88, 1, :], A["head_norm"].rearrange("l (c p) -> (l c) p", p=P)).then_inc(small_loaded, 16)
            act.dma_start(bif[:, 0:1], A["b_igate"].rearrange("a h -> h a")).then_inc(small_loaded, 16)
            act.dma_start(bif[:, 1:2], A["b_fgate"].rearrange("a h -> h a")).then_inc(small_loaded, 16)
            act.dma_start(xin[:, :, :], A["x_prompt"][0].rearrange("(c p) d -> p c d", p=P)).then_inc(S["x_loaded"], 16)
            act.dma_start(xsin[:, :], A["x_sample"].rearrange("b t d -> (b t) d")).then_inc(S["x_loaded"], 16)
            act.dma_start(ptab[:, :], A["page_table"].rearrange("b (g a) -> a (b g)", a=1)).then_inc(ptab_loaded, 16)
            for s, n in ((proj_free, PF), (S["kt_read"], 2), (S["cp_read"], 1), (S["hs_squared"], 1)):
                AO.credit(s, n)
            act.sem_inc(unit_used, 3)
            act.sem_inc(S["v_used"], VD)
            act.wait_ge(S["c_turned"], 1)
            A1(act.activation(cexp[:, :], bank[2][:, 0:KC * NC], ACT.Exp, scale=-1.0), S["c_exp"])
            act.wait_ge(S["c_silu"], 1)
            A1(act.activation(c_hi[:, :, :].rearrange("p a n -> p (a n)"), scT[:, :], ACT.Copy), S["c_rounded"])
            high("ada0", 0, 0, range(4))
            act.wait_ge(small_loaded, 16 * N_SMALL)

            def read_mod(phase, layer, i, j):
                evacuate(phase, i, j, lambda mt, b: A1(act.activation(
                    mod_rows[layer][:, bass.ds(i * (4 * P) + (2 * j + mt) * P, P)], proj[j][0:NC, mt * P:(mt + 1) * P], ACT.Copy), proj_free))

            half = TRIPS["ada"] // 2
            with AO.turns(0, half, proj_free=4, hi_ready=8) as i:
                for j in range(2):
                    read_mod("ada0", 0, i, j)
            act.wait_ge(S["x_read"], KC)
            squares("pre0", xT, yT)
            with AO.turns(half, TRIPS["ada"] - 2, proj_free=4, hi_ready=8) as i:
                for j in range(2):
                    read_mod("ada0", 0, i, j)
            root("pre0", bank[4][:, 0:NT], D)
            with AO.turns(TRIPS["ada"] - 2, TRIPS["ada"], proj_free=4, hi_ready=8) as i:
                for j in range(2):
                    read_mod("ada0", 0, i, j)
            act.sem_inc(phase_met, 1)
            high_h("even", lambda q: act.wait_ge(S["norm_done"], 4 * norm["pre0"] + q + 1))

            act.wait_ge(phase_met, 3)
            act.dma_start(hist[:, :], A["state_pool"][0].rearrange("b j c -> (b j) c")).then_inc(S["hist_loaded"], 16)

            def into(z):
                return lambda mt, b: A1(act.activation(z[:, mt, :], b[:, 0:NT], ACT.Copy), proj_free)

            kout = OUT["k_prompt"][0, 0].rearrange("(c p) h d -> p c (h d)", p=P)
            vout = OUT["v_prompt"][0, 0].rearrange("(c p) h d -> p c (h d)", p=P)
            with AO.turns(0, TRIPS["even"], hi_ready=24, proj_free=12, ktok_read=1, vtok_read=1, ga_exp=1, gb_exp=1, p_exp=2, pt_read=2, act_order=8) as g:
                act.wait_ge(S["qk_kept"], g + 1)
                evacuate("even", g, 0, into(zq))
                evacuate("even", g, 1, into(zk))
                evacuate("even", g, 2, into(zv))

                def tokens(tok, tok_s, turned, read, out):
                    act.wait_ge(S[turned], g + 1)
                    act.wait_ge(stored, g * 32 + (16 if tok is ktok else 32))
                    A1(act.activation(tok[:, :, :].rearrange("p a n -> p (a n)"), bank[4][:, :], ACT.Copy))
                    A1(act.activation(tok_s[:, bass.ds(g * GW, GW)], bank[5][0:TS, 0:GW], ACT.Copy), S[read])
                    act.dma_start(out[:, :, bass.ds(g * GW, GW)], tok[:, :, :]).then_inc(stored, 16)

                tokens(ktok, ktok_s, "ktok_turned", "ktok_read", kout)
                act.wait_ge(S["att_read"], g + 1)

                def gate_a(mt, b):
                    A1(act.activation(zga[:, mt, :], b[:, 0:NT], ACT.Copy))
                    A1(act.activation(ega[:, mt, :], b[:, 0:NT], ACT.Exp, scale=-1.0), proj_free)

                evacuate("even", g, 3, gate_a)
                act.sem_inc(S["ga_exp"], 1)
                AO.count(S["ga_exp"]).k += 1
                for hh in range(2):
                    act.wait_ge(S["x_max"], g * 2 + (hh + 1))
                    for c, (a, b) in enumerate(((0, P), (P, 384))):
                        A1(act.activation(xs[hh][:, a:b], xs[hh][:, a:b], ACT.Exp, bias=stat[:, 2 * hh + c, 1:2], scale=SCALE,
                                          accum_out=stat[:, 2 * hh + c, 2:3]), S["p_exp"] if c else None)
                tokens(vtok, vtok_s, "vtok_turned", "vtok_read", vout)
                evacuate("even", g, 4, lambda mt, b: A1(act.activation(
                    yT[:, bass.ds(g * 2 + (8 + mt), 1), :].rearrange("p a t -> p (a t)"), b[:, 0:NT], ACT.Copy), proj_free))
                for hh in range(2):
                    act.wait_ge(S["pt_turned"], g * 2 + (hh + 1))
                    A1(act.activation(pts[hh][:, :], bank[6 + hh][:, 0:384], ACT.Copy), S["pt_read"])
                act.wait_ge(S["silu_gb"], g + 1)

                def gate_b(mt, b):
                    A1(act.activation(gbs[:, bass.ds(g * 2 + mt, 1), :].rearrange("p a t -> p (a t)"), b[:, 0:NT], ACT.Copy))
                    A1(act.activation(egb[:, mt, :], b[:, 0:NT], ACT.Exp, scale=-1.0), proj_free)

                evacuate("even", g, 5, gate_b)
                act.sem_inc(S["gb_exp"], 1)
                AO.count(S["gb_exp"]).k += 1
            even_stored = 16 * 2 * TRIPS["even"] + 16
            act.wait_ge(stored, even_stored)
            for name, tok in (("k_sample", ktok_s), ("v_sample", vtok_s)):
                store(OUT[name][0].rearrange("b t h d -> (b t) (h d)"), tok[:, :])
            act.sem_inc(phase_met, 1)

            act.wait_ge(phase_met, 6)
            act.wait_ge(stored, even_stored + 32)
            act.dma_start(pw[:, :, :], A["pool_w"][0].rearrange("g (c p) d -> p (g c) d", p=P)).then_inc(S["pool_loaded"], 16)
            store(OUT["pool_sample"][0][:, 0:HIST - ST, :], A["state_pool"][0][:, ST:HIST, :])
            act.wait_ge(S["u_turned"], 1)
            act.wait_ge(S["hist_turned"], 1)
            A1(act.activation(utok[:, :], pair[0][0:HIST, :], ACT.Copy))
            A1(act.activation(ustok[:, :], pair[1][0:TS, :], ACT.Copy), S["u_read"])
            store(OUT["pool_prompt"][0, 0], utok[:, :])
            for b in range(SB):
                store(OUT["pool_sample"][0][b, HIST - ST:HIST, :], ustok[b * ST:(b + 1) * ST, :])
            act.wait_ge(stored, even_stored + 32 + 16 * (2 + SB))
            act.sem_inc(phase_met, 1)

            act.wait_ge(phase_met, 9)
            def halves(b, behind={}):
                for j in range(PAGES):
                    for hh in range(2):
                        act.wait_ge(S["kt_turned"], b * (2 * PAGES) + (2 * j + hh + 1))
                        A1(act.activation(ktp[j % 2][:, hh, :], bank[hh][:, :], ACT.Copy), S["kt_read"])
                    if j in behind:
                        behind[j]()

            def softmax(b):
                act.wait_ge(S["s_max"], b + 1)
                A1(act.activation(sx[0][:, :], sx[0][:, :], ACT.Exp, bias=sstat[:, 1:2], scale=SCALE, accum_out=sstat[:, 2:3]), S["s_exp"])

            def high_v(b, pages):
                for j in pages:
                    act.wait_ge(v_loaded[j % VD], b * (16 * PAGES // VD) + 16 * (j // VD + 1))
                    act.wait_ge(S["v_used"], b * PAGES + (j + 1))
                    A1(act.activation(v_hi[:, j % VD, :], vring[:, j % VD, :], ACT.Copy), S["v_high"])

            def high_p(b):
                act.wait_ge(S["s_turned"], b + 1)
                A1(act.activation(p_hi[:, :], bank[3][:, 0:PAGES * TS], ACT.Copy), S["p_high"])

            def values_out(b):
                act.wait_ge(S["s_rows"], b + 1)
                A1(act.activation(so[:, :], pair[1][0:TS, :], ACT.Copy), S["s_rows_read"])

            halves(0)
            with AO.turns(1, SB, kt_read=2 * PAGES, s_exp=1, s_rows_read=1, v_high=PAGES, p_high=1) as b:
                halves(b, {3: lambda: softmax(b - 1), 6: lambda: high_v(b - 1, [0]), 7: lambda: high_v(b - 1, [1, 2])})
                high_p(b - 1)
                high_v(b - 1, range(3, PAGES))
                values_out(b - 1)
            softmax(SB - 1)
            high_v(SB - 1, range(2))
            high_p(SB - 1)
            high_v(SB - 1, range(2, PAGES))
            values_out(SB - 1)
            act.sem_inc(phase_met, 1)

            act.wait_ge(phase_met, 12)
            act.dma_start(wg[:, :, :], w_odd[:, :, 5 * D:5 * D + 2 * H]).then_inc(S["wg_loaded"], 16)
            act.dma_start(snin[:, :], A["state_n"][0].rearrange("b h d -> (b h) d")).then_inc(S["sn_loaded"], 16)
            act.dma_start(gr["w"][:, 0:SB], A["state_m"][0].rearrange("b h -> h b"), allow_slow_non_contiguous=True).then_inc(S["m0_loaded"], 16)

            def read_mix(phase, last=False):
                def outs(i, j):
                    return lambda mt, b: A1(act.activation(yT[:, bass.ds(i * 4 + (2 * j + mt), 1), :].rearrange("p a t -> p (a t)"), b[:, 0:NT], ACT.Copy), proj_free)
                def squared(i):
                    c = bass.ds(i * 4, 4)
                    A1(act.activation(sq[:, c, :], yT[:, c, :], ACT.Square), S["x_squared"])

                with AO.turns(0, TRIPS["out"] - last, proj_free=4, hi_ready=8, x_squared=1) as i:
                    for j in range(2):
                        evacuate(phase, i, j, outs(i, j))
                    squared(i)
                if last:
                    i = TRIPS["out"] - 1
                    for j in range(2):
                        evacuate(phase, i, j, outs(i, j), more=j == 0)
                    squared(i)

            high_h("out0")
            read_mix("out0")
            root("post0", bank[4][:, 0:NT], D)
            with AO.turns(0, TRIPS["ada"] // 2, proj_free=4, hi_ready=8) as i:
                for j in range(2):
                    read_mod("ada1", 1, i, j)
            act.wait_ge(S["norm_done"], 4 * norm["post0"] + 4)
            squares("pre1", xT, yT)
            with AO.turns(TRIPS["ada"] // 2, TRIPS["ada"] - 2, proj_free=4, hi_ready=8) as i:
                for j in range(2):
                    read_mod("ada1", 1, i, j)
            root("pre1", bank[4][:, 0:NT], D)
            with AO.turns(TRIPS["ada"] - 2, TRIPS["ada"], proj_free=4, hi_ready=8) as i:
                for j in range(2):
                    read_mod("ada1", 1, i, j)
            high_h("odd", lambda q: act.wait_ge(S["norm_done"], 4 * norm["pre1"] + q + 1))

            act.wait_ge(S["gx"], 1)
            A1(act.activation(gr["w"][:, :], gr["M"][:, :], ACT.Exp, scale=-1.0))
            A1(act.activation(gr["w"][:, :], gr["w"][:, :], ACT.Ln, bias=1.0), S["g_ln"])
            act.wait_ge(S["gl_ready"], 1)
            A1(act.activation(rows[:, NT:2 * NT + TS], rows[:, NT:2 * NT + TS], ACT.Exp))
            A1(act.activation(gr["w"][:, :], gr["w"][:, :], ACT.Exp), S["rows_ready"])
            store(OUT["m_prompt"][0].rearrange("a h -> h a"), gr["t1"][:, TP - 1:TP])
            store(OUT["m_sample"][0].rearrange("b h -> h b"), gr["t1"][:, TP:NT].rearrange("h (b t) -> h b t", t=ST)[:, :, ST - 1], slow=True)
            act.wait_ge(stored, even_stored + 16 * n_store[0])
            n_store.append(even_stored + 16 * n_store[0])

            cp_stored = S["cp_stored"]
            with AO.turns(0, H, hi_ready=20, hs_squared=1, proj_free=10, kt_r=1, vt_r=1, e_exp=1, bc2_r=1, smp_r=1, ct_r=SB, ns_read=1, cp_read=1, act_order=4) as h:
                for j, z in enumerate((oz["q"], oz["k"])):
                    evacuate("odd", h, j, lambda mt, b: A1(act.activation(z[:, mt, :], b[:, 0:NT], ACT.Copy, scale=KSCALE if j else 1.0), proj_free))
                act.wait_ge(S["kt_t"], h + 1)
                A1(act.activation(otk[:, :, :].rearrange("p a n -> p (a n)"), bank[5][:, :], ACT.Copy), S["kt_r"])
                act.wait_ge(S["e_in"], h + 1)
                A1(act.activation(oe[:, 0:384], oe[:, 0:384], ACT.Exp))
                A1(act.activation(oe[0:TS, 384:384 + TS], oe[0:TS, 384:384 + TS], ACT.Exp), S["e_exp"])
                evacuate("odd", h, 2, into(ozv))
                act.wait_ge(S["vt_t"], h + 1)
                A1(act.activation(otv[:, :, :].rearrange("p a n -> p (a n)"), bank[5][:, :], ACT.Copy), S["vt_r"])
                act.wait_ge(S["bc2"], h + 1)
                act.wait_ge(S["den_read"], h + 1)
                A1(act.activation(obc[:, :], bank[6][:, 0:NT + TS], ACT.Copy), S["bc2_r"])
                act.wait_ge(S["num_read"], h + 1)
                evacuate("odd", h, 3, lambda mt, b: A1(act.activation(oz["eo"][:, mt, :], b[:, 0:NT], ACT.Exp, scale=-1.0), proj_free))
                act.wait_ge(S["smp_t"], h + 1)
                A1(act.activation(otks[:, :], bank[5][0:TS, 0:DC], ACT.Copy))
                A1(act.activation(otvs[:, :], bank[5][0:TS, DC:2 * DC], ACT.Copy), S["smp_r"])
                act.wait_ge(S["gate_done"], h + 1)

                def gate(mt, b):
                    A1(act.activation(oz["g"][:, mt, :], b[:, 0:NT], ACT.Copy))
                    A1(act.activation(oz["eg"][:, mt, :], b[:, 0:NT], ACT.Exp, scale=-1.0), proj_free)

                evacuate("odd", h, 4, gate)
                act.wait_ge(cp_stored, h * 16 + 16)
                for b in range(SB):
                    act.wait_ge(S["ct_t"], h * SB + (b + 1))
                    A1(act.activation(oct_[b % 2][:, :, :].rearrange("p a n -> p (a n)"), bank[5 + b % 2][:, :], ACT.Copy), S["ct_r"])
                act.wait_ge(S["ns_ready"], h + 1)
                A1(act.activation(ons[:, :], bank[2][0:TS, DC:2 * DC], ACT.Copy), S["ns_read"])
                act.wait_ge(S["cp_ready"], h + 1)
                A1(act.activation(ocp[:, :], bank[7][:, :], ACT.Copy), S["cp_read"])
                act.dma_start(OUT["C_prompt"][0, 0, bass.ds(h, 1), :, :].rearrange("h (v p) d -> p (h v) d", p=P),
                              ocp[:, :].rearrange("p (v d) -> p v d", v=2)).then_inc(cp_stored, 16)
                act.wait_ge(S["num_read"], h + 2)
                A1(act.activation(hsq[:, :, :], yT[:, bass.ds(h * 2, 2), :], ACT.Square), S["hs_squared"])

            act.wait_ge(S["hs_read"], H + 1)
            A1(act.activation(hsum[:, :], hsum[:, :], ACT.Ln, bias=eps[0:H, :], scale=1.0 / DC))
            A1(act.activation(hsum[:, :], hsum[:, :], ACT.Exp, scale=-0.5), S["hs_rstd"])
            high_h("out1", lambda q: act.wait_ge(S["hs_done"], 2 * q + 2))
            act.wait_ge(S["n_turned"], 1)
            A1(act.activation(nout[:, :, :].rearrange("p a n -> p (a n)"), bank[4][0:64, 0:DC], ACT.Copy))
            A1(act.activation(npout[:, :, :].rearrange("p a n -> p (a n)"), bank[2][0:H, 0:DC], ACT.Copy))
            store(OUT["n_sample"][0].rearrange("b h d -> (b h) d"), nout[:, :, :].rearrange("p a n -> p (a n)"))
            store(OUT["n_prompt"][0, 0], npout[:, :, :].rearrange("p a n -> p (a n)"))

            read_mix("out1", last=True)
            root("post1", bank[4][:, 0:NT], D)
            yout = [OUT["y_prompt"][0, 0:P, :], OUT["y_prompt"][0, P:TP, :], OUT["y_sample"].rearrange("b t d -> (b t) d")]
            for k in range(12):
                f, tc = k // 3, k % 3
                n = P if tc < 2 else TS
                if k < 9:
                    stage = sq.rearrange("p a t -> p (a t)")[0:n, k * 512:(k + 1) * 512]
                else:
                    stage = cring[0:n, k - 9, :]
                    act.wait_ge(c_stored[k - 9], 16 * H)
                act.wait_ge(S["y_turned"], k + 1)
                A1(act.activation(stage, bank[5 + k % 2][0:n, :], ACT.Copy), S["y_read"])
                store(yout[tc][:, f * 512:(f + 1) * 512], stage)
            act.wait_ge(stored, even_stored + 16 * n_store[0])
            act.wait_ge(cp_stored, 16 * H + 16)

        @block.vector
        def _(eng):
            V1 = VO.link

            def wide(ap, n):
                return ap.unsqueeze(2).broadcast_to([ap.shape[0], ap.shape[1], n])

            def over(ap, n):
                return ap.unsqueeze(1).broadcast_to([ap.shape[0], n, ap.shape[1]])

            def batches(t):
                return t[:, :, TP:NT].rearrange("p c (b t) -> p c b t", t=ST)

            def by_batch(m):
                return m[:, :, 1:NC].unsqueeze(3).broadcast_to([P, m.shape[1], SB, ST])

            def low(phase, i, j):
                s = slot[first[phase] + j]
                for q in range(4):
                    dve.wait_ge(hi_ready, quarter(phase, i, j, q))
                    V1(dve.tensor_tensor(w_lo[:, q, :, :], wbuf[:, s, 4 * q:4 * q + 4, :], w_hi[:, q, :, :].bitcast(F32), ALU.subtract), lo_ready)

            def low_h(phase, q):
                dve.wait_ge(h_hi_ready, 4 * in_phase[phase] + q + 1)
                c = slice(4 * q, 4 * q + 4)
                V1(dve.tensor_tensor(h_lo[:, c, :], yT[:, c, :], h_hi[:, c, :].bitcast(F32), ALU.subtract), h_lo_ready)

            def low_turns(phase, start, end):
                if end - start == 1:
                    low(phase, start, 1)
                    low(phase, end, 0)
                    return
                with VO.turns(start, end, lo_ready=8) as i:
                    low(phase, i, 1)
                    low(phase, i + 1, 0)

            def prepare(l):
                dve.wait_ge(S["mod_turned"], 2 * l + 2)
                m = modT[:, 48 * l:48 * (l + 1), :]
                V1(dve.tensor_tensor(m, bank[2][:, 0:48 * NC].rearrange("p (c n) -> p c n", n=NC), wide(adab[:, 48 * l:48 * (l + 1)], NC), ALU.add))
                V1(dve.scalar_tensor_tensor(out=m[:, 16:32, :], in0=m[:, 16:32, :], scalar=1.0, in1=wide(npre[:, 16 * l:16 * l + 16], NC),
                                            op0=ALU.add, op1=ALU.mult))
                V1(dve.tensor_tensor(m[:, 32:48, :], m[:, 32:48, :], wide(npost[:, 16 * l:16 * l + 16], NC), ALU.mult))

            def add_chunks(key, t, q, at=None):
                dve.wait_ge(S["x_squared"], q + (4 * norm[key] + 1))
                for n in (2, 1):
                    into = t[:, bass.ds(q * 4, n), :]
                    V1(dve.tensor_tensor(into, into, t[:, bass.ds(q * 4 + n, n), :], ALU.add), S["x_added"] if n == 1 else None)

            def mix_turns(phase, key, last=False):
                T = TRIPS["out"]
                low(phase, 0, 1)
                low(phase, 1, 0)
                with VO.turns(1, T - last, lo_ready=8, x_added=1, dve_order=1) as i:
                    low(phase, i, 1)
                    add_chunks(key, sq, i - 1)
                    low(phase, i + 1, 0)
                if last:
                    low(phase, T - 1, 1)
                    add_chunks(key, sq, T - 2)
                add_chunks(key, sq, T - 1)

            def scale(l):
                dve.wait_ge(S["x_rstd"], norm[f"pre{l}"] + 1)
                V1(dve.tensor_tensor(yT[:, :, :], xT[:, :, :], over(rstd[:, :], KC), ALU.mult))

            def pre_norm(l, phase):
                m = modT[:, 48 * l:48 * (l + 1), :]
                prepare(l)
                for q in range(4):
                    y = yT[:, 4 * q:4 * q + 4, :]
                    for c in range(4 * q, 4 * q + 4):
                        V1(dve.tensor_scalar(yT[:, c, 0:TP], yT[:, c, 0:TP], m[:, 16 + c, 0:1], m[:, c, 0:1], ALU.mult, ALU.add))
                    V1(dve.tensor_tensor(batches(y), batches(y), by_batch(m[:, 16 + 4 * q:20 + 4 * q, :]), ALU.mult))
                    V1(dve.tensor_tensor(batches(y), batches(y), by_batch(m[:, 4 * q:4 * q + 4, :]), ALU.add), S["norm_done"])
                    if q:
                        low_h(phase, q - 1)
                low_h(phase, 3)

            def post_norm(l, quarters=range(4)):
                m = modT[:, 48 * l:48 * (l + 1), :]
                dve.wait_ge(S["x_rstd"], norm[f"post{l}"] + 1)
                for q in quarters:
                    c4 = slice(4 * q, 4 * q + 4)
                    y, x = yT[:, c4, :], xT[:, c4, :]
                    V1(dve.tensor_tensor(y, y, over(rstd[:, :], 4), ALU.mult))
                    for c in range(4 * q, 4 * q + 4):
                        V1(dve.scalar_tensor_tensor(out=xT[:, c, 0:TP], in0=yT[:, c, 0:TP], scalar=m[:, 32 + c, 0:1], in1=xT[:, c, 0:TP],
                                                    op0=ALU.mult, op1=ALU.add))
                    V1(dve.tensor_tensor(batches(y), batches(y), by_batch(m[:, 32 + 4 * q:36 + 4 * q, :]), ALU.mult))
                    V1(dve.tensor_tensor(batches(x), batches(x), batches(y), ALU.add), S["norm_done"])

            for s, n in ((S["att_read"], 1), (S["qk_kept"], 1), (S["silu_gb"], 1), (S["s_read"], 1), (S["s_out_read"], 1),
                         (S["num_read"], 1), (S["den_read"], 1), (S["gate_done"], 1), (stored, 16), (S["cp_stored"], 16)):
                VO.credit(s, n)
            V1(dve.memset(ones[:, :], 1.0), S["ones_set"])
            dve.wait_ge(S["c_exp"], 1)
            V1(dve.tensor_scalar(cexp[:, :], cexp[:, :], 1.0, None, ALU.add))
            V1(dve.reciprocal(cexp[:, :], cexp[:, :]))
            V1(dve.tensor_tensor(scT[:, :], bank[2][:, 0:KC * NC], cexp[:, :], ALU.mult), S["c_silu"])
            dve.wait_ge(S["c_rounded"], 1)
            V1(dve.tensor_tensor(c_lo[:, :, :].rearrange("p a n -> p (a n)"), scT[:, :], c_hi[:, :, :].rearrange("p a n -> p (a n)").bitcast(F32),
                                 ALU.subtract), S["c_read"])
            low("ada0", 0, 0)
            low_turns("ada0", 0, TRIPS["ada"] // 2)
            dve.wait_ge(S["prm_turned"], 1)
            V1(dve.tensor_copy(prm[:, :], bank[5][:, 0:184]))
            for c in range(KC):
                dve.wait_ge(S["x_turned"], c + 1)
                V1(dve.tensor_copy(xT[:, c, :], bank[6 + c % 2][:, 0:NT]), S["x_read"])
            low_turns("ada0", TRIPS["ada"] // 2, TRIPS["ada"] - 3)
            for q in range(4):
                add_chunks("pre0", yT, q)
            low_turns("ada0", TRIPS["ada"] - 3, TRIPS["ada"] - 2)
            scale(0)
            low_turns("ada0", TRIPS["ada"] - 2, TRIPS["ada"])
            dve.sem_inc(phase_met, 1)
            pre_norm(0, "even")

            dve.wait_ge(phase_met, 3)
            with VO.turns(0, TRIPS["even"], lo_ready=24, qk_kept=1, x_max=2, p_ready=2, silu_gb=1, att_read=1, dve_order=17) as g:
                low("even", g, 1)
                low("even", g, 2)
                dve.wait_ge(proj_free, g * 12 + (2 * first["even"] + 4 + PF))
                V1(dve.tensor_copy(qTs[:, bass.ds(g * 2, 2), :], zq[:, :, TP:NT]))
                V1(dve.tensor_copy(kTs[:, bass.ds(g * 2, 2), :], zk[:, :, TP:NT]), S["qk_kept"])
                low("even", g, 3)
                for hh in range(2):
                    dve.wait_ge(S["scores"], g * 2 + (hh + 1))
                    V1(dve.scalar_tensor_tensor(out=xs[hh][:, :], in0=const("dist"), scalar=const("slope")[:, bass.ds(g * 2 + hh, 1)],
                                                in1=bank[2 + hh][:, 0:384], op0=ALU.mult, op1=ALU.add))
                    V1(dve.reduce_max(stat[:, 2 * hh, 0:1], xs[hh][:, 0:P], AX.X))
                    V1(dve.reduce_max(stat[:, 2 * hh + 1, 0:1], xs[hh][:, P:384], AX.X))
                    V1(dve.tensor_scalar(stat[:, 2 * hh:2 * hh + 2, 1], stat[:, 2 * hh:2 * hh + 2, 0], -SCALE, None, ALU.mult), S["x_max"])
                low("even", g, 4)
                dve.wait_ge(S["ga_exp"], g + 1)
                V1(dve.tensor_scalar(ega[:, :, :], ega[:, :, :], 1.0, None, ALU.add))
                V1(dve.reciprocal(ega[:, :, :], ega[:, :, :]))
                V1(dve.tensor_tensor(ega[:, :, :], ega[:, :, :], zga[:, :, :], ALU.mult))
                V1(dve.tensor_copy(gas[:, bass.ds(g * 2, 2), :], ega[:, :, TP:NT]))
                for hh in range(2):
                    dve.wait_ge(S["p_exp"], g * 2 + (hh + 1))
                    V1(dve.reciprocal(stat[:, 2 * hh:2 * hh + 2, 3], stat[:, 2 * hh:2 * hh + 2, 2]))
                    V1(dve.tensor_scalar(xs[hh][:, 0:P], xs[hh][:, 0:P], stat[:, 2 * hh, 3:4], None, ALU.mult))
                    V1(dve.tensor_scalar(xs[hh][:, P:384], xs[hh][:, P:384], stat[:, 2 * hh + 1, 3:4], None, ALU.mult), S["p_ready"])
                low("even", g, 5)
                low("even", g + 1, 0)
                dve.wait_ge(S["gb_exp"], g + 1)
                V1(dve.tensor_scalar(egb[:, :, :], egb[:, :, :], 1.0, None, ALU.add))
                V1(dve.reciprocal(egb[:, :, :], egb[:, :, :]))
                gb = gbs[:, bass.ds(g * 2, 2), :]
                V1(dve.tensor_tensor(gb, gb, egb[:, :, :], ALU.mult), S["silu_gb"])
                dve.wait_ge(S["att_out"], g + 1)
                V1(dve.tensor_tensor(yT[:, bass.ds(g * 2, 2), 0:TP], bank[2][:, :].rearrange("p (a t) -> p a t", a=2), ega[:, :, 0:TP], ALU.mult), S["att_read"])
            dve.sem_inc(phase_met, 1)

            dve.wait_ge(phase_met, 6)
            for t in uext:
                V1(dve.memset(t[:, :, 0:16], 0.0))
            sv = sext.rearrange("p c (b t) -> p c b t", t=19)
            def history():
                dve.wait_ge(S["hist_turned"], 1)
                for k in range(2):
                    V1(dve.tensor_copy(sv[:, 4 * k:4 * k + 4, :, 0:HIST], bank[2 + k][:, 0:480].rearrange("p (c b j) -> p c b j", c=4, b=SB)), S["hist_read"])
                V1(dve.tensor_copy(sv[:, :, :, HIST:19], yT[:, 8:16, TP:NT].rearrange("p c (b t) -> p c b t", t=ST)))

            def pool_read(g):
                dve.wait_ge(S["pool_out"], g + 1)
                for mt in range(2):
                    V1(dve.scalar_tensor_tensor(out=yT[:, 8 + 2 * g + mt, :], in0=bank[2 + 2 * (g % 2) + mt][:, 0:NT], scalar=pscale[:, 2 * g + mt:2 * g + mt + 1],
                                                in1=gbs[:, 2 * g + mt, :], op0=ALU.mult, op1=ALU.mult), S["pool_read"])

            for g, w in enumerate(WINDOWS):
                u = yT[:, 8 + 2 * g:10 + 2 * g, :]
                V1(dve.tensor_copy(uext[0][:, :, 16:], u[:, :, 0:TP]))
                se = sext[:, 2 * g:2 * g + 2, :].rearrange("p c (b t) -> p (c b) t", t=19)
                for k in range(g + 1):
                    d = 1 << k
                    a, b = uext[k % 2], uext[(k + 1) % 2]
                    V1(dve.tensor_tensor(b[:, :, 16:], a[:, :, 16:], a[:, :, 16 - d:16 + TP - d], ALU.add))
                if g == 0:
                    history()
                ssrc = se
                for k in range(g + 1):
                    d = 1 << k
                    lo = 2 * d - 1
                    V1(dve.tensor_tensor(swin[k % 2][:, :, lo:19], ssrc[:, :, lo:19], ssrc[:, :, lo - d:19 - d], ALU.add))
                    ssrc = swin[k % 2]
                win = uext[(g + 1) % 2]
                if g:
                    dve.wait_ge(S["pool_out"], g)
                V1(dve.scalar_tensor_tensor(out=dT[:, :, 0:TP], in0=win[:, :, 16:], scalar=1.0 / w, in1=u[:, :, 0:TP], op0=ALU.mult, op1=ALU.subtract))
                V1(dve.tensor_tensor(dT[:, :, 0:16], win[:, :, 16:32], over(const("invcnt")[:, 16 * g:16 * g + 16], 2), ALU.mult))
                V1(dve.tensor_tensor(dT[:, :, 0:16], dT[:, :, 0:16], u[:, :, 0:16], ALU.subtract))
                for cc in range(2):
                    V1(dve.scalar_tensor_tensor(out=dT[:, cc, TP:NT].rearrange("p (b t) -> p b t", t=ST), in0=ssrc[:, SB * cc:SB * (cc + 1), HIST:19],
                                                scalar=1.0 / w, in1=se[:, SB * cc:SB * (cc + 1), HIST:19], op0=ALU.mult, op1=ALU.subtract),
                       S["d_ready"] if cc else None)
                if g == 0:
                    dve.wait_ge(S["u_turned"], 1)
                else:
                    pool_read(g - 1)
            pool_read(3)
            dve.sem_inc(phase_met, 1)

            dve.wait_ge(phase_met, 9)
            V1(dve.memset(qm[0][:, 0:288], 0.0))
            heads_q = qm[0][:, 0:288].rearrange("p (h x) -> p h x", x=TS + ST)[:, :, 0:ST]
            x = sx[0]
            x4 = x[:, 0:PAST].rearrange("p (n k) -> p n k", n=NB)
            gates, least, rank, drop = sstat[:, 4:8], sstat[:, 8:9], sstat[:, 9:13], sstat[:, 13:14]

            def queries_of(b):
                V1(dve.tensor_copy(heads_q, qTs[:, :, bass.ds(b * ST, ST)]), S["qm_ready"])

            def scores_done(b):
                dve.wait_ge(S["s_scores"], b + 1)

            def weights_of(b):
                scores_done(b)
                V1(dve.tensor_tensor(x[:, 0:PAST], pair[0][0:TS, :], const("sbias", TS), ALU.add))
                V1(dve.tensor_tensor(x[:, PAST:XW], bank[2][0:TS, 0:TS], const("own", TS)[:, bass.ds(b * TS, TS)], ALU.add))
                V1(dve.tensor_reduce(gates, pair[0][0:TS, :].rearrange("p (n k) -> p n k", n=NB), AX.X, ALU.add), S["s_read"])
                V1(dve.tensor_reduce(least, gates, AX.X, ALU.min))
                V1(dve.scalar_tensor_tensor(out=rank, in0=gates, scalar=least, in1=const("rank", TS), op0=ALU.is_equal, op1=ALU.mult))
                V1(dve.reduce_max(drop, rank, AX.X))
                V1(dve.tensor_scalar(rank, const("rank", TS), drop, -BIG, ALU.is_equal, ALU.mult))
                V1(dve.tensor_tensor(x4, x4, wide(rank, BLOCK), ALU.add))
                V1(dve.reduce_max(sstat[:, 0:1], x, AX.X))
                V1(dve.tensor_scalar(sstat[:, 1:2], sstat[:, 0:1], -SCALE, None, ALU.mult), S["s_max"])

            def normalise(b):
                dve.wait_ge(S["s_exp"], b + 1)
                V1(dve.reciprocal(sstat[:, 3:4], sstat[:, 2:3]))
                V1(dve.tensor_scalar(x, x, sstat[:, 3:4], None, ALU.mult), S["s_ready"])

            def turned_weights(b):
                dve.wait_ge(S["s_turned"], b + 1)
                dve.wait_ge(S["p_high"], b + 1)
                V1(dve.tensor_tensor(p_lo[:, :], bank[3][:, 0:PAGES * TS], p_hi[:, :].bitcast(F32), ALU.subtract))
                V1(dve.tensor_copy(pT[0:TS, PAGES * TS:(PAGES + 1) * TS], bank[3][0:TS, PAGES * TS:(PAGES + 1) * TS]), S["s_pt"])

            def low_v(b, pages):
                for j in pages:
                    dve.wait_ge(S["v_high"], b * PAGES + (j + 1))
                    V1(dve.tensor_tensor(v_lo[:, j % VD, :], vring[:, j % VD, :], v_hi[:, j % VD, :].bitcast(F32), ALU.subtract), S["v_taken"])

            def output_of(b):
                dve.wait_ge(S["s_out"], b + 1)
                V1(dve.tensor_tensor(yT[:, 0:H, bass.ds(b * ST + TP, ST)], bank[3][:, 0:H * (TS + ST)].rearrange("p (h x) -> p h x", x=TS + ST)[:, :, 0:ST],
                                     gas[:, :, bass.ds(b * ST, ST)], ALU.mult), S["s_out_read"])

            queries_of(0)
            scores_done(0)
            queries_of(1)
            weights_of(0)
            normalise(0)
            with VO.turns(1, SB - 1, qm_ready=1, s_read=1, s_max=1, s_ready=1, s_pt=1, s_out_read=1, v_taken=PAGES, dve_order=10) as b:
                low_v(b - 1, range(2))
                turned_weights(b - 1)
                low_v(b - 1, range(2, PAGES))
                scores_done(b)
                queries_of(b + 1)
                weights_of(b)
                output_of(b - 1)
                normalise(b)
            low_v(SB - 2, range(2))
            turned_weights(SB - 2)
            low_v(SB - 2, range(2, PAGES))
            weights_of(SB - 1)
            output_of(SB - 2)
            normalise(SB - 1)
            low_v(SB - 1, range(2))
            turned_weights(SB - 1)
            low_v(SB - 1, range(2, PAGES))
            output_of(SB - 1)
            dve.sem_inc(phase_met, 1)

            dve.wait_ge(phase_met, 12)
            for q in range(4):
                low_h("out0", q)
            mix_turns("out0", "post0")
            V1(dve.memset(m0[:, 0:TP], 0.0))
            dve.wait_ge(S["m0_loaded"], 16)
            V1(dve.tensor_copy(m0[:, TP:NT].rearrange("h (b t) -> h b t", t=ST), wide(gr["w"][:, 0:SB], ST)))
            for q in range(4):
                low_turns("ada1", q, q + 1)
                post_norm(0, [q])
            low_turns("ada1", 4, TRIPS["ada"] - 4)
            for q in range(4):
                add_chunks("pre1", yT, q)
            low_turns("ada1", TRIPS["ada"] - 4, TRIPS["ada"] - 2)
            scale(1)
            low_turns("ada1", TRIPS["ada"] - 2, TRIPS["ada"])
            pre_norm(1, "odd")

            dve.wait_ge(S["gate_sums"], 1)
            V1(dve.tensor_scalar(gr["ig"][:, :], bank[2][0:H, 0:NT], bif[:, 0:1], None, ALU.add))
            V1(dve.tensor_scalar(gr["t1"][:, :], bank[3][0:H, 0:NT], bif[:, 1:2], None, ALU.add))
            V1(dve.scalar_tensor_tensor(out=gr["M"][:, :], in0=gr["t1"][:, :], scalar=-1.0, in1=gr["t1"][:, :], op0=ALU.mult, op1=ALU.max), S["gx"])
            dve.wait_ge(S["g_ln"], 1)
            V1(dve.scalar_tensor_tensor(out=gr["lf"][:, :], in0=gr["t1"][:, :], scalar=0.0, in1=gr["w"][:, :], op0=ALU.min, op1=ALU.subtract))
            V1(dve.tensor_tensor_scan(gr["b"][:, :], const("keep", H), gr["lf"][:, :], 0.0, ALU.mult, ALU.add))
            V1(dve.tensor_tensor(gr["c"][:, :], gr["ig"][:, :], gr["b"][:, :], ALU.subtract))
            V1(dve.tensor_tensor_scan(gr["M"][:, :], const("cut", H), gr["c"][:, :], 0.0, ALU.add, ALU.max))
            V1(dve.tensor_tensor(gr["M"][:, :], gr["M"][:, :], m0[:, :], ALU.max))
            V1(dve.tensor_tensor(gr["t1"][:, :], gr["b"][:, :], gr["M"][:, :], ALU.add))
            V1(dve.tensor_scalar(rows[:, 0:NT], gr["M"][:, :], -1.0, None, ALU.mult))
            V1(dve.tensor_scalar(rows[:, NT:2 * NT], gr["t1"][:, :], -1.0, None, ALU.mult))
            V1(dve.tensor_tensor(rows[:, 2 * NT:2 * NT + TS], m0[:, TP:NT], gr["M"][:, TP:NT], ALU.subtract))
            V1(dve.tensor_scalar(gr["w"][:, 0:TP], gr["c"][:, 0:TP], gr["M"][:, TP - 1:TP], None, ALU.subtract))
            end = gr["M"][:, TP:NT].rearrange("h (b t) -> h b t", t=ST)[:, :, ST - 1]
            V1(dve.tensor_tensor(gr["w"][:, TP:NT].rearrange("h (b t) -> h b t", t=ST), gr["c"][:, TP:NT].rearrange("h (b t) -> h b t", t=ST),
                                 wide(end, ST), ALU.subtract), S["gl_ready"])
            dve.wait_ge(S["cw_turned"], 1)
            for k, t in enumerate((cT, wT)):
                V1(dve.tensor_copy(t[:, 0:2, :], bank[5][:, 24 * k:24 * k + 16].rearrange("p (a h) -> p a h", a=2)))
                V1(dve.tensor_copy(t[0:TS, 2, :], bank[5][0:TS, 24 * k + 16:24 * k + 24]))
            V1(dve.tensor_copy(nT[:, :, :].rearrange("p a n -> p (a n)"), bank[4][:, 0:128]), S["cw_read"])

            V1(dve.memset(oqm[:, :, :], 0.0))
            dve.wait_ge(stored, n_store[1])
            V1(dve.memset(hsq[:, :, :], 0.0))
            V1(dve.memset(hsum[:, :], 0.0))
            diag = oqm.rearrange("p d (b x) -> p d b x", x=TS + ST)[:, :, :, 0:ST]
            n_bh = nT.rearrange("p d (b h) -> p d b h", h=H)
            nn_bh = nnew.rearrange("p d (b h) -> p d b h", h=H)

            def add_squares(h):
                dve.wait_ge(S["hs_summed"], h + 1)
                V1(dve.tensor_tensor(hsum[:, :], hsum[:, :], bank[4][0:H, 0:NT], ALU.add), S["hs_read"])

            def weighted_keys(b):
                V1(dve.tensor_scalar(okm[b % 2], otks[:, :], wm[:, b:b + 1], None, ALU.mult), S["km_ready"])

            with VO.turns(0, H, lo_ready=20, hs_read=1, rm=1, wc_ready=1, e_in=1, kw_ready=1, w_ready=1, qi_ready=1, km_ready=SB, ws_ready=1, c_new=SB,
                          den_read=1, num_read=1, gate_done=1, dve_order=19) as h:
                def head(ap):
                    return ap[:, :, bass.ds(h, 1)]

                V1(dve.tensor_copy(csel[:, :], const("colsel")[:, bass.ds(h * H, H)]))
                V1(dve.tensor_scalar(rsel[:, :], ones[0:H, :], ident[0:H, bass.ds(h, 1)], None, ALU.mult), S["rm"])
                V1(dve.tensor_copy(wcol[:, :].unsqueeze(2), head(wT[:, 0:2, :])))
                V1(dve.tensor_scalar(wm[:, :], const("bsel", TS), wT[0:TS, 2, bass.ds(h, 1)], None, ALU.mult), S["wc_ready"])
                low("odd", h, 1)
                add_squares(h)
                low("odd", h, 2)
                dve.wait_ge(S["nm_bc"], h + 1)
                V1(dve.scalar_tensor_tensor(out=oe[:, 0:TP], in0=bank[6][:, 0:TP], scalar=cT[:, 0, bass.ds(h, 1)], in1=const("cneg")[:, 0:TP],
                                            op0=ALU.add, op1=ALU.add))
                V1(dve.scalar_tensor_tensor(out=oe[:, TP:384], in0=bank[6][:, P:TP], scalar=cT[:, 1, bass.ds(h, 1)], in1=const("cneg")[:, TP:384],
                                            op0=ALU.add, op1=ALU.add))
                V1(dve.scalar_tensor_tensor(out=oe[0:TS, 384:384 + TS], in0=bank[6][0:TS, TP:NT], scalar=cT[0:TS, 2, bass.ds(h, 1)], in1=const("sneg", TS),
                                            op0=ALU.add, op1=ALU.add), S["e_in"])
                dve.wait_ge(S["kt_r"], h + 1)
                for sc in range(2):
                    V1(dve.tensor_scalar(otk[:, sc, :], otk[:, sc, :], wcol[:, sc:sc + 1], None, ALU.mult), S["kw_ready"] if sc else None)
                low("odd", h, 3)
                dve.wait_ge(S["st"], h + 1)
                dve.wait_ge(S["e_exp"], h + 1)
                V1(dve.tensor_tensor(ow[:, 0:384], bank[7][:, 0:384], oe[:, 0:384], ALU.mult), S["w_ready"])
                dve.wait_ge(S["bc2_r"], h + 1)
                V1(dve.tensor_tensor(oqi[:, :, :], oz["q"][:, :, TP:NT], over(obc[:, NT:NT + TS], 2), ALU.mult))
                V1(dve.tensor_copy(diag, oqi.rearrange("p d (b t) -> p d b t", t=ST)))
                V1(dve.tensor_tensor(onq.rearrange("p d (b t) -> p d b t", t=ST), oqi.rearrange("p d (b t) -> p d b t", t=ST),
                                     n_bh[:, :, :, bass.ds(h, 1)].broadcast_to([P, 2, SB, ST]), ALU.mult), S["qi_ready"])
                low("odd", h, 4)
                dve.wait_ge(S["sst"], h + 1)
                V1(dve.tensor_tensor(ow[0:TS, 384:384 + TS], bank[7][0:TS, 0:TS], oe[0:TS, 384:384 + TS], ALU.mult), S["ws_ready"])
                dve.wait_ge(S["smp_r"], h + 1)
                for b in range(2):
                    weighted_keys(b)
                low("odd", h + 1, 0)
                carried = obc[:, NT:NT + TS].rearrange("p (b t) -> p b t", t=ST)[:, :, ST - 1]
                dve.wait_ge(S["den_ready"], h + 1)
                V1(dve.scalar_tensor_tensor(out=odd_[:, :], in0=bank[4][:, 0:NT], scalar=-1.0, in1=obc[:, 0:NT], op0=ALU.mult, op1=ALU.max))
                V1(dve.tensor_tensor(odd_[:, :], odd_[:, :], bank[4][:, 0:NT], ALU.max))
                new = nn_bh[:, :, :, bass.ds(h, 1)].rearrange("p d b h -> p d (b h)")
                V1(dve.tensor_tensor(new, n_bh[:, :, :, bass.ds(h, 1)].rearrange("p d b h -> p d (b h)"), over(carried, 2), ALU.mult))
                V1(dve.tensor_tensor(new, new, bank[4][:, 320:336].rearrange("p (d b) -> p d b", d=2), ALU.add))
                V1(dve.tensor_copy(head(nprm), bank[4][:, 336:338].unsqueeze(2)))
                for b in range(SB):
                    dve.wait_ge(S["outer"], h * SB + (b + 1))
                    V1(dve.scalar_tensor_tensor(out=cring[:, b, :], in0=cring[:, b, :], scalar=obc[:, NT + ST * b + ST - 1:NT + ST * b + ST], in1=bank[7][:, :],
                                                op0=ALU.mult, op1=ALU.add), S["c_new"])
                    if b + 2 < SB:
                        weighted_keys(b + 2)
                dve.wait_ge(proj_free, h * 10 + (2 * first["odd"] + 8 + PF))
                V1(dve.scalar_tensor_tensor(out=ort[:, :, :], in0=oz["eo"][:, :, :], scalar=1.0, in1=over(odd_[:, :], 2), op0=ALU.add, op1=ALU.mult), S["den_read"])
                V1(dve.reciprocal(ort[:, :, :], ort[:, :, :]))
                dve.wait_ge(S["num_ready"], h + 1)
                for vc in range(2):
                    V1(dve.tensor_tensor(yT[:, bass.ds(h * 2 + vc, 1), 0:TP].rearrange("p a t -> p (a t)"), bank[2 + vc][:, 0:TP], ort[:, vc, 0:TP], ALU.mult))
                V1(dve.tensor_tensor(yT[:, bass.ds(h * 2, 2), TP:NT], bank[3][:, DC:DC + 2 * TS].rearrange("p (a t) -> p a t", a=2), ort[:, :, TP:NT], ALU.mult),
                   S["num_read"])
                dve.wait_ge(proj_free, h * 10 + (2 * first["odd"] + 10 + PF))
                V1(dve.tensor_scalar(oz["eg"][:, :, :], oz["eg"][:, :, :], 1.0, None, ALU.add))
                V1(dve.reciprocal(oz["eg"][:, :, :], oz["eg"][:, :, :]))
                for mt in range(2):
                    V1(dve.scalar_tensor_tensor(out=oz["g"][:, mt, :], in0=oz["eg"][:, mt, :],
                                                scalar=hgain[:, bass.ds(h * 2 + mt, 1)], in1=oz["g"][:, mt, :], op0=ALU.mult, op1=ALU.mult))
                dve.wait_ge(S["hs_squared"], h + 2)
                y = yT[:, bass.ds(h * 2, 2), :]
                V1(dve.tensor_tensor(y, y, oz["g"][:, :, :], ALU.mult), S["gate_done"])

            add_squares(H)
            V1(dve.tensor_copy(rsel8[:, :, :], wide(ident[0:H, 0:H], P)), S["sel_ready"])
            for k in range(H):
                dve.wait_ge(S["hs_spread"], k + 1)
                y = yT[:, 2 * k:2 * k + 2, :]
                V1(dve.tensor_tensor(y, y, over(bank[5 + k % 2][:, 0:NT], 2), ALU.mult), S["hs_done"])
                if k % 2:
                    low_h("out1", k // 2)
            mix_turns("out1", "post1", last=True)
            post_norm(1)


def shape_constants():
    import numpy as np
    c = np.zeros((P, CW), np.float32)

    def put(name, a):
        lo, hi = CONST[name]
        c[0:a.shape[0], lo:hi] = a.reshape(a.shape[0], -1)

    p = np.arange(P)[:, None]
    s = np.arange(TP)[None, :]
    slopes = 2.0 ** (-8.0 * np.arange(1, H + 1) / H)
    put("ident", np.eye(P))
    put("dist", np.concatenate([np.where(s[:, :P] <= p, s[:, :P] - p, -BIG), np.where(s <= p + P, s - p - P, -BIG)], 1))
    put("slope", np.broadcast_to(slopes / SCALE, (P, H)))
    put("cneg", np.concatenate([np.where(s >= p, 0, -BIG), np.where(s[:, :P] >= p, 0, -BIG)], 1))
    r = np.arange(TS)
    hr, tr = r // ST, r % ST
    put("sbias", -slopes[hr][:, None] / SCALE * (PAST + tr[:, None] - np.arange(PAST)[None, :]))
    own = np.full((TS, SB, SB, ST), -BIG)
    for b in range(SB):
        for t in range(ST):
            own[tr >= t, b, b, t] = (-slopes[hr] / SCALE * (tr - t))[tr >= t]
    put("own", own.reshape(TS, -1))
    bt = r // ST
    put("sneg", np.where((bt[:, None] == bt[None, :]) & (tr[:, None] <= tr[None, :]), 0, -BIG))
    put("bsel", (bt[:, None] == np.arange(SB)[None, :]).astype(float))
    put("eps", np.full((P, 1), EPS))
    start = np.zeros(NT, bool)
    start[0] = True
    start[TP::ST] = True
    put("keep", np.broadcast_to(np.where(start, 0.0, 1.0), (H, NT)))
    put("cut", np.broadcast_to(np.where(start, -BIG, 0.0), (H, NT)))
    put("invcnt", np.broadcast_to(np.stack([1.0 / np.minimum(w, np.arange(16) + 1) for w in WINDOWS]).reshape(-1), (P, 64)))
    put("rank", np.broadcast_to(np.arange(1, NB + 1), (P, NB)))
    put("colsel", np.broadcast_to(np.eye(H + 1)[:, 1:].reshape(-1), (P, (H + 1) * H)))
    return c


IN_NAMES = ['x_prompt', 'x_sample', 'cache_k', 'cache_v', 'state_pool', 'state_C', 'state_n', 'state_m', 'page_table', 'c_prompt',
            'c_sample', 'ada_w', 'ada_b', 'norm_pre', 'norm_post', 'w_in_even', 'pool_w', 'pool_scale', 'w_out_even', 'w_in_odd',
            'b_igate', 'b_fgate', 'head_norm', 'w_out_odd']
OUT_SHAPES = [("y_prompt", (1, TP, D)), ("y_sample", (SB, ST, D)), ("k_prompt", (1, 1, TP, H, DH)), ("v_prompt", (1, 1, TP, H, DH)),
              ("k_sample", (1, SB, ST, H, DH)), ("v_sample", (1, SB, ST, H, DH)), ("pool_prompt", (1, 1, HIST, WA)),
              ("pool_sample", (1, SB, HIST, WA)), ("C_prompt", (1, 1, H, DC, DC)), ("n_prompt", (1, 1, H, DC)), ("m_prompt", (1, 1, H)),
              ("C_sample", (1, SB, H, DC, DC)), ("n_sample", (1, SB, H, DC)), ("m_sample", (1, SB, H))]


def kernel(**inputs):
    import numpy as np
    import concourse.bacc as bacc
    from concourse.bass_utils import run_bass_kernel_spmd

    nc = bacc.Bacc("TRN2", target_bir_lowering=False, num_devices=1)
    arrays = {name: np.ascontiguousarray(inputs[name]) for name in IN_NAMES}
    arrays["constants"] = shape_constants()
    ins = {name: nc.dram_tensor(name, a.shape, mybir.dt.from_np(a.dtype), kind="ExternalInput").ap() for name, a in arrays.items()}
    outs = {name: nc.dram_tensor("out_" + name, shape, F32, kind="ExternalOutput").ap() for name, shape in OUT_SHAPES}
    trunk_kernel(nc, ins, outs)
    r = run_bass_kernel_spmd(nc, [arrays], core_ids=[0])
    return tuple(r.results[0]["out_" + name] for name, _ in OUT_SHAPES)
```
